# Optimizing a Trainium2 kernel written in Bass

```python
import jax, jax.numpy as jnp
from jax import lax
import numpy as np

D_MODEL = 1024
BATCH = 1
SEQ = 512
DEPTH = 2
DEC_BATCH = 8
DEC_SEQ = 1
PAST_LEN = 2048
PAGE_SIZE = 128

MIX_HALF = D_MODEL // 2
SC_WIDTH = MIX_HALF
SC_K = 3
GLA_HEADS = 4
GLA_DV = MIX_HALF // GLA_HEADS
GLA_DK = GLA_DV // 2
GLA_RANK = 16
GLA_TAU = 16.0
GLA_CHUNK = 16
FOX_HEADS = 8
FOX_HD = MIX_HALF // FOX_HEADS
Q_BLOCK = 128
FOX_BIAS_LO = 3.0
FOX_BIAS_HI = 12.0
CF_WIDTH = MIX_HALF
CF_K = 31
D_FF = ((8 * D_MODEL + 3 * 256 - 1) // (3 * 256)) * 256
DN_ALPHA = (2 * DEPTH) ** 0.25
DN_BETA = (8 * DEPTH) ** -0.25
EPS = 1e-5
AB_SPLITS = (SC_WIDTH, SC_WIDTH, SC_WIDTH, GLA_HEADS * GLA_DK, GLA_HEADS * GLA_DK, GLA_HEADS * GLA_DV, GLA_HEADS * GLA_DV, GLA_RANK)
CD_SPLITS = (FOX_HEADS * FOX_HD, FOX_HEADS * FOX_HD, FOX_HEADS * FOX_HD, FOX_HEADS, CF_WIDTH, CF_WIDTH)
F32 = jnp.float32

kernel_name = 'hybrid_conv_gla_fox_conformer_step'

def _split(t, sizes):
    idx = [int(i) for i in np.cumsum(sizes)[:-1]]
    return jnp.split(t, idx, axis=-1)

def _layernorm(x, g, b):
    xf = x.astype(F32)
    mu = jnp.mean(xf, axis=-1, keepdims=True)
    var = jnp.mean(jnp.square(xf - mu), axis=-1, keepdims=True)
    return ((xf - mu) * lax.rsqrt(var + EPS) * g + b).astype(x.dtype)

def _rmsnorm(x, g):
    xf = x.astype(F32)
    return (xf * lax.rsqrt(jnp.mean(xf * xf, axis=-1, keepdims=True) + EPS) * g).astype(x.dtype)

def _causal_dwconv(u, prev, w):
    ext = jnp.concatenate([prev.astype(u.dtype), u], axis=1)
    y = lax.conv_general_dilated(ext, w[:, None, :].astype(u.dtype), window_strides=(1,), padding='VALID',
                                 dimension_numbers=('NWC', 'WIO', 'NWC'), feature_group_count=u.shape[-1])
    return y, ext[:, -(w.shape[0] - 1):]

def _gla(q, k, v, log_a, s0):
    b_, l_, h_, _ = q.shape
    dv = v.shape[-1]
    c = min(GLA_CHUNK, l_)
    n = -(-l_ // c)
    pad = ((0, 0), (0, n * c - l_), (0, 0), (0, 0))
    q, k, v, log_a = (jnp.pad(t, pad) for t in (q, k, v, log_a))

    def chunks(t):
        return t.reshape(b_, n, c, h_, t.shape[-1]).transpose(1, 0, 3, 2, 4)

    qc, kc, vc = chunks(q), chunks(k), chunks(v)
    g = jnp.cumsum(chunks(log_a).astype(F32), axis=3)
    g_last = g[:, :, :, -1:, :]
    causal = jnp.tril(jnp.ones((c, c), bool))
    rel = g[:, :, :, :, None, :] - g[:, :, :, None, :, :]
    decay = jnp.exp(jnp.where(causal[:, :, None], rel, -jnp.inf))
    scores = jnp.einsum('nbhtd,nbhsd,nbhtsd->nbhts', qc, kc, decay)
    o_intra = jnp.einsum('nbhts,nbhsv->nbhtv', scores, vc)
    q_read = qc * jnp.exp(g)
    k_write = kc * jnp.exp(g_last - g)
    a_chunk = jnp.exp(g_last[:, :, :, 0, :])

    def step(s, xs):
        qr, kw, vv, ac = xs
        o = jnp.einsum('bhtd,bhdv->bhtv', qr, s)
        s = ac[..., None] * s + jnp.einsum('bhtd,bhtv->bhdv', kw, vv)
        return s, o

    s_fin, o_inter = lax.scan(step, s0.astype(F32), (q_read, k_write, vc, a_chunk))
    o = (o_intra + o_inter).transpose(1, 0, 3, 2, 4).reshape(b_, n * c, h_, dv)[:, :l_]
    return o.astype(v.dtype), s_fin.astype(s0.dtype)

def _fox_cum(lf):
    lf = lf.astype(F32).transpose(0, 2, 1)
    return lf - lax.cumsum(lf, axis=2, reverse=True)

def _fox_logits(q, k, cq, ck, qi, ki):
    s = jnp.einsum('bqhd,bkhd->bhqk', q, k, preferred_element_type=F32) * (FOX_HD ** -0.5)
    s = s + cq[..., :, None] - ck[..., None, :]
    return jnp.where(ki[None, :] <= qi[:, None], s, -jnp.inf)

def _fox_prompt(q, k, v, lf):
    b_, l_, h_, hd = q.shape
    c = _fox_cum(lf)
    ki = jnp.arange(l_)
    nb = l_ // Q_BLOCK
    qb = q.reshape(b_, nb, Q_BLOCK, h_, hd).transpose(1, 0, 2, 3, 4)
    cb = c.reshape(b_, h_, nb, Q_BLOCK).transpose(2, 0, 1, 3)
    ib = ki.reshape(nb, Q_BLOCK)

    def block(args):
        qq, cc, ii = args
        p = jax.nn.softmax(_fox_logits(qq, k, cc, c, ii, ki), axis=-1)
        return jnp.einsum('bhqk,bkhd->bqhd', p.astype(v.dtype), v)

    o = lax.map(block, (qb, cb, ib))
    return o.transpose(1, 0, 2, 3, 4).reshape(b_, l_, h_, hd)

def _fox_sample(q, k, v, lf, k_past, v_past, lf_past):
    l_ = q.shape[1]
    p_len = k_past.shape[1]
    c = _fox_cum(jnp.concatenate([lf_past.astype(F32), lf], axis=1))
    c_past, c_new = c[..., :p_len], c[..., p_len:]
    qi = p_len + jnp.arange(l_)
    s_past = _fox_logits(q, k_past, c_new, c_past, qi, jnp.arange(p_len))
    s_new = _fox_logits(q, k, c_new, c_new, qi, qi)
    p = jax.nn.softmax(jnp.concatenate([s_past, s_new], axis=-1), axis=-1).astype(v.dtype)
    return (jnp.einsum('bhqk,bkhd->bqhd', p[..., :p_len], v_past)
            + jnp.einsum('bhqk,bkhd->bqhd', p[..., p_len:], v))

def _mixer_ab(x, conv_prev, gla_s0, p):
    w_in, conv_w, w_gate2, b_gate, norm_g, w_out = p
    b_, l_, _ = x.shape
    bg, cg, hv, q, k, v, g, r = _split(x @ w_in, AB_SPLITS)
    y_a, conv_state = _causal_dwconv(cg * hv, conv_prev, conv_w)
    y_a = bg * y_a
    log_a = jax.nn.log_sigmoid((r @ w_gate2 + b_gate).astype(F32)) / GLA_TAU
    hk = lambda t: t.reshape(b_, l_, GLA_HEADS, GLA_DK)
    o, gla_state = _gla(hk(q) * (GLA_DK ** -0.5), hk(k), v.reshape(b_, l_, GLA_HEADS, GLA_DV), hk(log_a), gla_s0)
    o = _rmsnorm(o, norm_g).reshape(b_, l_, -1) * jax.nn.silu(g)
    return jnp.concatenate([y_a, o], axis=-1) @ w_out, conv_state, gla_state

def _mixer_cd(x, past, conv_prev, p):
    w_in, b_f, conv_w, conv_b, ln_g, ln_b, w_out = p
    b_, l_, _ = x.shape
    q, k, v, f, a, gate = _split(x @ w_in, CD_SPLITS)
    hs = lambda t: t.reshape(b_, l_, FOX_HEADS, FOX_HD)
    q, k, v = hs(q), hs(k), hs(v)
    logf = jax.nn.log_sigmoid((f + b_f).astype(F32))
    if past is None:
        o_c = _fox_prompt(q, k, v, logf)
    else:
        o_c = _fox_sample(q, k, v, logf, *past)
    u = a * jax.nn.sigmoid(gate)
    y_d, conv_state = _causal_dwconv(u, conv_prev, conv_w)
    y_d = jax.nn.silu(_layernorm(y_d + conv_b, ln_g, ln_b))
    out = jnp.concatenate([o_c.reshape(b_, l_, -1), y_d], axis=-1) @ w_out
    return out, k, v, logf.astype(x.dtype), conv_state

def _ffn(x, w_in, w_out):
    gate, up = jnp.split(x @ w_in, 2, axis=-1)
    return (jax.nn.silu(gate) * up) @ w_out

def _trunk(x, conv_a, gla_s, past, conv_d, ab_p, cd_p, ffn_w_in, ffn_w_out, ln_g, ln_b):
    for layer in range(DEPTH):
        if layer % 2 == 0:
            m, conv_a, gla_s = _mixer_ab(x, conv_a, gla_s, ab_p)
        else:
            m, k_rows, v_rows, lf_rows, conv_d = _mixer_cd(x, past, conv_d, cd_p)
        x = _layernorm(DN_ALPHA * x + m, ln_g[layer, 0], ln_b[layer, 0])
        x = _layernorm(DN_ALPHA * x + _ffn(x, ffn_w_in[layer], ffn_w_out[layer]), ln_g[layer, 1], ln_b[layer, 1])
    return x, conv_a, gla_s, k_rows, v_rows, lf_rows, conv_d

def setup_inputs(seed: int = 0) -> dict:
    key = jax.random.key(seed)
    ks = iter(jax.random.split(key, 32))

    def nrm(shape, scale):
        return jax.random.normal(next(ks), shape, F32) * scale

    n_pages = PAST_LEN // PAGE_SIZE
    used = DEC_BATCH * n_pages
    n_phys = used + max(1, used // 4)
    page_table = jax.random.permutation(next(ks), n_phys)[:used].reshape(DEC_BATCH, n_pages).astype(jnp.int32)
    fox_b_f = jnp.linspace(FOX_BIAS_LO, FOX_BIAS_HI, FOX_HEADS, dtype=F32) + nrm((FOX_HEADS,), 0.1)
    return {
        'x_prompt': nrm((BATCH, SEQ, D_MODEL), 1.0),
        'x_sample': nrm((DEC_BATCH, DEC_SEQ, D_MODEL), 1.0),
        'state_conv_a': nrm((DEC_BATCH, SC_K - 1, SC_WIDTH), 1.0),
        'state_gla': nrm((DEC_BATCH, GLA_HEADS, GLA_DK, GLA_DV), 1.0),
        'cache_k': nrm((n_phys, PAGE_SIZE, FOX_HEADS, FOX_HD), 1.0),
        'cache_v': nrm((n_phys, PAGE_SIZE, FOX_HEADS, FOX_HD), 1.0),
        'cache_logf': jax.nn.log_sigmoid(fox_b_f + nrm((n_phys, PAGE_SIZE, FOX_HEADS), 1.0)),
        'state_conv_d': nrm((DEC_BATCH, CF_K - 1, CF_WIDTH), 0.5),
        'page_table': page_table,
        'ab_w_in': nrm((D_MODEL, sum(AB_SPLITS)), D_MODEL ** -0.5),
        'ab_conv_w': nrm((SC_K, SC_WIDTH), SC_K ** -0.5),
        'gla_w_gate2': nrm((GLA_RANK, GLA_HEADS * GLA_DK), GLA_RANK ** -0.5),
        'gla_b_gate': nrm((GLA_HEADS * GLA_DK,), 0.01),
        'gla_norm_g': 1.0 + nrm((GLA_DV,), 0.01),
        'ab_w_out': nrm((D_MODEL, D_MODEL), DN_BETA * D_MODEL ** -0.5),
        'cd_w_in': nrm((D_MODEL, sum(CD_SPLITS)), D_MODEL ** -0.5),
        'fox_b_f': fox_b_f,
        'cf_conv_w': nrm((CF_K, CF_WIDTH), CF_K ** -0.5),
        'cf_conv_b': nrm((CF_WIDTH,), 0.01),
        'cf_ln_g': 1.0 + nrm((CF_WIDTH,), 0.01),
        'cf_ln_b': nrm((CF_WIDTH,), 0.01),
        'cd_w_out': nrm((D_MODEL, D_MODEL), DN_BETA * D_MODEL ** -0.5),
        'ffn_w_in': nrm((DEPTH, D_MODEL, 2 * D_FF), D_MODEL ** -0.5),
        'ffn_w_out': nrm((DEPTH, D_FF, D_MODEL), DN_BETA * D_FF ** -0.5),
        'ln_g': 1.0 + nrm((DEPTH, 2, D_MODEL), 0.01),
        'ln_b': nrm((DEPTH, 2, D_MODEL), 0.01),
    }

def reference(x_prompt, x_sample, state_conv_a, state_gla, cache_k, cache_v, cache_logf, state_conv_d, page_table,
              ab_w_in, ab_conv_w, gla_w_gate2, gla_b_gate, gla_norm_g, ab_w_out,
              cd_w_in, fox_b_f, cf_conv_w, cf_conv_b, cf_ln_g, cf_ln_b, cd_w_out,
              ffn_w_in, ffn_w_out, ln_g, ln_b):
    ab_p = (ab_w_in, ab_conv_w, gla_w_gate2, gla_b_gate, gla_norm_g, ab_w_out)
    cd_p = (cd_w_in, fox_b_f, cf_conv_w, cf_conv_b, cf_ln_g, cf_ln_b, cd_w_out)
    nb, dt = x_prompt.shape[0], x_prompt.dtype
    y_prompt, conv_a_p, gla_p, k_p, v_p, lf_p, conv_d_p = _trunk(
        x_prompt, jnp.zeros((nb, SC_K - 1, SC_WIDTH), dt), jnp.zeros((nb, GLA_HEADS, GLA_DK, GLA_DV), dt),
        None, jnp.zeros((nb, CF_K - 1, CF_WIDTH), dt), ab_p, cd_p, ffn_w_in, ffn_w_out, ln_g, ln_b)
    nd, n_pages = page_table.shape
    p_len = n_pages * PAGE_SIZE
    k_past = cache_k[page_table].reshape(nd, p_len, FOX_HEADS, FOX_HD)
    v_past = cache_v[page_table].reshape(nd, p_len, FOX_HEADS, FOX_HD)
    lf_past = cache_logf[page_table].reshape(nd, p_len, FOX_HEADS)
    y_sample, conv_a_s, gla_s, k_s, v_s, lf_s, conv_d_s = _trunk(
        x_sample, state_conv_a, state_gla, (k_past, v_past, lf_past), state_conv_d,
        ab_p, cd_p, ffn_w_in, ffn_w_out, ln_g, ln_b)
    return (y_prompt, y_sample, conv_a_p, conv_a_s, gla_p, gla_s, k_p, k_s, v_p, v_s, lf_p, lf_s, conv_d_p, conv_d_s)


_drawn_inputs = setup_inputs


def setup_inputs(seed=0):
    import zlib

    import numpy as np

    out = dict(_drawn_inputs(seed))
    spreads = {}
    factors = {'gla_b_gate': 8.0,
     'gla_norm_g': 8.0,
     'cf_conv_b': 8.0,
     'cf_ln_g': 8.0,
     'cf_ln_b': 8.0,
     'ln_g': 2.851,
     'ln_b': 2.673}
    for name, (base, spread) in spreads.items():
        noise = np.random.default_rng([zlib.crc32(name.encode()), seed]).standard_normal(out[name].shape)
        drawn = base * np.exp(spread * noise) if base else spread * noise
        out[name] = __import__('jax').numpy.asarray(drawn.astype(out[name].dtype))
    for name, factor in factors.items():
        out[name] = (out[name] * factor).astype(out[name].dtype)
    return out
```

```python
from contextlib import ExitStack

import numpy as np
import concourse.bass as bass
from concourse import mybir

F32 = mybir.dt.float32
F32R = mybir.dt.float32r
BF16 = mybir.dt.bfloat16
I32 = mybir.dt.int32
ALU = mybir.AluOpType
ACT = mybir.ActivationFunctionType
AX = mybir.AxisListType.X

P = 128
D = 1024
KD = D // P
TP = 512
TS = 8
T = TP + TS
HT = T // 2
NB = 8
PAGES = 16
PHYS = 160
DFF = 2816
KF = DFF // P
HALF_KF = KF // 2
ALPHA = float(4 ** 0.25)
EPS = 1e-5
NEG = -1e30
GC = TP // P
LEVELS = 7
CF_TAPS = 31
RAW = 4
SPLIT = 2
TILES_AB = 24
TILES_CD = 20
AB_V, AB_Q, AB_K, AB_G, AB_CG, AB_HV, AB_BG = 0, 4, 6, 8, 12, 16, 20
CD_Q, CD_K, CD_V, CD_GATE, CD_A = 0, 4, 8, 12, 16

_PARAMS = [("ln_g", 32), ("ln_b", 32), ("conv_a", 12), ("conv_d", 124), ("cf_b", 4), ("cf_g", 4), ("cf_lb", 4),
           ("b_gate", 2), ("norm_g", 1), ("b_f", 1), ("w_gate2", 256), ("w_r", 128), ("w_f", 320)]
PARAM_AT, _n = {}, 0
for _name, _w in _PARAMS:
    PARAM_AT[_name] = _n
    _n += _w
PARAM_COLS = _n
CONST_AT = {"ident": 0, "ones": 128, "later": 256, "scan": 384, "pick": 896, "causal": 904}
CONST_COLS = 904 + 128
IMASK_COLS = LEVELS * 64 + 128


def bass_hybrid_step(nc, A, O):
    with ExitStack() as ctx:
        base = (nc.sbuf_base + 31) // 32 * 32

        def at(name, shape, offset, dt=F32):
            return nc.alloc_sbuf_tensor_at(name, shape, dt, offset=base + offset)

        def sem(name):
            return ctx.enter_context(nc.semaphore(name))

        TB = T * 4
        x = at("x", [P, KD, T], 0)
        o_xs = KD * TB
        xh = at("xh", [P, KD, T], o_xs, F32R)
        xl = at("xl", [P, KD, T], o_xs + KD * TB, F32R)
        o_w = o_xs + 2 * KD * TB
        SLOT = HALF_KF * P
        raw = at("raw", [P, RAW, SLOT], o_w)
        wh = at("wh", [P, SPLIT, SLOT], o_w + RAW * SLOT * 4, F32R)
        wl = at("wl", [P, SPLIT, SLOT], o_w + (RAW + SPLIT) * SLOT * 4, F32R)
        o_z = o_w + (RAW + 2 * SPLIT) * SLOT * 4
        zone = 2 * KF * TB
        o_s = o_z + zone
        small = [o_s]

        def keep(name, shape, dt=F32):
            n = int(np.prod(shape[1:])) * (2 if dt == BF16 else 4)
            t = at(name, shape, small[0], dt)
            small[0] += (n + 31) // 32 * 32
            return t

        par = keep("par", [P, PARAM_COLS])
        con = keep("con", [P, CONST_COLS])
        imask = keep("imask", [P, IMASK_COLS], I32)
        table = keep("table", [1, NB * PAGES], I32)
        ident_b = keep("ident_b", [P, P], BF16)
        causal_b = keep("causal_b", [P, P], BF16)
        rstd = keep("rstd", [P, T])
        conv_a_state = keep("conv_a_state", [P, 4, TS, 2])
        lf_pages = keep("lf_pages", [P, PAGES, NB, 8])
        qblk = keep("qblk", [P, 4, NB, 2])
        small_a = keep("small_a", [P, 64])
        small_b = keep("small_b", [P, 64])
        small_c = keep("small_c", [P, 64])
        small_d = keep("small_d", [P, 64])
        tiny = keep("tiny", [P, 16])
        zeros = keep("zeros", [P, P])
        eps_c = keep("eps_c", [P, 1])
        assert base + small[0] <= nc.sbuf_usable_end, (base + small[0], nc.sbuf_usable_end)

        def par_of(name, w):
            return par[:, PARAM_AT[name]:PARAM_AT[name] + w]

        ident = con[:, 0:128]
        ones = con[:, 128:256]
        later = con[:, 256:384]
        scan_on = con[:, 384:896]
        pick = con[:, 896:904]

        hh = at("hh", [P, KF, T], o_z, F32R)
        hl = at("hl", [P, KF, T], o_z + KF * TB, F32R)
        gate_t = keep("gate_t", [P, T])
        hid_t = keep("hid_t", [P, T])
        squares = at("squares", [P, KD, T], o_z)
        assert base + small[0] <= nc.sbuf_usable_end, (base + small[0], nc.sbuf_usable_end)

        pj = at("pj", [P, TILES_AB, T], o_z)
        o_g = o_z + TILES_AB * TB
        attn = at("attn", [P, GC * 4, P], o_g)
        vtok = at("vtok", [P, GC, 512], o_g + 8192)
        kwtok = at("kwtok", [P, GC, 256], o_g + 16384)
        gla_s = at("gla_s", [P, GC, 2, P], o_g + 20480)
        gla_o = at("gla_o", [P, 4, T], o_g + 24576)
        gla_s0 = at("gla_s0", [P, NB, 2, P], o_g + 24576 + 8320)
        assert 24576 + 8320 + 8192 + TILES_AB * TB <= zone
        rms_r = at("rms_r", [P, 4 * T], o_g)
        gla_kv = at("gla_kv", [P, NB, 2, P], o_z + AB_V * TB)
        rms_sq = at("rms_sq", [P, 4 * T], o_z + AB_Q * TB)
        loga = at("loga", [P, 2, T], o_xs)
        gcum = at("gcum", [P, 2, TP], o_xs + 4160)
        gdiff = at("gdiff", [P, 2, 2, TP], o_xs + 8256)
        qk = at("qk", [P, 2, 2, TP], o_xs + 16448)
        zpre = at("zpre", [P, 2, T], o_xs + 24640)
        zexp = at("zexp", [P, 2, T], o_xs + 28800)
        r_t = at("r_t", [16, T], o_g + 24576)
        vsam = at("vsam", [NB, 512], o_xs + 24640)
        assert 28800 + 4160 <= 2 * KD * TB

        pj2 = at("pj2", [P, TILES_CD, T], o_z)
        U_PAD = CF_TAPS - 1
        upad = at("upad", [P, 4, U_PAD + TP], o_z + CD_A * TB)
        o_k = o_z + TILES_CD * TB + 384
        assert 4 * (U_PAD + TP) * 4 <= 4 * TB + 384
        pages = at("pages", [P, 4, 4, 512], o_k)
        lf_later = at("lf_later", [P, PAGES, 64], o_k)
        frow = [at(f"frow{i}", [40, T], o_k + 4096 + i * TB) for i in range(6)]
        squares_d = at("squares_d", [P, 4, T], o_k)
        s_all = at("s_all", [P, NB, 8, PAGES + 1], o_k + 32768)
        decay = at("decay", [P, NB, 8, PAGES], o_k + 32768 + 4352)
        ext_d = at("ext_d", [P, 4, TS, 31], o_k + 32768 + 8448)
        prod_d = at("prod_d", [P, 4, TS, 31], o_k + 32768 + 8448 + 3968)
        assert TILES_CD * TB + 384 + 32768 + 8448 + 7936 <= zone
        vtok2 = at("vtok2", [P, GC, 512], o_xs)
        prob = at("prob", [P, 2, 512], o_xs + 8192)
        prob_t = at("prob_t", [P, 2, 512], o_xs + 12288)
        q_st = at("q_st", [P, 512], o_xs + 16384)
        v_st = at("v_st", [P, GC, P], o_xs + 18432)
        grow = at("grow", [P, 512], o_xs + 20480)
        hrow = at("hrow", [P, 512], o_xs + 22528)
        hsel = at("hsel", [P, 2, 512], o_xs + 24576)
        k_st = at("k_st", [P, 512], o_xs + 28672)
        assert 28672 + 2048 <= 2 * KD * TB

        ps = ctx.enter_context(nc.psum_tensor("ps", [P, 8, 512], F32))


        x_in = sem("x_in")
        par_in = sem("par_in")
        state_in = sem("state_in")
        conv_d_in = sem("conv_d_in")
        w_landed = [sem(f"w_landed{i}") for i in range(RAW)]
        w_rounded = sem("w_rounded")
        w_rest = sem("w_rest")
        slot_used = sem("slot_used")
        x_hi = sem("x_hi")
        x_split = sem("x_split")
        acc_free = [sem(f"acc_free{i}") for i in range(2)]
        dve_own = sem("dve_own")
        act_own = sem("act_own")
        pool_own = sem("pool_own")
        setup = sem("setup")
        ln_in = sem("ln_in")
        ln_sum = sem("ln_sum")
        ln_centered = sem("ln_centered")
        ln_sq = sem("ln_sq")
        ln_var = sem("ln_var")
        ln_veps = sem("ln_veps")
        ln_std = sem("ln_std")
        ln_scaled = sem("ln_scaled")
        ln_out = sem("ln_out")
        gate_ready = sem("gate_ready")
        hid_ready = sem("hid_ready")
        hid_hi = sem("hid_hi")
        hid_split = sem("hid_split")
        out_sent = sem("out_sent")
        y_sent = sem("y_sent")
        logf_sent = sem("logf_sent")
        r_sum, r_copied, z_sum, z_pre, z_log, log_a = (sem(n) for n in ("r_sum", "r_copied", "z_sum", "z_pre", "z_log", "log_a"))
        v_turned, v_tok = sem("v_turned"), sem("v_tok")
        lv_diff, lv_exp, lv_qk, lv_scores, lv_kept = (sem(n) for n in ("lv_diff", "lv_exp", "lv_qk", "lv_scores", "lv_kept"))
        attn_zero = sem("attn_zero")
        kw_diff, kw_exp, kw_ready, kw_turned, kw_tok = (sem(n) for n in ("kw_diff", "kw_exp", "kw_ready", "kw_turned", "kw_tok"))
        kv_sum, state_c, o_sum, o_copied = (sem(n) for n in ("kv_sum", "state_c", "o_sum", "o_copied"))
        sam_decay, vsam_turned, vsam_copied, vb_sum, vb_used, sam_state, sam_o = (
            sem(n) for n in ("sam_decay", "vsam_turned", "vsam_copied", "vb_sum", "vb_used", "sam_state", "sam_o"))
        rms_squared, rms_sum, rms_eps, rms_std, g_silu, y_ab = (
            sem(n) for n in ("rms_squared", "rms_sum", "rms_eps", "rms_std", "g_silu", "y_ab"))
        conv_a_ready = sem("conv_a_ready")
        f_sum, f_pre, f_log, f_done, later_in, later_sum, decay_ready = (
            sem(n) for n in ("f_sum", "f_pre", "f_log", "f_done", "later_in", "later_sum", "decay_ready"))
        fox_staged, s_ready, neg_max, exp_done, p_ready, p_turned, pt_copied, pv_done, o_evac = (
            sem(n) for n in ("fox_staged", "s_ready", "neg_max", "exp_done", "p_ready", "p_turned", "pt_copied", "pv_done", "o_evac"))
        self_in, self_sum = sem("self_in"), sem("self_sum")
        page_in = [sem(f"page_in{i}") for i in range(4)]
        lf_in = sem("lf_in")
        pages_free = sem("pages_free")
        s_ready_all, m_turned, m_diag, m_cast, s_shifted, p_all, l_part, l_sum, pv_all, self_cast = (
            sem(n) for n in ("s_ready_all", "m_turned", "m_diag", "m_cast", "s_shifted", "p_all", "l_part", "l_sum", "pv_all", "self_cast"))
        d_sig, d_u, d_biased, d_silu, y_cd = (sem(n) for n in ("d_sig", "d_u", "d_biased", "d_silu", "y_cd"))

        block = ctx.enter_context(nc.Block())

        PH = {}
        s0 = t0 = 0
        for name, slots, tiles in (("ab_in", 24, 24), ("ab_out", 8, 8), ("f0_in", 44, 44), ("f0_out", 16, 8),
                                   ("cd_in", 20, 20), ("cd_out", 8, 8), ("f1_in", 44, 44), ("f1_out", 16, 8)):
            PH[name] = (s0, slots, t0, tiles)
            s0, t0 = s0 + slots, t0 + tiles
        SLOTS = s0
        BLOCKS = {"f0_out": HALF_KF, "f1_out": HALF_KF}

        def halves(ap):
            return ap.rearrange("p (h n) -> p h n", h=2)

        @block.sync
        def _(sp):
            for c in range(2):
                sp.dma_start(x[:, 4 * c:4 * c + 4, :], A["xt"][:, 4 * c:4 * c + 4, :]).then_inc(x_in, 16)
            sp.dma_start(par[:], A["params"]).then_inc(par_in, 16)
            sp.dma_start(con[:], A["consts"]).then_inc(par_in, 16)

            def weights(name, i, first=False):
                s, _, _, _ = PH[name]
                b = BLOCKS.get(name, KD)
                for j in range(RAW):
                    if not first:
                        sp.wait_ge(w_rest, s + 4 * i + j + 1 - RAW)
                    src = A["w_" + name][bass.ds(4 * i + j, 1)].rearrange("o p n -> p (o n)")
                    sp.dma_start(raw[:, j, 0:b * P], src).then_inc(w_landed[j], 16)

            weights("ab_in", 0, first=True)
            sp.dma_start(imask[:], A["imask"]).then_inc(state_in, 16)
            sp.dma_start(table[:], A["table"]).then_inc(state_in, 16)
            sp.dma_start(conv_a_state[:], A["conv_a_state"]).then_inc(state_in, 16)
            sp.dma_start(gla_s0[:], A["gla_state"]).then_inc(state_in, 16)
            with sp.Fori(1, 6) as i:
                weights("ab_in", i)
            with sp.Fori(0, 2) as i:
                weights("ab_out", i)
            sp.wait_ge(state_in, 64)
            with sp.Fori(0, NB) as i:
                weights("f0_in", i)
                for g in range(PAGES):
                    page = sp.value_load(table[0:1, bass.ds(i * PAGES + g, 1)], min_val=0, max_val=PHYS - 1)
                    sp.dma_start(lf_pages[:, g, bass.ds(i, 1), :].rearrange("p o h -> p (o h)"),
                                 A["cache_logf"][bass.ds(page, 1)].rearrange("o p h -> p (o h)")).then_inc(lf_in, 16)
            with sp.Fori(NB, 11) as i:
                weights("f0_in", i)
            with sp.Fori(0, 4) as i:
                weights("f0_out", i)
            with sp.Fori(0, 5) as i:
                weights("cd_in", i)
            weights("cd_out", 0)
            sp.wait_ge(decay_ready, 1)
            sp.wait_ge(logf_sent, 16)
            sp.dma_start(ext_d[:, :, :, 0:CF_TAPS - 1], A["conv_d_state"]).then_inc(conv_d_in, 16)
            for which, cache in enumerate((A["cache_kt"], A["cache_v"])):
                with sp.Fori(0, NB) as b:
                    for s in range(4):
                        sp.wait_ge(pages_free, 32 * which + b * 4 + s + 1)
                        for g in range(4):
                            page = sp.value_load(table[0:1, bass.ds(b * PAGES + 4 * s + g, 1)], min_val=0, max_val=PHYS - 1)
                            sp.dma_start(pages[:, s, g, :], cache[bass.ds(page, 1)].rearrange("o p n -> p (o n)"))\
                              .then_inc(page_in[s], 16)
            weights("cd_out", 1)
            with sp.Fori(0, 11) as i:
                weights("f1_in", i)
            with sp.Fori(0, 4) as i:
                weights("f1_out", i)
            sp.wait_ge(ln_out, 4 * KD + 4)
            sp.dma_start(O["y"], x[:]).then_inc(y_sent, 16)
            sp.wait_ge(y_sent, 16)
            sp.wait_ge(out_sent, 16 * OUT_CD)

        @block.scalar
        def _(act):
            own = [0]

            def link(ins):
                own[0] += 1
                ins.then_inc(act_own, 1)
                act.wait_ge(act_own, own[0])

            act.wait_ge(par_in, 32)
            nc.scalar.activation(ident_b[:], ident, ACT.Copy)
            nc.scalar.activation(causal_b[:], con[:, 904:1032], ACT.Copy).then_inc(setup, 1)
            act.sem_inc(exp_done, 2)
            act.sem_inc(pt_copied, 2)

            def rounded(i4, n, j, b):
                act.wait_ge(w_landed[j], i4)
                act.wait_ge(slot_used, n + 1)
                nc.scalar.activation(wh[:, j % SPLIT, 0:b * P], raw[:, j, 0:b * P], ACT.Copy).then_inc(w_rounded, 1)

            def next_rounded(name, i, j, last):
                s, slots, _, _ = PH[name]
                n = s + 4 * i + j + 1
                b = BLOCKS.get(name, KD)
                if last and j == 3:
                    if n == SLOTS:
                        return
                    b = BLOCKS.get(NEXT[name], KD)
                first = s // 4 + i + (j + 1) // 4
                rounded(first * 16 + 16, n, (j + 1) % 4, b)

            def product(name, tile):
                n = PH[name][1] // 4
                if n > 1:
                    with act.Fori(0, n - 1) as i:
                        for j in range(4):
                            next_rounded(name, i, j, False)
                            tile(i, j)
                for j in range(4):
                    next_rounded(name, n - 1, j, True)
                    tile(n - 1, j)

            def nothing(i, j):
                pass

            def split_rows(src, k, done):
                nc.scalar.activation(xh[:, k, :], src, ACT.Copy).then_inc(x_hi, 1)

            def normalise(idx, src, n, g, b, func):
                sq = squares_d if idx == D_LN else squares
                for k in range(n):
                    act.wait_ge(ln_centered, LN_BASE[idx] + k + 1)
                    nc.scalar.activation(sq[:, k, :], src(k), ACT.Square).then_inc(ln_sq, 1)
                act.wait_ge(ln_veps, idx + 1)
                nc.scalar.activation(rstd[:], rstd[:], ACT.Sqrt).then_inc(ln_std, 1)
                for k in range(n):
                    act.wait_ge(ln_scaled, LN_BASE[idx] + k + 1)
                    nc.scalar.activation(src(k), src(k), func, bias=b[:, k:k + 1], scale=g[:, k:k + 1]).then_inc(ln_out, 1)

            def normal_rows(i, layer_norm):
                g = par[:, PARAM_AT["ln_g"] + 8 * layer_norm:PARAM_AT["ln_g"] + 8 * layer_norm + 8]
                b = par[:, PARAM_AT["ln_b"] + 8 * layer_norm:PARAM_AT["ln_b"] + 8 * layer_norm + 8]
                normalise(i, lambda k: x[:, k, :], KD, g, b, ACT.Identity)

            def split_x(lo):
                for k in range(KD):
                    act.wait_ge(ln_out, lo + k + 1)
                    split_rows(x[:, k, :], k, None)

            def gate_up(name):
                s, _, _, _ = PH[name]
                m0 = 0 if name == "f0_in" else 22

                def tile(i, j):
                    m = i * 2 + j // 2
                    act.wait_ge(slot_used, i * 4 + (SPLIT + s + j + 1))
                    if j % 2 == 0:
                        act.wait_ge(hid_ready, m0 + m)
                        nc.scalar.activation(halves(gate_t[:]), ps[:, 0:2, 0:HT], ACT.Silu).then_inc(gate_ready, 1)
                        act.wait_ge(gate_ready, m0 + m + 1)
                        nc.scalar.sem_inc(acc_free[0], 1)
                    else:
                        act.wait_ge(hid_ready, m0 + m + 1)
                        nc.scalar.activation(hh[:, bass.ds(m, 1), :].rearrange("p o n -> p (o n)"), hid_t[:], ACT.Copy)\
                            .then_inc(hid_hi, 1)
                return tile

            rounded(16, 0, 0, KD)
            for k in range(KD):
                act.wait_ge(x_in, 32)
                split_rows(x[:, k, :], k, None)
            product("ab_in", nothing)

            act.wait_ge(z_sum, 1)
            for t in range(2):
                last = nc.scalar.activation(halves(zpre[:, t, :]), ps[:, 4 + 2 * t:6 + 2 * t, 0:HT], ACT.Identity,
                                            bias=par[:, PARAM_AT["b_gate"] + t:PARAM_AT["b_gate"] + t + 1])
            link(last)
            link(nc.scalar.activation(zexp[:], zpre[:], ACT.Abs))
            link(nc.scalar.activation(zexp[:], zexp[:], ACT.Exp, scale=-1.0))
            nc.scalar.activation(zexp[:], zexp[:], ACT.Ln, bias=1.0).then_inc(z_log, 1)
            act.wait_ge(v_turned, 1)
            for c in range(GC):
                last = nc.scalar.activation(vtok[:, c, :], ps[:, c, :], ACT.Copy)
            last.then_inc(v_tok, 1)
            act.wait_ge(vsam_turned, 1)
            act.wait_ge(log_a, 1)
            nc.scalar.activation(vsam[:], ps[0:NB, 7, :], ACT.Copy).then_inc(vsam_copied, 1)
            nc.scalar.activation(tiny[:].rearrange("p (a b) -> p a b", a=2), loga[:, :, TP:T], ACT.Exp).then_inc(sam_decay, 1)
            for l in range(LEVELS):
                act.wait_ge(lv_diff, l + 1)
                nc.scalar.activation(gdiff[:, l % 2], gdiff[:, l % 2], ACT.Exp).then_inc(lv_exp, 1)
            act.wait_ge(kw_diff, 1)
            nc.scalar.activation(gdiff[:, 0], gdiff[:, 0], ACT.Exp)
            nc.scalar.activation(gdiff[:, 1], gcum[:], ACT.Exp).then_inc(kw_exp, 1)
            act.wait_ge(kw_turned, 1)
            for c in range(GC):
                last = nc.scalar.activation(kwtok[:, c, :], ps[:, 4 + c // 2, 256 * (c % 2):256 * (c % 2) + 256], ACT.Copy)
            last.then_inc(kw_tok, 1)
            for c in range(GC):
                act.wait_ge(o_sum, c + 1)
                nc.scalar.activation(gla_o[:, :, P * c:P * c + P].rearrange("p (a c) t -> p c a t", c=2),
                                     ps[:, 2 * (c % 2):2 * (c % 2) + 2, 0:256].rearrange("p c (a t) -> p c a t", a=2),
                                     ACT.Copy).then_inc(o_copied, 1)
            act.wait_ge(sam_o, 1)
            link(nc.scalar.activation(gla_o[:, :, TP:T].rearrange("p (a c) b -> p c a b", c=2),
                                      ps[:, 0:2, 0:2 * TS].rearrange("p c (a b) -> p c a b", a=2), ACT.Copy))
            act.wait_ge(o_copied, GC)
            nc.scalar.activation(rms_sq[:], gla_o[:].rearrange("p h t -> p (h t)"), ACT.Square).then_inc(rms_squared, 1)
            act.wait_ge(rms_eps, 1)
            nc.scalar.activation(rms_r[:], rms_r[:], ACT.Sqrt).then_inc(rms_std, 1)
            nc.scalar.activation(pj[:, AB_G:AB_G + 4, :], pj[:, AB_G:AB_G + 4, :], ACT.Silu).then_inc(g_silu, 1)
            act.wait_ge(y_ab, 1)
            for k in range(KD):
                split_rows(pj[:, AB_HV + k, :] if k < 4 else gla_o[:, k - 4, :], k, None)
            product("ab_out", nothing)
            act.wait_ge(out_sent, 16 * OUT_AB)
            normal_rows(0, 0)
            split_x(0)
            product("f0_in", gate_up("f0_in"))
            product("f0_out", nothing)
            normal_rows(1, 1)
            split_x(KD)
            product("cd_in", nothing)

            act.wait_ge(f_sum, 1)
            link(nc.scalar.activation(halves(frow[0][:]), ps[0:40, 4:6, 0:HT], ACT.Identity,
                                      bias=par[0:40, PARAM_AT["b_f"]:PARAM_AT["b_f"] + 1]))
            link(nc.scalar.activation(frow[1][:], frow[0][:], ACT.Abs))
            link(nc.scalar.activation(frow[1][:], frow[1][:], ACT.Exp, scale=-1.0))
            nc.scalar.activation(frow[2][:], frow[1][:], ACT.Ln, bias=1.0).then_inc(f_log, 1)
            act.wait_ge(v_turned, 2)
            for c in range(GC):
                last = nc.scalar.activation(vtok2[:, c, :], ps[:, c, :], ACT.Copy)
            last.then_inc(v_tok, 1)
            act.wait_ge(acc_free[1], PH["cd_in"][2] // 2 + 10 + 1)
            act.wait_ge(acc_free[0], PH["cd_in"][2] // 2 + 10 + 1)
            nc.scalar.activation(pj2[:, CD_GATE:CD_GATE + 4, :], pj2[:, CD_GATE:CD_GATE + 4, :], ACT.Sigmoid).then_inc(d_sig, 1)

            def exps(hp, u):
                n = hp * 8 + u
                tt = u % 4
                act.wait_ge(neg_max, n + 1)
                act.wait_ge(p_turned, n + 1)
                nc.scalar.activation(prob[:, u % 2, 0:P * (tt + 1)], ps[:, u % 2, 0:P * (tt + 1)], ACT.Exp,
                                     bias=tiny[:, u % 2:u % 2 + 1], accum_out=tiny[:, 2 + u % 2:3 + u % 2]).then_inc(exp_done, 1)

            def pt_copy(hp, u):
                n = hp * 8 + u
                tt = u % 4
                act.wait_ge(p_turned, n + 3)
                act.wait_ge(pv_done, n + 1)
                nc.scalar.activation(prob_t[:, u % 2, 0:P * (tt + 1)], ps[:, 2 + u % 2, 0:P * (tt + 1)], ACT.Copy)\
                    .then_inc(pt_copied, 1)

            with act.Fori(0, 4) as hp:
                exps(hp, 0)
                for u in range(8):
                    if u < 7:
                        exps(hp, u + 1)
                    pt_copy(hp, u)
                act.wait_ge(pv_done, hp * 8 + 10)
                nc.scalar.activation(pj2[:, bass.ds(hp, 1), 0:TP].rearrange("p o n -> p (o n)"), ps[:, 4, :], ACT.Copy)\
                    .then_inc(o_evac, 1)
            act.wait_ge(s_shifted, 1)
            nc.scalar.activation(s_all[:], s_all[:], ACT.Exp).then_inc(p_all, 1)
            act.wait_ge(d_u, 1)
            for k in range(4):
                nc.scalar.activation(pj2[:, CD_GATE + k, :], pj2[:, CD_GATE + k, :], ACT.Identity,
                                     bias=par[:, PARAM_AT["cf_b"] + k:PARAM_AT["cf_b"] + k + 1]).then_inc(ln_in, 1)
            normalise(D_LN, lambda k: pj2[:, CD_GATE + k, :], 4, par_of("cf_g", 4), par_of("cf_lb", 4), ACT.Silu)
            act.wait_ge(ln_out, 2 * KD + 4)
            act.wait_ge(y_cd, 1)
            for k in range(KD):
                split_rows(pj2[:, k if k < 4 else CD_GATE + k - 4, :], k, None)
            product("cd_out", nothing)
            act.wait_ge(out_sent, 16 * OUT_CD)
            normal_rows(3, 2)
            split_x(2 * KD + 4)
            product("f1_in", gate_up("f1_in"))
            product("f1_out", nothing)
            normal_rows(4, 3)

        @block.gpsimd
        def _(pool):
            def rest(n, j, b):
                pool.wait_ge(w_rounded, n + 1)
                nc.gpsimd.tensor_tensor(wl[:, j % SPLIT, 0:b * P], raw[:, j, 0:b * P],
                                        wh[:, j % SPLIT, 0:b * P].bitcast(F32), ALU.subtract).then_inc(w_rest, 1)

            def next_rest(name, i, j, last):
                s, _, _, _ = PH[name]
                n = s + 4 * i + j + 1
                b = BLOCKS.get(name, KD)
                if last and j == 3:
                    if n == SLOTS:
                        return
                    b = BLOCKS.get(NEXT[name], KD)
                rest(n, (j + 1) % 4, b)

            def product(name, tile=None):
                n = PH[name][1] // 4
                with pool.Fori(0, n - 1) as i:
                    for j in range(4):
                        next_rest(name, i, j, False)
                        if tile:
                            tile(i, j)
                for j in range(4):
                    next_rest(name, n - 1, j, True)
                    if tile:
                        tile(n - 1, j)

            def hidden(name):
                m0 = 0 if name == "f0_in" else 22

                def tile(i, j):
                    if j % 2 == 1:
                        m = i * 2 + j // 2
                        pool.wait_ge(hid_hi, m0 + m + 1)
                        nc.gpsimd.tensor_tensor(hl[:, bass.ds(m, 1), :].rearrange("p o n -> p (o n)"), hid_t[:],
                                                hh[:, bass.ds(m, 1), :].rearrange("p o n -> p (o n)").bitcast(F32),
                                                ALU.subtract).then_inc(hid_split, 1)
                return tile

            nc.gpsimd.memset(zeros[:], 0.0)
            nc.gpsimd.memset(eps_c[:], EPS).then_inc(setup, 1)
            rest(0, 0, KD)
            product("ab_in")
            nc.gpsimd.memset(attn[:], 0.0).then_inc(attn_zero, 1)
            pool.wait_ge(conv_a_ready, 1)
            pool.dma_start(O["conv_a_p"], pj[:, AB_CG:AB_CG + 4, TP - 2:TP]).then_inc(out_sent, 16)
            pool.dma_start(O["conv_a_s"], conv_a_state[:]).then_inc(out_sent, 16)
            pool.wait_ge(state_c, GC)
            pool.dma_start(O["gla_p"], gla_s[:, GC - 1]).then_inc(out_sent, 16)
            pool.wait_ge(sam_state, 1)
            pool.dma_start(O["gla_s"], gla_s0[:]).then_inc(out_sent, 16)
            product("ab_out")
            product("f0_in", hidden("f0_in"))
            product("f0_out")
            product("cd_in")
            pool.wait_ge(acc_free[1], PH["cd_in"][2] // 2 + 10 + 1)
            pool.wait_ge(acc_free[0], PH["cd_in"][2] // 2 + 10 + 1)
            pool.dma_start(O["kt"], pj2[:, CD_K:CD_K + 4, :]).then_inc(out_sent, 16)
            pool.dma_start(O["vt"], pj2[:, CD_V:CD_V + 4, :]).then_inc(out_sent, 16)
            pool.wait_ge(f_done, 1)
            pool.dma_start(O["logf"], frow[3][0:8, :]).then_inc(logf_sent, 16)
            pool.wait_ge(d_u, 1)
            pool.dma_start(O["conv_d_p"], upad[:, :, TP:TP + CF_TAPS - 1]).then_inc(out_sent, 16)
            pool.dma_start(O["conv_d_s"], ext_d[:, :, :, 1:CF_TAPS]).then_inc(out_sent, 16)
            product("cd_out")
            product("f1_in", hidden("f1_in"))
            product("f1_out")

        @block.tensor
        def _(pe):
            pe.sem_inc(slot_used, SPLIT)
            pe.sem_inc(p_turned, 2)
            pe.sem_inc(pv_done, 2)
            pe.sem_inc(pages_free, 4)

            def three(out, slot, k, block_at, hi, lo, start, stop):
                for w, rows, a, z in ((wh, hi, True, False), (wh, lo, False, False), (wl, hi, False, True)):
                    for h in range(2):
                        mm = nc.tensor.matmul(out[h], w[:, slot, block_at * P:block_at * P + P],
                                              rows[:, k, HT * h:HT * h + HT], start=start and a, stop=stop and z)
                return mm

            def product(name):
                s, slots, t, _ = PH[name]

                def body(i):
                    for j in range(4):
                        n = s + i * 4 + j
                        pe.wait_ge(w_rest, n + 1)
                        if name in BLOCKS:
                            par2, tile, first, lastk = j // 2, t // 2 + i, j % 2 == 0, j % 2 == 1
                            if first:
                                pe.wait_ge(acc_free[par2], tile + 1)
                            out = [ps[:, 2 * par2 + h, 0:HT] for h in range(2)]
                            for k in range(HALF_KF):
                                kk = k + (0 if first else HALF_KF)
                                mm = three(out, j % 2, kk, k, hh, hl, first and k == 0, lastk and k == HALF_KF - 1)
                            mm.then_inc(slot_used, 1)
                        else:
                            pe.wait_ge(acc_free[j % 2], t // 2 + i * 2 + j // 2 + 1)
                            out = [ps[:, 2 * (j % 2) + h, 0:HT] for h in range(2)]
                            for k in range(KD):
                                mm = three(out, j % 2, k, k, xh, xl, k == 0, k == KD - 1)
                            mm.then_inc(slot_used, 1)

                with pe.Fori(0, slots // 4) as i:
                    body(i)

            def column_sums(idx, src, n):
                pe.wait_ge(ln_in, LN_BASE[idx] + n)
                for h in range(2):
                    for k in range(n):
                        mm = nc.tensor.matmul(ps[:, 4 + h, 0:HT], ones, src(k)[:, HT * h:HT * h + HT],
                                              start=k == 0, stop=k == n - 1)
                mm.then_inc(ln_sum, 1)
                sq = squares_d if idx == D_LN else squares
                for k in range(n):
                    pe.wait_ge(ln_sq, LN_BASE[idx] + k + 1)
                    for h in range(2):
                        mm = nc.tensor.matmul(ps[:, 6 + h, 0:HT], ones, sq[:, k, HT * h:HT * h + HT],
                                              start=k == 0, stop=k == n - 1)
                mm.then_inc(ln_var, 1)

            def x_rows(k):
                return x[:, k, :]

            pe.wait_ge(par_in, 32)
            pe.wait_ge(x_in, 32)
            for h in range(2):
                for k in range(KD):
                    a = PARAM_AT["w_r"] + 16 * k
                    mm = nc.tensor.matmul(ps[0:16, 4 + h, 0:HT], par[:, a:a + 16], x[:, k, HT * h:HT * h + HT],
                                          start=k == 0, stop=k == KD - 1)
            mm.then_inc(r_sum, 1)
            pe.wait_ge(x_split, KD)
            product("ab_in")
            pe.wait_ge(r_copied, 1)
            for t in range(2):
                for h in range(2):
                    a = PARAM_AT["w_gate2"] + P * t
                    mm = nc.tensor.matmul(ps[:, 4 + 2 * t + h, 0:HT], par[0:16, a:a + P], r_t[:, HT * h:HT * h + HT],
                                          start=True, stop=True)
            mm.then_inc(z_sum, 1)
            pe.wait_ge(acc_free[0], 12 + 1)
            pe.wait_ge(acc_free[1], 12 + 1)
            for c in range(GC):
                for h in range(4):
                    mm = nc.tensor.transpose(ps[:, c, P * h:P * h + P], pj[:, AB_V + h, P * c:P * c + P], ident)
            mm.then_inc(v_turned, 1)
            pe.wait_ge(z_log, 1)
            for h in range(4):
                mm = nc.tensor.transpose(ps[0:NB, 7, P * h:P * h + P], pj[:, AB_V + h, TP:T], ident)
            mm.then_inc(vsam_turned, 1)
            pe.wait_ge(vsam_copied, 1)
            for l in range(LEVELS):
                half = P >> (l + 1)
                pe.wait_ge(lv_qk, l + 1)
                if l >= 2:
                    pe.wait_ge(lv_kept, l - 1)
                for u in range(GC * 4):
                    h2, c, hp = u // 8, u // 2 % 4, u % 2
                    r0 = 64 * h2
                    rows = qk[r0:r0 + 64, l % 2, hp, P * c:P * c + P]
                    bank = 4 + 2 * (l % 2) + h2
                    out = ps[:, bank, 64 * (u % 8):64 * (u % 8) + 64].rearrange("p (n b) -> p n b", b=half)
                    mm = nc.tensor.matmul(out, rows, rows.rearrange("p (n b) -> p n b", b=2 * half)[:, :, half:],
                                          start=True, stop=True)
                mm.then_inc(lv_scores, 1)
            for part in range(2):
                pe.wait_ge(lv_kept, LEVELS - 1 + part)
                for u in range(8):
                    c, hp, r0 = u // 2, u % 2, 64 * part
                    b0 = (4 + 2 * ((LEVELS + part) % 2)) + (u % 8) // 4
                    mm = nc.tensor.matmul(ps[:, b0, P * (u % 4):P * (u % 4) + P],
                                          pj[r0:r0 + 64, AB_K + hp, P * c:P * c + P],
                                          pj[r0:r0 + 64, AB_Q + hp, P * c:P * c + P], start=True, stop=True)
                mm.then_inc(lv_scores, 1)
            pe.wait_ge(kw_ready, 1)
            pe.wait_ge(lv_kept, LEVELS + 2)
            for c in range(GC):
                for hp in range(2):
                    mm = nc.tensor.transpose(ps[:, 4 + c // 2, 256 * (c % 2) + P * hp:256 * (c % 2) + P * hp + P],
                                             qk[:, 0, hp, P * c:P * c + P], ident)
            mm.then_inc(kw_turned, 1)
            pe.wait_ge(kw_tok, 1)
            pe.wait_ge(v_tok, 1)
            for c in range(GC):
                for hp in range(2):
                    mm = nc.tensor.matmul(ps[:, 4 + c, 256 * hp:256 * hp + 256], kwtok[:, c, P * hp:P * hp + P],
                                          vtok[:, c, 256 * hp:256 * hp + 256], start=True, stop=True)
                mm.then_inc(kv_sum, 1)
            for c in range(GC):
                if c > 0:
                    pe.wait_ge(state_c, c)
                if c >= 2:
                    pe.wait_ge(o_copied, c - 1)
                for h in range(4):
                    r0, hp = 64 * (h % 2), h // 2
                    out = ps[:, 2 * (c % 2) + h % 2, P * hp:P * hp + P]
                    mm = nc.tensor.matmul(out, vtok[:, c, P * h:P * h + P], attn[:, 8 * (h % 2) + 2 * c + hp, :], start=True, stop=c == 0)
                    if c > 0:
                        mm = nc.tensor.matmul(out, gla_s[r0:r0 + 64, c - 1, hp, :],
                                              qk[r0:r0 + 64, 1, hp, P * c:P * c + P], start=False, stop=True)
                mm.then_inc(o_sum, 1)
            pe.wait_ge(state_c, GC)
            for b in range(NB):
                if b == 4:
                    pe.wait_ge(vb_used, 1)
                mm = nc.tensor.matmul(ps[:, 4 + b % 4, :], ident[0:NB, b:b + 1].to_broadcast([NB, P]), vsam[:],
                                      start=True, stop=True)
                if b % 4 == 3:
                    mm.then_inc(vb_sum, 1)
            pe.wait_ge(sam_state, 1)
            pe.wait_ge(o_copied, GC - 1)
            for h in range(4):
                for b in range(NB):
                    r0, hp = 64 * (h % 2), h // 2
                    mm = nc.tensor.matmul(ps[:, h % 2, TS * hp + b:TS * hp + b + 1], gla_s0[r0:r0 + 64, b, hp, :],
                                          pj[r0:r0 + 64, AB_Q + hp, TP + b:TP + b + 1], start=True, stop=True)
            mm.then_inc(sam_o, 1)
            pe.wait_ge(rms_squared, 1)
            for i in range(5):
                mm = nc.tensor.matmul(ps[:, i, 0:416], ones, rms_sq[:, 416 * i:416 * i + 416], start=True, stop=True)
            mm.then_inc(rms_sum, 1)

            pe.wait_ge(x_split, 2 * KD)
            product("ab_out")
            column_sums(0, x_rows, KD)
            pe.wait_ge(x_split, 3 * KD)
            product("f0_in")
            pe.wait_ge(hid_split, 22)
            product("f0_out")
            column_sums(1, x_rows, KD)
            pe.wait_ge(ln_out, 2 * KD)
            for h in range(2):
                for k in range(KD):
                    a = PARAM_AT["w_f"] + 40 * k
                    mm = nc.tensor.matmul(ps[0:40, 4 + h, 0:HT], par[:, a:a + 40], x[:, k, HT * h:HT * h + HT],
                                          start=k == 0, stop=k == KD - 1)
            mm.then_inc(f_sum, 1)
            pe.wait_ge(x_split, 4 * KD)
            product("cd_in")

            pe.wait_ge(acc_free[0], PH["cd_in"][2] // 2 + 10 + 1)
            pe.wait_ge(acc_free[1], PH["cd_in"][2] // 2 + 10 + 1)
            for c in range(GC):
                for h in range(4):
                    mm = nc.tensor.transpose(ps[:, c, P * h:P * h + P], pj2[:, CD_V + h, P * c:P * c + P], ident)
            mm.then_inc(v_turned, 1)
            pe.wait_ge(later_in, 1)
            for h in range(2):
                out = ps[:, 6 + h, :]
                nc.tensor.matmul(out, later, lf_pages[:, 8 * h:8 * h + 8].rearrange("p g b h -> p (g b h)"), start=True, stop=False)
                nc.tensor.matmul(out, ones, lf_later[:, 8 * h:8 * h + 8, :].rearrange("p g n -> p (g n)"), start=False, stop=False)
                mm = nc.tensor.matmul(out.rearrange("p (g n) -> p g n", g=8), ones[0:8, :],
                                      small_b[0:8, None, :].to_broadcast([8, 8, 64]), start=False, stop=True)
            mm.then_inc(later_sum, 1)
            pe.wait_ge(self_in, 1)
            nc.tensor.matmul(ps[0:1, 5, 0:64], ones[:, 0:1], small_a[:], start=True, stop=True).then_inc(self_sum, 1)

            def scores(hp, u):
                n = hp * 8 + u
                h2, tt = u // 4, u % 4
                r0, w = 64 * h2, P * (tt + 1)
                pe.wait_ge(exp_done, n + 1)
                out = ps[:, u % 2, 0:w]
                nc.tensor.matmul(out, q_st[r0:r0 + 64, P * tt:P * tt + P], k_st[r0:r0 + 64, 0:w], start=True, stop=False)
                nc.tensor.matmul(out, grow[:, P * tt:P * tt + P], hsel[:, h2, 0:w], start=False, stop=False)
                nc.tensor.matmul(ps[:, u % 2, P * tt:w], ident_b[:], causal_b[:], start=False, stop=True).then_inc(s_ready, 1)

            with pe.Fori(0, 4) as hp:
                pe.wait_ge(fox_staged, hp + 1)
                if True:
                    pe.wait_ge(v_tok, 2)
                    pe.wait_ge(setup, 2)
                scores(hp, 0)
                for u in range(8):
                    n = hp * 8 + u
                    h2, tt = u // 4, u % 4
                    r0 = 64 * h2
                    if u < 7:
                        scores(hp, u + 1)
                    pe.wait_ge(p_ready, n + 1)
                    pe.wait_ge(pt_copied, n + 1)
                    for c in range(tt + 1):
                        mm = nc.tensor.transpose(ps[:, 2 + u % 2, P * c:P * c + P], prob[:, u % 2, P * c:P * c + P], ident)
                    mm.then_inc(p_turned, 1)
                    pe.wait_ge(pt_copied, n + 3)
                    if u == 0:
                        pe.wait_ge(o_evac, hp)
                    for c in range(tt + 1):
                        mm = nc.tensor.matmul(ps[r0:r0 + 64, 4, P * tt:P * tt + P], v_st[:, c, r0:r0 + 64],
                                              prob_t[:, u % 2, P * c:P * c + P], start=c == 0, stop=c == tt)
                    mm.then_inc(pv_done, 1)

            pe.wait_ge(s_ready_all, 1)
            pe.wait_ge(o_evac, 4)
            with pe.Fori(0, NB) as b:
                for s in range(4):
                    pe.wait_ge(page_in[s], b * 64 + 64)
                    for g in range(4):
                        for hp in range(4):
                            a = 32 * hp + 2 * (4 * s + g)
                            mm = nc.tensor.matmul(ps[:, bass.ds(b, 1), a:a + 2].rearrange("p o n -> p (o n)"),
                                                  pages[:, s, g, P * hp:P * hp + P],
                                                  qblk[:, hp, bass.ds(b, 1), :].rearrange("p o n -> p (o n)"), start=True, stop=True)
                    mm.then_inc(pages_free, 1)
            pe.wait_ge(m_turned, 1)
            nc.tensor.transpose(ps[0:64, 5, 0:P], small_a[:], ident).then_inc(m_turned, 1)
            pe.wait_ge(m_diag, 1)
            nc.tensor.matmul(ps[:, 6, 0:64], ones[0:64, :], small_b[0:64, :], start=True, stop=True).then_inc(m_cast, 1)
            pe.wait_ge(l_part, 1)
            nc.tensor.matmul(ps[:, 7, 0:64], ones, small_c[:], start=True, stop=True).then_inc(l_sum, 1)
            nc.tensor.matmul(ps[:, 6, 64:128], ones[0:1, :], s_all[0:1, :, :, PAGES].rearrange("p b h -> p (b h)"),
                             start=True, stop=True).then_inc(self_cast, 1)
            nc.tensor.matmul(ps[:, 0, 0:64], zeros[:], zeros[:, 0:64], start=True, stop=False, skip_group_check=True)
            with pe.Fori(0, NB) as b:
                for s in range(4):
                    pe.wait_ge(page_in[s], b * 64 + 64 * 9)
                    for g in range(4):
                        for hp in range(4):
                            mm = nc.tensor.matmul(ps[:, 0, bass.ds(b * 8 + 2 * hp, 2)], pages[:, s, g, P * hp:P * hp + P],
                                                  s_all[:, bass.ds(b, 1), 2 * hp:2 * hp + 2, 4 * s + g].rearrange("p o n -> p (o n)"),
                                                  start=False, stop=False, skip_group_check=True)
                    mm.then_inc(pages_free, 1)
            nc.tensor.matmul(ps[:, 0, 0:64], zeros[:], zeros[:, 0:64], start=False, stop=True, skip_group_check=True).then_inc(pv_all, 1)
            column_sums(D_LN, lambda k: pj2[:, CD_GATE + k, :], 4)

            pe.wait_ge(x_split, 5 * KD)
            product("cd_out")
            column_sums(3, x_rows, KD)
            pe.wait_ge(x_split, 6 * KD)
            product("f1_in")
            pe.wait_ge(hid_split, 44)
            product("f1_out")
            column_sums(4, x_rows, KD)

        @block.vector
        def _(dve):
            own = [0]
            V = nc.vector

            def link(ins):
                own[0] += 1
                ins.then_inc(dve_own, 1)
                dve.wait_ge(dve_own, own[0])

            dve.sem_inc(acc_free[0], 1)
            dve.sem_inc(acc_free[1], 1)

            def acc(j):
                return ps[:, 2 * (j % 2):2 * (j % 2) + 2, 0:HT]

            def copy_tiles(name, dst):
                s, _, _, tiles = PH[name]
                with dve.Fori(0, tiles // 2) as i:
                    for j in range(2):
                        dve.wait_ge(slot_used, i * 2 + (SPLIT + s + j + 1))
                        V.tensor_copy(dst[:, bass.ds(i * 2 + j, 1), :].rearrange("p o (h n) -> p (o h) n", h=2), acc(j))\
                            .then_inc(acc_free[j], 1)

            def residual_tiles(name):
                s, slots, t, tiles = PH[name]
                for m in range(tiles):
                    dve.wait_ge(slot_used, SPLIT + s + (m + 1) * slots // tiles)
                    V.scalar_tensor_tensor(out=halves(x[:, m, :]), in0=halves(x[:, m, :]), scalar=ALPHA, in1=acc(m),
                                           op0=ALU.mult, op1=ALU.add).then_inc(acc_free[m % 2], 1)
                dve.wait_ge(acc_free[0], (t + tiles) // 2 + 1)
                dve.wait_ge(acc_free[1], (t + tiles) // 2 + 1)
                dve.sem_inc(ln_in, tiles)

            def rest_rows(src, lo):
                for k in range(KD):
                    dve.wait_ge(x_hi, lo + k + 1)
                    V.tensor_tensor(xl[:, k, :], src(k), xh[:, k, :].bitcast(F32), ALU.subtract).then_inc(x_split, 1)

            def normalise(idx, src, n):
                dve.wait_ge(ln_sum, idx + 1)
                for k in range(n):
                    V.scalar_tensor_tensor(out=halves(src(k)), in0=ps[:, 4:6, 0:HT], scalar=-1.0 / (P * n),
                                           in1=halves(src(k)), op0=ALU.mult, op1=ALU.add).then_inc(ln_centered, 1)
                dve.wait_ge(ln_var, idx + 1)
                V.tensor_scalar(halves(rstd[:]), ps[:, 6:8, 0:HT], 1.0 / (P * n), EPS, ALU.mult, ALU.add).then_inc(ln_veps, 1)
                dve.wait_ge(ln_std, idx + 1)
                link(V.reciprocal(rstd[:], rstd[:]))
                dve.wait_ge(ln_centered, LN_BASE[idx] + n)
                for k in range(n):
                    V.tensor_tensor(src(k), src(k), rstd[:], ALU.mult).then_inc(ln_scaled, 1)

            def x_rows(k):
                return x[:, k, :]

            def hidden(name):
                s, _, _, _ = PH[name]
                m0 = 0 if name == "f0_in" else 22
                with dve.Fori(0, 22) as m:
                    dve.wait_ge(gate_ready, m0 + m + 1)
                    dve.wait_ge(slot_used, m * 2 + (SPLIT + s + 2))
                    dve.wait_ge(hid_split, m0 + m)
                    V.tensor_tensor(halves(hid_t[:]), acc(1), halves(gate_t[:]), ALU.mult).then_inc(hid_ready, 1)
                    dve.wait_ge(hid_ready, m0 + m + 1)
                    dve.sem_inc(acc_free[1], 1)

            rest_rows(x_rows, 0)
            dve.wait_ge(r_sum, 1)
            V.tensor_copy(halves(r_t[:]), ps[0:16, 4:6, 0:HT]).then_inc(r_copied, 1)
            copy_tiles("ab_in", pj)
            dve.wait_ge(acc_free[0], 13)
            dve.wait_ge(acc_free[1], 13)
            dve.wait_ge(par_in, 32)
            dve.wait_ge(state_in, 64)

            link(V.tensor_scalar(pj[:, AB_Q:AB_Q + 2, :], pj[:, AB_Q:AB_Q + 2, :], 64 ** -0.5, None, ALU.mult))
            dve.wait_ge(z_log, 1)
            link(V.scalar_tensor_tensor(out=loga[:], in0=zpre[:], scalar=0.0, in1=zexp[:], op0=ALU.min, op1=ALU.subtract))
            V.tensor_scalar(loga[:], loga[:], 1.0 / 16.0, None, ALU.mult).then_inc(log_a, 1)
            dve.wait_ge(log_a, 1)
            for t in range(2):
                last = V.tensor_tensor_scan(gcum[:, t, :], scan_on, loga[:, t, 0:TP], 0.0, ALU.mult, ALU.add)
            link(last)

            def level_diff(l):
                half = P >> (l + 1)
                g = gcum[:].rearrange("p t (n b) -> p (t n) b", b=2 * half)
                d = gdiff[:, l % 2].rearrange("p t (n b) -> p (t n) b", b=2 * half)
                mid = g[:, :, half - 1:half].to_broadcast([P, 2 * TP // (2 * half), half])
                V.tensor_tensor(d[:, :, half:], g[:, :, half:], mid, ALU.subtract)
                V.tensor_tensor(d[:, :, 0:half], mid, g[:, :, 0:half], ALU.subtract).then_inc(lv_diff, 1)

            def level_qk(l):
                half = P >> (l + 1)

                def by_block(ap):
                    return ap.rearrange("p t (n b) -> p t n b", b=2 * half)
                d, o = by_block(gdiff[:, l % 2]), by_block(qk[:, l % 2])
                q, k = by_block(pj[:, AB_Q:AB_Q + 2, 0:TP]), by_block(pj[:, AB_K:AB_K + 2, 0:TP])
                dve.wait_ge(lv_exp, l + 1)
                if l >= 2:
                    dve.wait_ge(lv_scores, l - 1)
                V.tensor_tensor(o[:, :, :, half:], q[:, :, :, half:], d[:, :, :, half:], ALU.mult)
                V.tensor_tensor(o[:, :, :, 0:half], k[:, :, :, 0:half], d[:, :, :, 0:half], ALU.mult).then_inc(lv_qk, 1)

            def level_keep(l):
                half = P >> (l + 1)
                dve.wait_ge(lv_scores, l + 1)
                if l >= 1:
                    dve.wait_ge(lv_kept, l)
                out = attn[:].rearrange("p u (n b) -> p u n b", b=2 * half)[:, :, :, half:]
                mask = imask[:, None, 64 * l:64 * l + 64].to_broadcast([P, 16, 64]).rearrange("p u (n b) -> p u n b", b=half)
                bank = 4 + 2 * (l % 2)
                V.copy_predicated(out, mask, ps[:, bank:bank + 2, :].rearrange("p k (u n b) -> p (k u) n b", u=8, b=half))\
                    .then_inc(lv_kept, 1)

            level_diff(0)
            dve.wait_ge(attn_zero, 1)
            for l in range(LEVELS):
                if l + 1 < LEVELS:
                    if l >= 1:
                        dve.wait_ge(lv_qk, l)
                    level_diff(l + 1)
                level_qk(l)
                if l >= 1:
                    level_keep(l - 1)
            dve.wait_ge(lv_qk, LEVELS)
            g4 = gcum[:].rearrange("p t (n b) -> p (t n) b", b=P)
            V.tensor_tensor(gdiff[:, 0].rearrange("p t (n b) -> p (t n) b", b=P),
                            g4[:, :, P - 1:P].to_broadcast([P, 8, P]), g4, ALU.subtract).then_inc(kw_diff, 1)
            level_keep(LEVELS - 1)
            for part in range(2):
                bank = 4 + 2 * ((LEVELS + part) % 2)
                dve.wait_ge(lv_scores, LEVELS + part + 1)
                dve.wait_ge(lv_kept, LEVELS + part)
                V.copy_predicated(attn[:, 8 * part:8 * part + 8, :],
                                  imask[:, None, 64 * LEVELS:64 * LEVELS + P].to_broadcast([P, 8, P]),
                                  ps[:, bank:bank + 2, :].rearrange("p k (u t) -> p (k u) t", u=4)).then_inc(lv_kept, 1)
            dve.wait_ge(kw_exp, 1)
            V.tensor_tensor(qk[:, 0], pj[:, AB_K:AB_K + 2, 0:TP], gdiff[:, 0], ALU.mult)
            V.tensor_tensor(qk[:, 1], pj[:, AB_Q:AB_Q + 2, 0:TP], gdiff[:, 1], ALU.mult).then_inc(kw_ready, 1)
            for c in range(GC):
                dve.wait_ge(kv_sum, c + 1)
                if c > 0:
                    dve.wait_ge(state_c, c)
                for hp in range(2):
                    for h2 in range(2):
                        r = slice(64 * h2, 64 * h2 + 64)
                        src = ps[r, 4 + c, 256 * hp + P * h2:256 * hp + P * h2 + P]
                        if c == 0:
                            last = V.tensor_copy(gla_s[r, 0, hp, :], src)
                        else:
                            last = V.scalar_tensor_tensor(out=gla_s[r, c, hp, :], in0=gla_s[r, c - 1, hp, :],
                                                          scalar=gdiff[r, 1, hp, P * c + P - 1:P * c + P], in1=src,
                                                          op0=ALU.mult, op1=ALU.add)
                last.then_inc(state_c, 1)
            dve.wait_ge(sam_decay, 1)
            for b in range(NB):
                dve.wait_ge(vb_sum, b // 4 + 1)
                for h2 in range(2):
                    r = slice(64 * h2, 64 * h2 + 64)
                    last = V.tensor_tensor(gla_kv[r, b], ps[r, 4 + b % 4, :].rearrange("p (a c v) -> p a c v", a=2, c=2)[:, :, h2, :],
                                           pj[r, AB_K:AB_K + 2, TP + b:TP + b + 1].to_broadcast([64, 2, P]), ALU.mult)
                if b == 3:
                    last.then_inc(vb_used, 1)
            link(last)
            link(V.tensor_tensor(gla_s0[:], gla_s0[:],
                                 tiny[:].rearrange("p (a b) -> p b a", a=2)[:, :, :, None].to_broadcast([P, NB, 2, P]), ALU.mult))
            V.tensor_tensor(gla_s0[:], gla_s0[:], gla_kv[:], ALU.add).then_inc(sam_state, 1)

            U, Y = AB_CG, AB_HV
            link(V.tensor_tensor(pj[:, U:U + 4, :], pj[:, U:U + 4, :], pj[:, Y:Y + 4, :], ALU.mult))
            wa = par_of("conv_a", 12).rearrange("p (t j) -> p t j", j=3)
            for t in range(4):
                last = V.tensor_scalar(pj[:, Y + t, :], pj[:, U + t, :], wa[:, t, 2:3], None, ALU.mult)
            link(last)
            for s in (1, 2):
                for t in range(4):
                    V.scalar_tensor_tensor(out=pj[:, Y + t, s:TP], in0=pj[:, U + t, 0:TP - s], scalar=wa[:, t, 2 - s:3 - s],
                                           in1=pj[:, Y + t, s:TP], op0=ALU.mult, op1=ALU.add)
                    last = V.scalar_tensor_tensor(out=pj[:, Y + t, TP:T], in0=conv_a_state[:, t, :, 2 - s], scalar=wa[:, t, 2 - s:3 - s],
                                                  in1=pj[:, Y + t, TP:T], op0=ALU.mult, op1=ALU.add)
                link(last)
            link(V.tensor_copy(conv_a_state[:, :, :, 0], conv_a_state[:, :, :, 1]))
            V.tensor_copy(conv_a_state[:, :, :, 1], pj[:, U:U + 4, TP:T]).then_inc(conv_a_ready, 1)
            V.tensor_tensor(pj[:, Y:Y + 4, :], pj[:, Y:Y + 4, :], pj[:, AB_BG:AB_BG + 4, :], ALU.mult)
            dve.wait_ge(rms_sum, 1)
            V.tensor_scalar(rms_r[:].rearrange("p (i n) -> p i n", i=5), ps[:, 0:5, 0:416], 1.0 / P, EPS, ALU.mult, ALU.add)\
                .then_inc(rms_eps, 1)
            dve.wait_ge(rms_std, 1)
            link(V.reciprocal(rms_r[:], rms_r[:]))
            flat = gla_o[:].rearrange("p h t -> p (h t)")
            link(V.scalar_tensor_tensor(out=flat, in0=flat, scalar=par_of("norm_g", 1), in1=rms_r[:], op0=ALU.mult, op1=ALU.mult))
            dve.wait_ge(g_silu, 1)
            V.tensor_tensor(gla_o[:], gla_o[:], pj[:, AB_G:AB_G + 4, :], ALU.mult).then_inc(y_ab, 1)
            rest_rows(lambda k: pj[:, AB_HV + k, :] if k < 4 else gla_o[:, k - 4, :], KD)
            residual_tiles("ab_out")
            normalise(0, x_rows, KD)
            rest_rows(x_rows, 2 * KD)
            hidden("f0_in")
            residual_tiles("f0_out")
            normalise(1, x_rows, KD)
            rest_rows(x_rows, 3 * KD)
            copy_tiles("cd_in", pj2)
            a0 = PH["cd_in"][2] // 2 + 10 + 1
            dve.wait_ge(acc_free[0], a0)
            dve.wait_ge(acc_free[1], a0)

            z, e, ln1, lf, t4, t5 = (frow[i][:] for i in range(6))
            dve.wait_ge(f_log, 1)
            link(V.tensor_scalar(t4, e, 1.0, None, ALU.add))
            link(V.scalar_tensor_tensor(out=t5, in0=t4, scalar=-1.0, in1=e, op0=ALU.add, op1=ALU.subtract))
            link(V.reciprocal(t4, t4))
            link(V.tensor_tensor(t5, t5, t4, ALU.mult))
            link(V.tensor_tensor(t5, t5, ln1, ALU.subtract))
            link(V.scalar_tensor_tensor(out=lf, in0=z, scalar=0.0, in1=t5, op0=ALU.min, op1=ALU.add))
            dve.sem_inc(f_done, 1)
            V.memset(hrow[:], 0.0)
            V.memset(grow[:], 0.0)
            link(V.memset(hsel[:], 0.0))
            V.memset(hrow[0:8, :], 1.0)
            V.memset(grow[32:40, :], 1.0)
            V.memset(t4[:, 0:TP], 1.0)
            link(V.memset(small_b[:], 0.0))
            link(V.tensor_tensor_scan(t5[:, 0:TP], t4[:, 0:TP], lf[:, 0:TP], 0.0, ALU.mult, ALU.add))
            V.tensor_copy(grow[0:8, :], t5[0:8, 0:TP])
            link(V.tensor_scalar(hrow[32:40, :], t5[32:40, 0:TP], -1.0, None, ALU.mult))
            link(V.tensor_tensor(small_b[0:8, :].rearrange("p (b h) -> p b h", h=8),
                                 lf[0:8, TP:T][:, :, None].to_broadcast([8, NB, 8]),
                                 ident[0:8, None, 0:8].to_broadcast([8, NB, 8]), ALU.mult))
            dve.wait_ge(lf_in, 16 * PAGES * NB)
            lfp = lf_pages[:].rearrange("p g b h -> p g (b h)")
            V.memset(lf_later[:, PAGES - 1, :], 0.0)
            link(V.tensor_copy(lf_later[:, PAGES - 2, :], lfp[:, PAGES - 1, :]))
            for g in range(PAGES - 3, -1, -1):
                link(V.tensor_tensor(lf_later[:, g, :], lf_later[:, g + 1, :], lfp[:, g + 1, :], ALU.add))
            dve.sem_inc(later_in, 1)
            dve.wait_ge(later_sum, 1)
            V.tensor_copy(decay[:].rearrange("p b h g -> p g (b h)"),
                          ps[:, 6:8, :].rearrange("p k (g n) -> p (k g) n", g=8)).then_inc(decay_ready, 1)
            link(V.memset(qblk[:], 0.0))
            for h2 in range(2):
                r = slice(64 * h2, 64 * h2 + 64)
                last = V.tensor_scalar(qblk[r, :, :, h2], pj2[r, CD_Q:CD_Q + 4, TP:T], 64 ** -0.5, None, ALU.mult)
            link(last)
            V.tensor_tensor(small_a[:].rearrange("p (a b c) -> p a b c", a=4, b=NB), qblk[:],
                            pj2[:, CD_K:CD_K + 4, TP:T][:, :, :, None].to_broadcast([P, 4, NB, 2]), ALU.mult).then_inc(self_in, 1)
            link(V.memset(s_all[:, :, :, PAGES], NEG))
            dve.wait_ge(self_sum, 1)
            V.tensor_copy(s_all[0:1, :, :, PAGES].rearrange("p b (a c) -> p b a c", a=4),
                          ps[0:1, 5, 0:64].rearrange("p (a b c) -> p b a c", a=4, b=NB)).then_inc(s_ready_all, 1)
            dve.wait_ge(d_sig, 1)
            U = CD_GATE
            link(V.tensor_tensor(pj2[:, U:U + 4, :], pj2[:, U:U + 4, :], pj2[:, CD_A:CD_A + 4, :], ALU.mult))
            V.memset(upad[:, :, 0:U_PAD], 0.0)
            V.tensor_copy(upad[:, :, U_PAD:U_PAD + TP], pj2[:, U:U + 4, 0:TP])
            dve.wait_ge(conv_d_in, 16)
            link(V.tensor_copy(ext_d[:, :, :, CF_TAPS - 1], pj2[:, U:U + 4, TP:T]))

            dve.wait_ge(v_tok, 2)

            def unit_max(hp, u):
                tt = u % 4
                dve.wait_ge(s_ready, hp * 8 + u + 1)
                V.tensor_reduce(tiny[:, u % 2:u % 2 + 1], ps[:, u % 2, 0:P * (tt + 1)], AX, ALU.max, negate=True).then_inc(neg_max, 1)

            o0 = own[0]
            with dve.Fori(0, 4) as hp:
                dve.wait_ge(pv_done, hp * 8 + 2)
                V.tensor_scalar(q_st[:], pj2[:, bass.ds(hp, 1), 0:TP].rearrange("p o n -> p (o n)"), 64 ** -0.5, None, ALU.mult)
                V.tensor_copy(k_st[:], pj2[:, bass.ds(hp + CD_K, 1), 0:TP].rearrange("p o n -> p (o n)"))
                V.tensor_copy(v_st[:], vtok2[:, :, bass.ds(hp * P, P)])
                for h2 in range(2):
                    last = V.tensor_scalar(hsel[:, h2, :], hrow[:], pick[:, bass.ds(hp * 2 + h2, 1)], None, ALU.mult)
                last.then_inc(fox_staged, 1)
                unit_max(hp, 0)
                for u in range(8):
                    tt = u % 4
                    if u < 7:
                        unit_max(hp, u + 1)
                    dve.wait_ge(exp_done, hp * 8 + u + 3)
                    V.reciprocal(tiny[:, 4 + u % 2:5 + u % 2], tiny[:, 2 + u % 2:3 + u % 2]).then_inc(dve_own, 1)
                    dve.wait_ge(dve_own, hp * 8 + (o0 + u + 1))
                    V.tensor_scalar(prob[:, u % 2, 0:P * (tt + 1)], prob[:, u % 2, 0:P * (tt + 1)],
                                    tiny[:, 4 + u % 2:5 + u % 2], None, ALU.mult).then_inc(p_ready, 1)
            own[0] += 32

            wd = par_of("conv_d", 4 * CF_TAPS).rearrange("p (t j) -> p t j", j=CF_TAPS)
            V.tensor_tensor(prod_d[:], ext_d[:], wd[:, :, None, :].to_broadcast([P, 4, TS, CF_TAPS]), ALU.mult)
            for t in range(4):
                last = V.tensor_scalar(pj2[:, U + t, 0:TP], upad[:, t, 0:TP], wd[:, t, 0:1], None, ALU.mult)
            link(last)
            V.tensor_reduce(pj2[:, U:U + 4, TP:T], prod_d[:], AX, ALU.add)
            o1 = own[0]

            def taps(j, o):
                for t in range(4):
                    V.scalar_tensor_tensor(out=pj2[:, U + t, 0:TP], in0=upad[:, t, bass.ds(j, TP)], scalar=wd[:, t, bass.ds(j, 1)],
                                           in1=pj2[:, U + t, 0:TP], op0=ALU.mult, op1=ALU.add).then_inc(dve_own, 1)
                    if t == 3:
                        dve.wait_ge(dve_own, o)
            TAPS_K = 3
            with dve.Fori(0, NB) as b:
                for q in range(TAPS_K):
                    taps(b * TAPS_K + (1 + q), b * 4 * TAPS_K + (o1 + 4 * q + 4))
                dve.wait_ge(pages_free, b * 4 + 8)
                V.tensor_tensor(s_all[:, bass.ds(b, 1), :, 0:PAGES].rearrange("p o (a c) g -> p (o a) c g", a=4),
                                ps[:, bass.ds(b, 1), 0:P].rearrange("p o (a g c) -> p (o a) c g", a=4, c=2),
                                decay[:, bass.ds(b, 1)].rearrange("p o (a c) g -> p (o a) c g", a=4), ALU.add).then_inc(s_ready_all, 1)
            own[0] += NB * 4 * TAPS_K
            dve.wait_ge(s_ready_all, NB + 1)
            sa = s_all[:].rearrange("p b h g -> p (b h) g")
            V.tensor_reduce(small_a[:], sa, AX, ALU.max).then_inc(m_turned, 1)
            dve.wait_ge(m_turned, 2)
            link(V.tensor_reduce(small_c[0:64, 0:1], ps[0:64, 5, 0:P], AX, ALU.max))
            V.tensor_scalar(small_b[0:64, :], ident[0:64, 0:64], small_c[0:64, 0:1], None, ALU.mult).then_inc(m_diag, 1)
            dve.wait_ge(m_cast, 1)
            V.tensor_tensor(sa, sa, ps[:, 6, 0:64][:, :, None].to_broadcast([P, 64, PAGES + 1]), ALU.subtract).then_inc(s_shifted, 1)
            dve.wait_ge(p_all, 1)
            V.tensor_reduce(small_c[:], sa, AX, ALU.add).then_inc(l_part, 1)
            dve.wait_ge(l_sum, 1)
            link(V.reciprocal(small_d[:], ps[:, 7, 0:64]))
            o1 = own[0]
            j0 = 1 + NB * TAPS_K
            with dve.Fori(0, CF_TAPS - j0) as i:
                taps(i + j0, i * 4 + (o1 + 4))
            own[0] += 4 * (CF_TAPS - j0)
            dve.sem_inc(d_u, 1)
            dve.wait_ge(self_cast, 1)
            dve.wait_ge(pv_all, 1)
            for h2 in range(2):
                r = slice(64 * h2, 64 * h2 + 64)

                def of(ap):
                    return ap.rearrange("p (b a c) -> p a b c", b=NB, a=4)[:, :, :, h2]
                acc_o = small_a[r, 0:32].rearrange("p (a b) -> p a b", a=4)
                link(V.tensor_tensor(acc_o, of(ps[r, 6, 64:128]), pj2[r, CD_V:CD_V + 4, TP:T], ALU.mult))
                link(V.tensor_tensor(acc_o, acc_o, of(ps[r, 0, 0:64]), ALU.add))
                last = V.tensor_tensor(pj2[r, CD_Q:CD_Q + 4, TP:T], acc_o, of(small_d[r, :]), ALU.mult)
            last.then_inc(y_cd, 1)
            normalise(D_LN, lambda k: pj2[:, CD_GATE + k, :], 4)
            rest_rows(lambda k: pj2[:, k if k < 4 else CD_GATE + k - 4, :], 4 * KD)
            residual_tiles("cd_out")
            normalise(3, x_rows, KD)
            rest_rows(x_rows, 5 * KD)
            hidden("f1_in")
            residual_tiles("f1_out")
            normalise(4, x_rows, KD)


D_LN = 2
LN_BASE = [0, 8, 16, 20, 28]
NEXT = {"ab_in": "ab_out", "ab_out": "f0_in", "f0_in": "f0_out", "f0_out": "cd_in", "cd_in": "cd_out",
        "cd_out": "f1_in", "f1_in": "f1_out", "f1_out": None}
OUT_AB = 4
OUT_CD = 8

_OUTS = {
    "y": (P, KD, T), "conv_a_p": (P, 4, 2), "conv_a_s": (P, 4, TS, 2), "gla_p": (P, 2, P), "gla_s": (P, NB, 2, P),
    "kt": (P, 4, T), "vt": (P, 4, T), "logf": (8, T), "conv_d_p": (P, 4, 30), "conv_d_s": (P, 4, TS, 30),
}


def _chunks(a):
    return np.moveaxis(a.reshape((a.shape[0] // P, P) + a.shape[1:]), 0, 1)


def _slots(w, blocks):
    parts = w.shape[0] // (P * blocks)
    w = w.reshape(parts, blocks, P, w.shape[1] // P, P)
    return np.ascontiguousarray(w.transpose(3, 0, 2, 1, 4)).reshape(-1, P, blocks * P)


def _constants():
    c = np.zeros((P, CONST_COLS), np.float32)
    i = np.arange(P)
    c[:, 0:128] = np.eye(P)
    c[:, 128:256] = 1.0
    c[:, 256:384] = i[:, None] > i[None, :]
    c[:, 384:896] = np.arange(TP) % P != 0
    c[0:8, 896:904] = np.eye(8)
    c[32:40, 896:904] = np.eye(8)
    c[:, 904:1032] = np.where(i[None, :] > i[:, None], NEG, 0.0)
    m = np.zeros((P, IMASK_COLS), np.int32)
    for l in range(LEVELS):
        half = P >> (l + 1)
        t = i[(i % (2 * half)) >= half]
        s = i[:, None]
        m[:, 64 * l:64 * l + 64] = (s // (2 * half) == t // (2 * half)) & (s % (2 * half) < half)
    m[:, 64 * LEVELS:] = np.eye(P)
    return c, m


def kernel(x_prompt, x_sample, state_conv_a, state_gla, cache_k, cache_v, cache_logf, state_conv_d, page_table,
           ab_w_in, ab_conv_w, gla_w_gate2, gla_b_gate, gla_norm_g, ab_w_out,
           cd_w_in, fox_b_f, cf_conv_w, cf_conv_b, cf_ln_g, cf_ln_b, cd_w_out,
           ffn_w_in, ffn_w_out, ln_g, ln_b):
    import concourse.bacc as _bacc
    from concourse import mybir as _mybir
    from concourse.bass_utils import run_bass_kernel_spmd as _run

    def arr(a):
        return np.asarray(a)

    arrays = {}
    tokens = np.concatenate([arr(x_prompt)[0], arr(x_sample)[:, 0]], 0)
    arrays["xt"] = _chunks(tokens.T)
    w = arr(ab_w_in)
    bg, cg, hv, q, k, v, g, r = np.split(w, np.cumsum([512, 512, 512, 256, 256, 512, 512]), axis=1)
    arrays["w_ab_in"] = _slots(np.concatenate([v, q, k, g, cg, hv, bg], 1), KD)
    arrays["w_ab_out"] = _slots(arr(ab_w_out), KD)
    cq, ck, cv, cf, ca, cgate = np.split(arr(cd_w_in), np.cumsum([512, 512, 512, 8, 512]), axis=1)
    arrays["w_cd_in"] = _slots(np.concatenate([cq, ck, cv, cgate, ca], 1), KD)
    arrays["w_cd_out"] = _slots(arr(cd_w_out), KD)
    for l in range(2):
        wi = arr(ffn_w_in)[l].reshape(D, 2, KF, P).transpose(0, 2, 1, 3).reshape(D, 2 * DFF)
        arrays[f"w_f{l}_in"] = _slots(wi, KD)
        arrays[f"w_f{l}_out"] = _slots(arr(ffn_w_out)[l], HALF_KF)
    par = np.zeros((P, PARAM_COLS), np.float32)

    def put(name, a, rows=slice(0, P)):
        a = np.asarray(a)
        a = a.reshape(a.shape[0], -1)
        par[rows, PARAM_AT[name]:PARAM_AT[name] + a.shape[1]] = a

    put("ln_g", _chunks(arr(ln_g).reshape(4, D).T).transpose(0, 2, 1))
    put("ln_b", _chunks(arr(ln_b).reshape(4, D).T).transpose(0, 2, 1))
    put("conv_a", _chunks(arr(ab_conv_w).T))
    put("conv_d", _chunks(arr(cf_conv_w).T))
    put("cf_b", _chunks(arr(cf_conv_b)))
    put("cf_g", _chunks(arr(cf_ln_g)))
    put("cf_lb", _chunks(arr(cf_ln_b)))
    put("b_gate", _chunks(arr(gla_b_gate)))
    put("norm_g", arr(gla_norm_g)[:, None])
    put("b_f", arr(fox_b_f)[:, None], slice(0, 8))
    put("b_f", arr(fox_b_f)[:, None], slice(32, 40))
    put("w_gate2", arr(gla_w_gate2), slice(0, 16))
    put("w_r", _chunks(r))
    wf = np.zeros((D, 40), np.float32)
    wf[:, 0:8] = cf
    wf[:, 32:40] = cf
    put("w_f", _chunks(wf))
    arrays["params"] = par
    arrays["consts"], arrays["imask"] = _constants()
    arrays["table"] = arr(page_table).astype(np.int32).reshape(1, -1)
    arrays["conv_a_state"] = arr(state_conv_a).reshape(TS, 2, 4, P).transpose(3, 2, 0, 1)
    arrays["conv_d_state"] = arr(state_conv_d).reshape(TS, 30, 4, P).transpose(3, 2, 0, 1)
    arrays["gla_state"] = arr(state_gla).reshape(NB, 2, 2, 64, P).transpose(2, 3, 0, 1, 4).reshape(P, NB, 2, P)
    arrays["cache_kt"] = arr(cache_k).reshape(PHYS, P, 4, P).transpose(0, 3, 2, 1).reshape(PHYS, P, 512)
    arrays["cache_v"] = arr(cache_v).reshape(PHYS, P, 512)
    arrays["cache_logf"] = arr(cache_logf)

    nc = _bacc.Bacc("TRN2", target_bir_lowering=False, num_devices=1)
    A, O, feed = {}, {}, {}
    for name, a in arrays.items():
        a = np.ascontiguousarray(a)
        feed[f"in_{name}"] = a
        A[name] = nc.dram_tensor(f"in_{name}", a.shape, _mybir.dt.from_np(a.dtype), kind="ExternalInput").ap()
    for name, shape in _OUTS.items():
        O[name] = nc.dram_tensor(f"out_{name}", shape, F32, kind="ExternalOutput").ap()
    bass_hybrid_step(nc, A, O)
    res = _run(nc, [feed], core_ids=[0]).results[0]
    o = {n: np.asarray(res[f"out_{n}"]) for n in _OUTS}

    def rows(a):
        return np.ascontiguousarray(a.transpose(2, 1, 0)).reshape(a.shape[2], -1)

    y, kt, vt, lf = rows(o["y"]), rows(o["kt"]), rows(o["vt"]), o["logf"].T
    conv_a_p = np.ascontiguousarray(o["conv_a_p"].transpose(2, 1, 0)).reshape(1, 2, 512)
    conv_a_s = np.ascontiguousarray(o["conv_a_s"].transpose(2, 3, 1, 0)).reshape(NB, 2, 512)
    conv_d_p = np.ascontiguousarray(o["conv_d_p"].transpose(2, 1, 0)).reshape(1, 30, 512)
    conv_d_s = np.ascontiguousarray(o["conv_d_s"].transpose(2, 3, 1, 0)).reshape(NB, 30, 512)
    gla_p = np.ascontiguousarray(o["gla_p"].reshape(2, 64, 2, P).transpose(2, 0, 1, 3)).reshape(1, 4, 64, P)
    gla_s = np.ascontiguousarray(o["gla_s"].reshape(2, 64, NB, 2, P).transpose(2, 3, 0, 1, 4)).reshape(NB, 4, 64, P)

    def heads(a, n):
        return np.ascontiguousarray(a).reshape(n + (8, 64))

    return (y[None, :TP], y[TP:, None], conv_a_p, conv_a_s, gla_p, gla_s,
            heads(kt[:TP], (1, TP)), heads(kt[TP:], (TS, 1)), heads(vt[:TP], (1, TP)), heads(vt[TP:], (TS, 1)),
            np.ascontiguousarray(lf[None, :TP]), np.ascontiguousarray(lf[TP:, None]), conv_d_p, conv_d_s)
```

```python
from contextlib import ExitStack

import numpy as np
import concourse.bass as bass
from concourse import mybir

F32 = mybir.dt.float32
F32R = mybir.dt.float32r
BF16 = mybir.dt.bfloat16
I32 = mybir.dt.int32
ALU = mybir.AluOpType
ACT = mybir.ActivationFunctionType
AX = mybir.AxisListType.X

P = 128
D = 1024
KD = D // P
TP = 512
TS = 8
T = TP + TS
HT = T // 2
NB = 8
PAGES = 16
PHYS = 160
DFF = 2816
KF = DFF // P
HALF_KF = KF // 2
ALPHA = float(4 ** 0.25)
EPS = 1e-5
GUESS = 3
CENTERED = (3, 4, 0, 5, 1, 6, 2, 7)
NEG = -1e30
GC = TP // P
LEVELS = 7
CF_TAPS = 31
RAW = 4
SPLIT = 2
TILES_AB = 24
TILES_CD = 20
AB_V, AB_Q, AB_K, AB_G, AB_CG, AB_HV, AB_BG = 0, 4, 6, 8, 12, 16, 20
CD_Q, CD_K, CD_V, CD_GATE, CD_A = 0, 4, 8, 12, 16

_PARAMS = [("ln_g", 32), ("ln_b", 32), ("conv_a", 12), ("conv_d", 124), ("cf_b", 4), ("cf_g", 4), ("cf_lb", 4),
           ("b_gate", 2), ("norm_g", 1), ("b_f", 1), ("w_gate2", 256), ("w_r", 128), ("w_f", 320)]
PARAM_AT, _n = {}, 0
for _name, _w in _PARAMS:
    PARAM_AT[_name] = _n
    _n += _w
PARAM_COLS = _n
CONST_AT = {"ident": 0, "ones": 128, "later": 256, "scan": 384, "pick": 896, "causal": 904}
CONST_COLS = 904 + 128
IMASK_COLS = LEVELS * 64 + 128


def bass_hybrid_step(nc, A, O):
    with ExitStack() as ctx:
        base = (nc.sbuf_base + 31) // 32 * 32

        def at(name, shape, offset, dt=F32):
            return nc.alloc_sbuf_tensor_at(name, shape, dt, offset=base + offset)

        def sem(name):
            return ctx.enter_context(nc.semaphore(name))

        TB = T * 4
        x = at("x", [P, KD, T], 0)
        o_xs = KD * TB
        xh = at("xh", [P, KD, T], o_xs, F32R)
        xl = at("xl", [P, KD, T], o_xs + KD * TB, F32R)
        o_w = o_xs + 2 * KD * TB
        SLOT = HALF_KF * P
        raw = at("raw", [P, RAW, SLOT], o_w)
        wh = at("wh", [P, SPLIT, SLOT], o_w + RAW * SLOT * 4, F32R)
        wl = at("wl", [P, SPLIT, SLOT], o_w + (RAW + SPLIT) * SLOT * 4, F32R)
        o_z = o_w + (RAW + 2 * SPLIT) * SLOT * 4
        zone = 2 * KF * TB
        o_s = o_z + zone
        small = [o_s]

        def keep(name, shape, dt=F32):
            n = int(np.prod(shape[1:])) * (2 if dt == BF16 else 4)
            t = at(name, shape, small[0], dt)
            small[0] += (n + 31) // 32 * 32
            return t

        par = keep("par", [P, PARAM_COLS])
        con = keep("con", [P, CONST_COLS])
        imask = keep("imask", [P, IMASK_COLS], I32)
        table = keep("table", [1, NB * PAGES], I32)
        ident_b = keep("ident_b", [P, P], BF16)
        causal_b = keep("causal_b", [P, P], BF16)
        rstd = keep("rstd", [P, T])
        conv_a_state = keep("conv_a_state", [P, 4, TS, 2])
        lf_pages = keep("lf_pages", [P, PAGES, NB, 8])
        qblk = keep("qblk", [P, 4, NB, 2])
        q_wide = keep("q_wide", [P, 2, 4 * 34])
        small_a = keep("small_a", [P, 64])
        small_b = keep("small_b", [P, 64])
        small_c = keep("small_c", [P, 64])
        small_d = keep("small_d", [P, 64])
        tiny = keep("tiny", [P, 16])
        zeros = keep("zeros", [P, P])
        eps_c = keep("eps_c", [P, 1])
        assert base + small[0] <= nc.sbuf_usable_end, (base + small[0], nc.sbuf_usable_end)

        def par_of(name, w):
            return par[:, PARAM_AT[name]:PARAM_AT[name] + w]

        ident = con[:, 0:128]
        ones = con[:, 128:256]
        later = con[:, 256:384]
        scan_on = con[:, 384:896]
        pick = con[:, 896:904]

        hh = at("hh", [P, KF, T], o_z, F32R)
        hl = at("hl", [P, KF, T], o_z + KF * TB, F32R)
        o_gate_t = small[0]
        gate_t = keep("gate_t", [P, T])
        hid_t = keep("hid_t", [P, T])
        assert base + small[0] <= nc.sbuf_usable_end, (base + small[0], nc.sbuf_usable_end)

        pj = at("pj", [P, TILES_AB, T], o_z)
        o_g = o_z + TILES_AB * TB
        attn = at("attn", [P, GC * 4, P], o_g)
        vtok = at("vtok", [P, GC, 512], o_g + 8192)
        kwtok = at("kwtok", [P, GC, 256], o_g + 16384)
        gla_s = at("gla_s", [P, GC, 2, P], o_g + 20480)
        gla_o = at("gla_o", [P, 4, T], o_g + 24576)
        gla_s0 = at("gla_s0", [P, NB, 2, P], o_g + 24576 + 8320)
        assert 24576 + 8320 + 8192 + TILES_AB * TB <= zone
        rms_r = at("rms_r", [P, 4 * T], o_g)
        gla_kv = at("gla_kv", [P, NB, 2, P], o_z + AB_V * TB)
        rms_sq = at("rms_sq", [P, 4 * T], o_z + AB_Q * TB)
        loga = at("loga", [P, 2, T], o_xs)
        gcum = at("gcum", [P, 2, TP], o_xs + 4160)
        gdiff = at("gdiff", [P, 2, 2, TP], o_xs + 8256)
        qk = at("qk", [P, 2, 2, TP], o_xs + 16448)
        zpre = at("zpre", [P, 2, T], o_xs + 24640)
        zexp = at("zexp", [P, 2, T], o_xs + 28800)
        r_t = at("r_t", [16, T], o_g + 24576)
        vsam = at("vsam", [NB, 512], o_xs + 24640)
        assert 28800 + 4160 <= 2 * KD * TB

        pj2 = at("pj2", [P, TILES_CD, T], o_z)
        U_PAD = CF_TAPS - 1
        upad = at("upad", [P, 4, U_PAD + TP], o_z + CD_A * TB)
        o_k = o_z + TILES_CD * TB + 384
        assert 4 * (U_PAD + TP) * 4 <= 4 * TB + 384
        pages = at("pages", [P, 4, 4, 512], o_k)
        o_d = o_k + 32768
        lf_later = at("lf_later", [P, PAGES, 64], o_d)
        frow = [at(f"frow{i}", [40, T], o) for i, o in enumerate((o_gate_t, o_gate_t + TB, o_d + 8448, o_d + 8448 + TB,
                                                                  o_d + 8448 + 2 * TB))]
        squares_d = at("squares_d", [P, 4, T], o_k)
        s_all = at("s_all", [P, NB, 8, PAGES + 1], o_k + 32768)
        decay = at("decay", [P, NB, 8, PAGES], o_k + 32768 + 4352)
        ext_d = at("ext_d", [P, 4, TS, 31], o_k + 32768 + 8448)
        prod_d = at("prod_d", [P, 4, TS, 31], o_k + 32768 + 8448 + 3968)
        assert TILES_CD * TB + 384 + 32768 + 8448 + 7936 <= zone
        vtok2 = at("vtok2", [P, GC, 512], o_xs)
        prob = at("prob", [P, 2, 512], o_xs + 8192)
        prob_t = at("prob_t", [P, 2, 512], o_xs + 12288)
        q_st = at("q_st", [P, 512], o_xs + 16384)
        v_st = at("v_st", [P, GC, P], o_xs + 18432)
        grow = at("grow", [P, 512], o_xs + 20480)
        hrow = at("hrow", [P, 512], o_xs + 22528)
        hsel = at("hsel", [P, 2, 512], o_xs + 24576)
        k_st = at("k_st", [P, 512], o_xs + 28672)
        score_rows = at("score_rows", [P, 512], o_d + 8448 + TB)
        v_rows = at("v_rows", [P, 512], o_xs + 30720)
        assert 30720 + 2048 <= 2 * KD * TB
        p_blocks = at("p_blocks", [P, 2, PAGES, 32], o_d + 4352)

        ps = ctx.enter_context(nc.psum_tensor("ps", [P, 8, 512], F32))


        x_in = sem("x_in")
        par_in = sem("par_in")
        state_in = sem("state_in")
        conv_d_in = sem("conv_d_in")
        w_landed = [sem(f"w_landed{i}") for i in range(RAW)]
        w_rounded = sem("w_rounded")
        w_rest = sem("w_rest")
        slot_used = sem("slot_used")
        x_hi = sem("x_hi")
        x_split = sem("x_split")
        acc_free = [sem(f"acc_free{i}") for i in range(2)]
        dve_own = sem("dve_own")
        act_own = sem("act_own")
        pool_own = sem("pool_own")
        setup = sem("setup")
        ln_in = sem("ln_in")
        ln_first = sem("ln_first")
        ln_guess = sem("ln_guess")
        ln_part = sem("ln_part")
        ln_added = sem("ln_added")
        ln_sum = sem("ln_sum")
        ln_centered = sem("ln_centered")
        ln_sq = sem("ln_sq")
        ln_var = sem("ln_var")
        ln_veps = sem("ln_veps")
        ln_std = sem("ln_std")
        ln_scaled = sem("ln_scaled")
        ln_out = sem("ln_out")
        gate_ready = sem("gate_ready")
        hid_ready = sem("hid_ready")
        hid_hi = sem("hid_hi")
        hid_split = sem("hid_split")
        out_sent = sem("out_sent")
        y_sent = sem("y_sent")
        logf_sent = sem("logf_sent")
        r_sum, r_copied, z_sum, z_pre, z_log, log_a = (sem(n) for n in ("r_sum", "r_copied", "z_sum", "z_pre", "z_log", "log_a"))
        v_turned, v_tok = sem("v_turned"), sem("v_tok")
        lv_diff, lv_exp, lv_qk, lv_scores, lv_kept = (sem(n) for n in ("lv_diff", "lv_exp", "lv_qk", "lv_scores", "lv_kept"))
        attn_zero = sem("attn_zero")
        kw_diff, kw_exp, kw_ready, kw_turned, kw_tok = (sem(n) for n in ("kw_diff", "kw_exp", "kw_ready", "kw_turned", "kw_tok"))
        kv_sum, state_c, o_sum, o_copied = (sem(n) for n in ("kv_sum", "state_c", "o_sum", "o_copied"))
        sam_decay, vsam_turned, vsam_copied, vb_sum, vb_used, sam_state, sam_o = (
            sem(n) for n in ("sam_decay", "vsam_turned", "vsam_copied", "vb_sum", "vb_used", "sam_state", "sam_o"))
        rms_squared, rms_sum, rms_eps, rms_std, g_silu, y_ab = (
            sem(n) for n in ("rms_squared", "rms_sum", "rms_eps", "rms_std", "g_silu", "y_ab"))
        conv_a_ready = sem("conv_a_ready")
        f_sum, f_pre, f_log, f_done, later_in, later_sum, decay_ready, rows_used, q_staged, ks_copied, kt_done, p_staged, v_masked = (
            sem(n) for n in ("f_sum", "f_pre", "f_log", "f_done", "later_in", "later_sum", "decay_ready", "rows_used", "q_staged", "ks_copied",
                          "kt_done", "p_staged", "v_masked"))
        fox_staged, s_ready, neg_max, exp_done, p_ready, p_turned, pt_copied, pv_done, o_evac = (
            sem(n) for n in ("fox_staged", "s_ready", "neg_max", "exp_done", "p_ready", "p_turned", "pt_copied", "pv_done", "o_evac"))
        self_in, self_sum = sem("self_in"), sem("self_sum")
        page_in = [sem(f"page_in{i}") for i in range(4)]
        lf_in = sem("lf_in")
        pages_free = sem("pages_free")
        s_ready_all, m_turned, m_diag, m_cast, s_shifted, p_all, l_part, l_sum, pv_all, self_cast = (
            sem(n) for n in ("s_ready_all", "m_turned", "m_diag", "m_cast", "s_shifted", "p_all", "l_part", "l_sum", "pv_all", "self_cast"))
        d_sig, d_tap, d_u, y_cd = (sem(n) for n in ("d_sig", "d_tap", "d_u", "y_cd"))

        block = ctx.enter_context(nc.Block())

        PH = {}
        s0 = t0 = 0
        for name, slots, tiles in (("ab_in", 24, 24), ("ab_out", 8, 8), ("f0_in", 44, 44), ("f0_out", 16, 8),
                                   ("cd_in", 20, 20), ("cd_out", 8, 8), ("f1_in", 44, 44), ("f1_out", 16, 8)):
            PH[name] = (s0, slots, t0, tiles)
            s0, t0 = s0 + slots, t0 + tiles
        SLOTS = s0
        BLOCKS = {"f0_out": HALF_KF, "f1_out": HALF_KF}

        def halves(ap):
            return ap.rearrange("p (h n) -> p h n", h=2)

        @block.sync
        def _(sp):
            for c in range(2):
                sp.dma_start(x[:, 4 * c:4 * c + 4, :], A["xt"][:, 4 * c:4 * c + 4, :]).then_inc(x_in, 16)
            sp.dma_start(par[:], A["params"]).then_inc(par_in, 16)
            sp.dma_start(con[:], A["consts"]).then_inc(par_in, 16)

            def weights(name, i, first=False):
                for j in range(RAW):
                    weight_slot(name, i, j, first)

            def weight_slot(name, i, j, first=False):
                if not first:
                    sp.wait_ge(w_rest, PH[name][0] + 4 * i + j + 1 - RAW)
                src = A["w_" + name][bass.ds(4 * i + j, 1)].rearrange("o p n -> p (o n)")
                sp.dma_start(raw[:, j, 0:BLOCKS.get(name, KD) * P], src).then_inc(w_landed[j], 16)

            weights("ab_in", 0, first=True)
            sp.dma_start(imask[:], A["imask"]).then_inc(state_in, 16)
            sp.dma_start(table[:], A["table"]).then_inc(state_in, 16)
            sp.dma_start(conv_a_state[:], A["conv_a_state"]).then_inc(state_in, 16)
            sp.dma_start(gla_s0[:], A["gla_state"]).then_inc(state_in, 16)
            with sp.Fori(1, 6) as i:
                weights("ab_in", i)
            with sp.Fori(0, 2) as i:
                weights("ab_out", i)
            sp.wait_ge(state_in, 64)
            with sp.Fori(0, NB) as i:
                weights("f0_in", i)
                for g in range(PAGES):
                    if g % 8 == 0:
                        ids = nc.values_load_multi_w_load_instructions(
                            table[0:1, bass.ds(i * PAGES + g, 8)], engines=(mybir.EngineType.SP,),
                            min_val=0, max_val=PHYS - 1)[1]
                    sp.dma_start(lf_pages[:, g, bass.ds(i, 1), :].rearrange("p o h -> p (o h)"),
                                 A["cache_logf"][bass.ds(ids[g % 8], 1)].rearrange("o p h -> p (o h)")).then_inc(lf_in, 16)
            with sp.Fori(NB, 11) as i:
                weights("f0_in", i)
            with sp.Fori(0, 4) as i:
                weights("f0_out", i)
            for i in range(2):
                weights("cd_in", i)

            def page_slots(cache, n, used):
                ids = nc.values_load_multi_w_load_instructions(
                    table[0:1, bass.ds(n, 8)], engines=(mybir.EngineType.SP,), min_val=0, max_val=PHYS - 1)[1]
                for h, count in enumerate(used):
                    sp.wait_ge(pages_free, count + 1)
                    s = used_slot[0] % 4
                    used_slot[0] += 1
                    for g in range(4):
                        sp.dma_start(pages[:, s, g, :], cache[bass.ds(ids[4 * h + g], 1)].rearrange("o p n -> p (o n)"))\
                          .then_inc(page_in[s], 16)

            used_slot = [0]

            def weights_and_keys(i, name, k):
                for j in range(4):
                    weight_slot(name, k, j)
                    page_slots(A["cache_kt"], (i - 1) * 32 + 8 * j, [(i - 1) * 8 + (2 * j), (i - 1) * 8 + (2 * j + 1)])

            with sp.Fori(1, 4) as i:
                weights_and_keys(i, "cd_in", i + 1)
            weights_and_keys(4, "cd_out", 0)

            def values(b):
                for half in range(2):
                    page_slots(A["cache_v"], b * PAGES + 8 * half, [b * 4 + (32 + 2 * half), b * 4 + (33 + 2 * half)])

            values(0)
            sp.wait_ge(rows_used, 1)
            sp.wait_ge(logf_sent, 16)
            sp.dma_start(ext_d[:, :, :, 0:CF_TAPS - 1], A["conv_d_state"]).then_inc(conv_d_in, 16)
            with sp.Fori(1, NB) as b:
                values(b)
            weights("cd_out", 1)
            with sp.Fori(0, 11) as i:
                weights("f1_in", i)
            with sp.Fori(0, 4) as i:
                weights("f1_out", i)
            sp.wait_ge(ln_out, 4 * KD + 4)
            sp.dma_start(O["y"], x[:]).then_inc(y_sent, 16)
            sp.wait_ge(y_sent, 16)
            sp.wait_ge(out_sent, 16 * OUT_CD)

        @block.scalar
        def _(act):
            own = [0]

            def link(ins):
                own[0] += 1
                ins.then_inc(act_own, 1)
                act.wait_ge(act_own, own[0])

            act.wait_ge(par_in, 32)
            nc.scalar.activation(ident_b[:], ident, ACT.Copy)
            nc.scalar.activation(causal_b[:], con[:, 904:1032], ACT.Copy).then_inc(setup, 1)
            act.wait_ge(setup, 2)
            act.sem_inc(exp_done, 2)
            act.sem_inc(pt_copied, 2)
            act.sem_inc(ks_copied, 2)

            def rounded(i4, n, j, b):
                act.wait_ge(w_landed[j], i4)
                act.wait_ge(slot_used, n + 1)
                nc.scalar.activation(wh[:, j % SPLIT, 0:b * P], raw[:, j, 0:b * P], ACT.Copy).then_inc(w_rounded, 1)

            def next_rounded(name, i, j, last):
                s = PH[name][0]
                b = BLOCKS.get(name, KD)
                if last and j >= 4 - SPLIT:
                    if NEXT[name] is None:
                        return
                    b = BLOCKS.get(NEXT[name], KD)
                group = s // 4 + i + (j + SPLIT) // 4
                rounded(group * 16 + 16, s + 4 * i + j + SPLIT, (j + SPLIT) % 4, b)

            def product(name, tile=None, peeled=1, behind_first=None):
                n = PH[name][1] // 4
                start = 0
                if behind_first:
                    for j in range(4):
                        next_rounded(name, 0, j, False)
                    behind_first()
                    for j in range(4):
                        next_rounded(name, 1, j, False)
                        tile(1, j)
                    start = 2
                if n > peeled:
                    with act.Fori(start, n - peeled) as i:
                        for j in range(4):
                            next_rounded(name, i, j, False)
                            if tile and peeled == 1:
                                tile(i, j)
                for i in range(n - peeled, n):
                    for j in range(4):
                        next_rounded(name, i, j, i == n - 1)
                        if tile:
                            tile(i, j)

            def split_rows(src, k):
                nc.scalar.activation(xh[:, k, :], src, ACT.Copy).then_inc(x_hi, 1)

            def normalise_d():
                g, b = par_of("cf_g", 4), par_of("cf_lb", 4)
                base = LN_BASE[D_LN]
                for k in range(4):
                    act.wait_ge(ln_centered, base + k + 1)
                    nc.scalar.activation(squares_d[:, k, :], pj2[:, CD_GATE + k, :], ACT.Square).then_inc(ln_sq, 1)
                act.wait_ge(ln_veps, D_LN + 1)
                nc.scalar.activation(rstd[:], rstd[:], ACT.Sqrt, bias=eps_c[:, 0:1]).then_inc(ln_std, 1)
                for k in range(4):
                    act.wait_ge(ln_scaled, base + k + 1)
                    nc.scalar.activation(pj2[:, CD_GATE + k, :], pj2[:, CD_GATE + k, :], ACT.Silu,
                                         bias=b[:, k:k + 1], scale=g[:, k:k + 1]).then_inc(ln_out, 1)

            def squares_of(idx):
                base, of_d = LN_BASE[idx], LN_OF[idx]

                def after_tile(m):
                    for i in ((0, 1, 2) if m == 4 else (3, 4) if m == 5 else (5, 6) if m == 6 else (7,) if m == 7 else ()):
                        act.wait_ge(ln_centered, base + i + 1)
                        if i >= 2:
                            act.wait_ge(ln_added, 6 * of_d + i - 1)
                        nc.scalar.activation((gate_t if i == 0 else hid_t)[:], x[:, CENTERED[i], :], ACT.Square).then_inc(ln_sq, 1)
                return after_tile

            def product_and_squares(name, idx):
                after_tile = squares_of(idx)
                if name in BLOCKS:
                    product(name, lambda i, j: after_tile(2 * i + j // 2) if j % 2 == 1 else None, peeled=2)
                else:
                    product(name, lambda i, j: after_tile(4 * i + j))

            def normalise_x(idx, split):
                at_g, at_b = (PARAM_AT[n] + 8 * LN_OF[idx] for n in ("ln_g", "ln_b"))
                base = LN_BASE[idx]
                act.wait_ge(ln_veps, idx + 1)
                nc.scalar.activation(rstd[:], rstd[:], ACT.Sqrt, bias=eps_c[:, 0:1]).then_inc(ln_std, 1)
                for k in range(KD + 1):
                    if k < KD:
                        act.wait_ge(ln_scaled, base + k + 1)
                        nc.scalar.activation(x[:, k, :], x[:, k, :], ACT.Identity, bias=par[:, at_b + k:at_b + k + 1],
                                             scale=par[:, at_g + k:at_g + k + 1]).then_inc(ln_out, 1)
                    if k > 0 and split:
                        act.wait_ge(ln_out, base + k)
                        split_rows(x[:, k - 1, :], k - 1)

            def gate_up(name):
                s, _, _, _ = PH[name]
                m0 = 0 if name == "f0_in" else 22

                def tile(i, j):
                    m = i * 2 + j // 2
                    act.wait_ge(slot_used, i * 4 + (SPLIT + s + j + 1))
                    if j % 2 == 0:
                        act.wait_ge(hid_ready, m0 + m)
                        nc.scalar.activation(halves(gate_t[:]), ps[:, 0:2, 0:HT], ACT.Silu).then_inc(gate_ready, 1)
                        act.wait_ge(gate_ready, m0 + m + 1)
                        nc.scalar.sem_inc(acc_free[0], 1)
                    else:
                        act.wait_ge(hid_ready, m0 + m + 1)
                        nc.scalar.activation(hh[:, bass.ds(m, 1), :].rearrange("p o n -> p (o n)"), hid_t[:], ACT.Copy)\
                            .then_inc(hid_hi, 1)
                return tile

            for j in range(SPLIT):
                rounded(16, j, j, KD)
            for k in range(KD):
                act.wait_ge(x_in, 32)
                split_rows(x[:, k, :], k)
            product("ab_in")

            act.wait_ge(z_sum, 1)
            for t in range(2):
                last = nc.scalar.activation(halves(zpre[:, t, :]), ps[:, 4 + 2 * t:6 + 2 * t, 0:HT], ACT.Identity,
                                            bias=par[:, PARAM_AT["b_gate"] + t:PARAM_AT["b_gate"] + t + 1])
            link(last)
            link(nc.scalar.activation(zexp[:], zpre[:], ACT.Abs))
            link(nc.scalar.activation(zexp[:], zexp[:], ACT.Exp, scale=-1.0))
            nc.scalar.activation(zexp[:], zexp[:], ACT.Ln, bias=1.0).then_inc(z_log, 1)
            act.wait_ge(v_turned, 1)
            for c in range(GC):
                last = nc.scalar.activation(vtok[:, c, :], ps[:, c, :], ACT.Copy)
            last.then_inc(v_tok, 1)
            act.wait_ge(vsam_turned, 1)
            act.wait_ge(log_a, 1)
            nc.scalar.activation(vsam[:], ps[0:NB, 7, :], ACT.Copy).then_inc(vsam_copied, 1)
            nc.scalar.activation(tiny[:].rearrange("p (a b) -> p a b", a=2), loga[:, :, TP:T], ACT.Exp).then_inc(sam_decay, 1)
            for l in range(LEVELS):
                act.wait_ge(lv_diff, l + 1)
                nc.scalar.activation(gdiff[:, l % 2], gdiff[:, l % 2], ACT.Exp).then_inc(lv_exp, 1)
            act.wait_ge(kw_diff, 1)
            nc.scalar.activation(gdiff[:, 0], gdiff[:, 0], ACT.Exp)
            nc.scalar.activation(gdiff[:, 1], gcum[:], ACT.Exp).then_inc(kw_exp, 1)
            act.wait_ge(kw_turned, 1)
            for c in range(GC):
                last = nc.scalar.activation(kwtok[:, c, :], ps[:, 4 + c // 2, 256 * (c % 2):256 * (c % 2) + 256], ACT.Copy)
            last.then_inc(kw_tok, 1)
            for c in range(GC):
                act.wait_ge(o_sum, c + 1)
                nc.scalar.activation(gla_o[:, :, P * c:P * c + P].rearrange("p (a c) t -> p c a t", c=2),
                                     ps[:, 2 * (c % 2):2 * (c % 2) + 2, 0:256].rearrange("p c (a t) -> p c a t", a=2),
                                     ACT.Copy).then_inc(o_copied, 1)
            act.wait_ge(sam_o, 1)
            link(nc.scalar.activation(gla_o[:, :, TP:T].rearrange("p (a c) b -> p c a b", c=2),
                                      ps[:, 0:2, 0:2 * TS].rearrange("p c (a b) -> p c a b", a=2), ACT.Copy))
            act.wait_ge(o_copied, GC)
            nc.scalar.activation(rms_sq[:], gla_o[:].rearrange("p h t -> p (h t)"), ACT.Square).then_inc(rms_squared, 1)
            act.wait_ge(rms_eps, 1)
            nc.scalar.activation(rms_r[:], rms_r[:], ACT.Sqrt).then_inc(rms_std, 1)
            nc.scalar.activation(pj[:, AB_G:AB_G + 4, :], pj[:, AB_G:AB_G + 4, :], ACT.Silu).then_inc(g_silu, 1)
            act.wait_ge(y_ab, 1)
            for k in range(KD):
                split_rows(pj[:, AB_HV + k, :] if k < 4 else gla_o[:, k - 4, :], k)
            product_and_squares("ab_out", 0)
            normalise_x(0, True)
            act.wait_ge(out_sent, 16 * OUT_AB)
            product("f0_in", gate_up("f0_in"))
            product_and_squares("f0_out", 1)
            normalise_x(1, True)

            def forget_gates():
                act.wait_ge(f_sum, 1)
                link(nc.scalar.activation(halves(frow[0][:]), ps[0:40, 4:6, 0:HT], ACT.Identity,
                                          bias=par[0:40, PARAM_AT["b_f"]:PARAM_AT["b_f"] + 1]))
                link(nc.scalar.activation(frow[1][:], frow[0][:], ACT.Abs))
                link(nc.scalar.activation(frow[1][:], frow[1][:], ACT.Exp, scale=-1.0))
                nc.scalar.activation(frow[2][:], frow[1][:], ACT.Ln, bias=1.0).then_inc(f_log, 1)

            def keys(i, j):
                if j % 2 == 1:
                    if (i == 1) is True and j == 1:
                        act.wait_ge(f_done, 2)
                    act.wait_ge(pages_free, i * 8 + (4 * (j // 2)))
                    act.wait_ge(kt_done, i * 2 + (j // 2 - 2))
                    nc.scalar.activation(score_rows[:], ps[:, 5 + 2 * (j // 2), :], ACT.Copy).then_inc(ks_copied, 1)

            product("cd_in", tile=keys, behind_first=forget_gates)

            act.wait_ge(v_turned, 2)
            for c in range(GC):
                last = nc.scalar.activation(vtok2[:, c, :], ps[:, c, :], ACT.Copy)
            last.then_inc(v_tok, 1)
            act.wait_ge(acc_free[1], PH["cd_in"][2] // 2 + 10 + 1)
            act.wait_ge(acc_free[0], PH["cd_in"][2] // 2 + 10 + 1)
            nc.scalar.activation(pj2[:, CD_GATE:CD_GATE + 4, :], pj2[:, CD_GATE:CD_GATE + 4, :], ACT.Sigmoid).then_inc(d_sig, 1)

            act.wait_ge(s_shifted, 1)
            nc.scalar.activation(s_all[:], s_all[:], ACT.Exp).then_inc(p_all, 1)

            def exps(hp, u):
                n = hp * 8 + u
                tt = u % 4
                act.wait_ge(neg_max, n + 1)
                act.wait_ge(p_turned, n + 1)
                nc.scalar.activation(prob[:, u % 2, 0:P * (tt + 1)], ps[:, u % 2, 0:P * (tt + 1)], ACT.Exp,
                                     bias=tiny[:, u % 2:u % 2 + 1], accum_out=tiny[:, 2 + u % 2:3 + u % 2]).then_inc(exp_done, 1)

            def pt_copy(hp, u):
                n = hp * 8 + u
                tt = u % 4
                act.wait_ge(p_turned, n + 3)
                act.wait_ge(pv_done, n + 1)
                nc.scalar.activation(prob_t[:, u % 2, 0:P * (tt + 1)], ps[:, 2 + u % 2, 0:P * (tt + 1)], ACT.Copy)\
                    .then_inc(pt_copied, 1)

            with act.Fori(0, 4) as hp:
                exps(hp, 0)
                for u in range(8):
                    if u < 7:
                        exps(hp, u + 1)
                    pt_copy(hp, u)
                act.wait_ge(pv_done, hp * 8 + 10)
                nc.scalar.activation(pj2[:, bass.ds(hp, 1), 0:TP].rearrange("p o n -> p (o n)"), ps[:, 4, :], ACT.Copy)\
                    .then_inc(o_evac, 1)
            act.wait_ge(d_u, 1)
            for k in range(4):
                nc.scalar.activation(pj2[:, CD_GATE + k, :], pj2[:, CD_GATE + k, :], ACT.Identity,
                                     bias=par[:, PARAM_AT["cf_b"] + k:PARAM_AT["cf_b"] + k + 1]).then_inc(ln_in, 1)
            normalise_d()
            act.wait_ge(ln_out, 2 * KD + 4)
            act.wait_ge(y_cd, 1)
            for k in range(KD):
                split_rows(pj2[:, k if k < 4 else CD_GATE + k - 4, :], k)
            product_and_squares("cd_out", 3)
            normalise_x(3, True)
            act.wait_ge(out_sent, 16 * OUT_CD)
            product("f1_in", gate_up("f1_in"))
            product_and_squares("f1_out", 4)
            normalise_x(4, False)

        @block.gpsimd
        def _(pool):
            def rest(n, j, b):
                pool.wait_ge(w_rounded, n + 1)
                nc.gpsimd.tensor_tensor(wl[:, j % SPLIT, 0:b * P], raw[:, j, 0:b * P],
                                        wh[:, j % SPLIT, 0:b * P].bitcast(F32), ALU.subtract).then_inc(w_rest, 1)

            def next_rest(name, i, j, last):
                s = PH[name][0]
                b = BLOCKS.get(name, KD)
                if last and j >= 4 - SPLIT:
                    if NEXT[name] is None:
                        return
                    b = BLOCKS.get(NEXT[name], KD)
                rest(s + 4 * i + j + SPLIT, (j + SPLIT) % 4, b)

            def product(name, tile=None):
                n = PH[name][1] // 4
                with pool.Fori(0, n - 1) as i:
                    for j in range(4):
                        next_rest(name, i, j, False)
                        if tile:
                            tile(i, j)
                for j in range(4):
                    next_rest(name, n - 1, j, True)
                    if tile:
                        tile(n - 1, j)

            def hidden(name):
                m0 = 0 if name == "f0_in" else 22

                def tile(i, j):
                    if j % 2 == 1:
                        m = i * 2 + j // 2
                        pool.wait_ge(hid_hi, m0 + m + 1)
                        nc.gpsimd.tensor_tensor(hl[:, bass.ds(m, 1), :].rearrange("p o n -> p (o n)"), hid_t[:],
                                                hh[:, bass.ds(m, 1), :].rearrange("p o n -> p (o n)").bitcast(F32),
                                                ALU.subtract).then_inc(hid_split, 1)
                return tile

            def x_rest(lo):
                for k in range(KD):
                    pool.wait_ge(x_hi, lo + k + 1)
                    nc.gpsimd.tensor_tensor(xl[:, k, :], x[:, k, :], xh[:, k, :].bitcast(F32), ALU.subtract).then_inc(x_split, 1)

            nc.gpsimd.memset(zeros[:], 0.0)
            nc.gpsimd.memset(eps_c[:], EPS).then_inc(setup, 1)
            for j in range(SPLIT):
                rest(j, j, KD)
            product("ab_in")
            nc.gpsimd.memset(attn[:], 0.0).then_inc(attn_zero, 1)
            pool.wait_ge(conv_a_ready, 1)
            pool.dma_start(O["conv_a_p"], pj[:, AB_CG:AB_CG + 4, TP - 2:TP]).then_inc(out_sent, 16)
            pool.dma_start(O["conv_a_s"], conv_a_state[:]).then_inc(out_sent, 16)
            pool.wait_ge(state_c, GC)
            pool.dma_start(O["gla_p"], gla_s[:, GC - 1]).then_inc(out_sent, 16)
            pool.wait_ge(sam_state, 1)
            pool.dma_start(O["gla_s"], gla_s0[:]).then_inc(out_sent, 16)
            product("ab_out")
            x_rest(2 * KD)
            product("f0_in", hidden("f0_in"))
            product("f0_out")
            x_rest(3 * KD)
            product("cd_in")
            pool.wait_ge(acc_free[1], PH["cd_in"][2] // 2 + 10 + 1)
            pool.wait_ge(acc_free[0], PH["cd_in"][2] // 2 + 10 + 1)
            pool.dma_start(O["kt"], pj2[:, CD_K:CD_K + 4, :]).then_inc(out_sent, 16)
            pool.dma_start(O["vt"], pj2[:, CD_V:CD_V + 4, :]).then_inc(out_sent, 16)
            pool.wait_ge(f_done, 1)
            pool.dma_start(O["logf"], frow[2][0:8, :]).then_inc(logf_sent, 16)
            pool.wait_ge(d_u, 1)
            pool.dma_start(O["conv_d_p"], upad[:, :, TP:TP + CF_TAPS - 1]).then_inc(out_sent, 16)
            pool.dma_start(O["conv_d_s"], ext_d[:, :, :, 1:CF_TAPS]).then_inc(out_sent, 16)
            product("cd_out")
            x_rest(5 * KD)
            product("f1_in", hidden("f1_in"))
            product("f1_out")

        @block.tensor
        def _(pe):
            pe.sem_inc(slot_used, SPLIT)
            pe.sem_inc(p_turned, 2)
            pe.sem_inc(pv_done, 2)
            pe.sem_inc(pages_free, 4)

            def three(out, slot, k, block_at, hi, lo, start, stop):
                for w, rows, a, z in ((wh, hi, True, False), (wh, lo, False, False), (wl, hi, False, True)):
                    for h in range(2):
                        mm = nc.tensor.matmul(out[h], w[:, slot, block_at * P:block_at * P + P],
                                              rows[:, k, HT * h:HT * h + HT], start=start and a, stop=stop and z)
                return mm

            def product(name, split=None, idx=None, behind_first=None, behind_tile=None):
                s, slots, t, _ = PH[name]

                def body(i, first_slots=False, behind=None):
                    for j in range(4):
                        n = s + i * 4 + j
                        pe.wait_ge(w_rest, n + 1)
                        if name in BLOCKS:
                            par2, tile, first, lastk = j // 2, t // 2 + i, j % 2 == 0, j % 2 == 1
                            if first:
                                pe.wait_ge(acc_free[par2], tile + 1)
                            pe.wait_ge(hid_split, (0 if name == "f0_out" else KF) + (HALF_KF if first else KF))
                            out = [ps[:, 2 * par2 + h, 0:HT] for h in range(2)]
                            for k in range(HALF_KF):
                                kk = k + (0 if first else HALF_KF)
                                mm = three(out, j % 2, kk, k, hh, hl, first and k == 0, lastk and k == HALF_KF - 1)
                            mm.then_inc(slot_used, 1)
                        else:
                            pe.wait_ge(acc_free[j % 2], t // 2 + i * 2 + j // 2 + 1)
                            out = [ps[:, 2 * (j % 2) + h, 0:HT] for h in range(2)]
                            for k in range(KD):
                                if first_slots and j == 0:
                                    pe.wait_ge(x_split, split + k + 1)
                                mm = three(out, j % 2, k, k, xh, xl, k == 0, k == KD - 1)
                            mm.then_inc(slot_used, 1)
                            if behind:
                                behind(j)

                start = 0
                if split is not None:
                    body(0, True)
                    start = 1
                if behind_tile:
                    behind_first()
                    body(1, behind=lambda j: behind_tile(1, j, True))
                    with pe.Fori(2, slots // 4) as i:
                        body(i, behind=lambda j: behind_tile(i, j, False))
                    return
                if idx is not None:
                    half = slots // 8
                    if start < half:
                        with pe.Fori(start, half) as i:
                            body(i)
                    pe.wait_ge(ln_first, LN_OF[idx] + 1)
                    for h in range(2):
                        mm = nc.tensor.matmul(ps[:, 4 + h, 0:HT], ones, rstd[:, HT * h:HT * h + HT], start=True, stop=True)
                    mm.then_inc(ln_guess, 1)
                    start = half
                with pe.Fori(start, slots // 4) as i:
                    body(i)

            def sums(idx):
                j, base = LN_OF[idx], LN_BASE[idx]
                pe.wait_ge(ln_part, j + 1)
                nc.tensor.matmul(ps[:, 6, 0:HT], ones, rstd[:, 0:HT], start=True, stop=False)
                nc.tensor.matmul(ps[:, 7, 0:HT], ones, rstd[:, HT:T], start=True, stop=False)
                pe.wait_ge(ln_centered, base + KD)
                nc.tensor.matmul(ps[:, 6, 0:HT], ones, x[:, KD - 1, 0:HT], start=False, stop=True)
                nc.tensor.matmul(ps[:, 7, 0:HT], ones, x[:, KD - 1, HT:T], start=False, stop=True).then_inc(ln_sum, 1)
                pe.wait_ge(ln_added, 6 * j + 6)
                nc.tensor.matmul(ps[:, 4, 0:HT], ones, gate_t[:, 0:HT], start=True, stop=False)
                nc.tensor.matmul(ps[:, 5, 0:HT], ones, gate_t[:, HT:T], start=True, stop=False)
                pe.wait_ge(ln_sq, base + KD)
                nc.tensor.matmul(ps[:, 4, 0:HT], ones, hid_t[:, 0:HT], start=False, stop=True)
                nc.tensor.matmul(ps[:, 5, 0:HT], ones, hid_t[:, HT:T], start=False, stop=True).then_inc(ln_var, 1)

            def sums_d():
                base = LN_BASE[D_LN]
                pe.wait_ge(ln_in, 4)
                for h in range(2):
                    for k in range(4):
                        mm = nc.tensor.matmul(ps[:, 4 + h, 0:HT], ones, pj2[:, CD_GATE + k, HT * h:HT * h + HT],
                                              start=k == 0, stop=k == 3)
                mm.then_inc(ln_sum, 1)
                for k in range(4):
                    pe.wait_ge(ln_sq, base + k + 1)
                    for h in range(2):
                        mm = nc.tensor.matmul(ps[:, 6 + h, 0:HT], ones, squares_d[:, k, HT * h:HT * h + HT],
                                              start=k == 0, stop=k == 3)
                mm.then_inc(ln_var, 1)

            pe.wait_ge(par_in, 32)
            pe.wait_ge(x_in, 32)
            for h in range(2):
                for k in range(KD):
                    a = PARAM_AT["w_r"] + 16 * k
                    mm = nc.tensor.matmul(ps[0:16, 4 + h, 0:HT], par[:, a:a + 16], x[:, k, HT * h:HT * h + HT],
                                          start=k == 0, stop=k == KD - 1)
            mm.then_inc(r_sum, 1)
            product("ab_in", split=0)
            pe.wait_ge(r_copied, 1)
            for t in range(2):
                for h in range(2):
                    a = PARAM_AT["w_gate2"] + P * t
                    mm = nc.tensor.matmul(ps[:, 4 + 2 * t + h, 0:HT], par[0:16, a:a + P], r_t[:, HT * h:HT * h + HT],
                                          start=True, stop=True)
            mm.then_inc(z_sum, 1)
            pe.wait_ge(acc_free[0], 12 + 1)
            pe.wait_ge(acc_free[1], 12 + 1)
            for c in range(GC):
                for h in range(4):
                    mm = nc.tensor.transpose(ps[:, c, P * h:P * h + P], pj[:, AB_V + h, P * c:P * c + P], ident)
            mm.then_inc(v_turned, 1)
            pe.wait_ge(z_log, 1)
            for h in range(4):
                mm = nc.tensor.transpose(ps[0:NB, 7, P * h:P * h + P], pj[:, AB_V + h, TP:T], ident)
            mm.then_inc(vsam_turned, 1)
            pe.wait_ge(vsam_copied, 1)
            for l in range(LEVELS):
                half = P >> (l + 1)
                pe.wait_ge(lv_qk, l + 1)
                if l >= 2:
                    pe.wait_ge(lv_kept, l - 1)
                for u in range(GC * 4):
                    h2, c, hp = u // 8, u // 2 % 4, u % 2
                    r0 = 64 * h2
                    rows = qk[r0:r0 + 64, l % 2, hp, P * c:P * c + P]
                    bank = 4 + 2 * (l % 2) + h2
                    out = ps[:, bank, 64 * (u % 8):64 * (u % 8) + 64].rearrange("p (n b) -> p n b", b=half)
                    mm = nc.tensor.matmul(out, rows, rows.rearrange("p (n b) -> p n b", b=2 * half)[:, :, half:],
                                          start=True, stop=True)
                mm.then_inc(lv_scores, 1)
            for part in range(2):
                pe.wait_ge(lv_kept, LEVELS - 1 + part)
                for u in range(8):
                    c, hp, r0 = u // 2, u % 2, 64 * part
                    b0 = (4 + 2 * ((LEVELS + part) % 2)) + (u % 8) // 4
                    mm = nc.tensor.matmul(ps[:, b0, P * (u % 4):P * (u % 4) + P],
                                          pj[r0:r0 + 64, AB_K + hp, P * c:P * c + P],
                                          pj[r0:r0 + 64, AB_Q + hp, P * c:P * c + P], start=True, stop=True)
                mm.then_inc(lv_scores, 1)
            pe.wait_ge(kw_ready, 1)
            pe.wait_ge(lv_kept, LEVELS + 2)
            for c in range(GC):
                for hp in range(2):
                    mm = nc.tensor.transpose(ps[:, 4 + c // 2, 256 * (c % 2) + P * hp:256 * (c % 2) + P * hp + P],
                                             qk[:, 0, hp, P * c:P * c + P], ident)
            mm.then_inc(kw_turned, 1)
            pe.wait_ge(kw_tok, 1)
            pe.wait_ge(v_tok, 1)
            for c in range(GC):
                for hp in range(2):
                    mm = nc.tensor.matmul(ps[:, 4 + c, 256 * hp:256 * hp + 256], kwtok[:, c, P * hp:P * hp + P],
                                          vtok[:, c, 256 * hp:256 * hp + 256], start=True, stop=True)
                mm.then_inc(kv_sum, 1)
            for c in range(GC):
                if c > 0:
                    pe.wait_ge(state_c, c)
                if c >= 2:
                    pe.wait_ge(o_copied, c - 1)
                for h in range(4):
                    r0, hp = 64 * (h % 2), h // 2
                    out = ps[:, 2 * (c % 2) + h % 2, P * hp:P * hp + P]
                    mm = nc.tensor.matmul(out, vtok[:, c, P * h:P * h + P], attn[:, 8 * (h % 2) + 2 * c + hp, :], start=True, stop=c == 0)
                    if c > 0:
                        mm = nc.tensor.matmul(out, gla_s[r0:r0 + 64, c - 1, hp, :],
                                              qk[r0:r0 + 64, 1, hp, P * c:P * c + P], start=False, stop=True)
                mm.then_inc(o_sum, 1)
            pe.wait_ge(state_c, GC)
            for b in range(NB):
                if b == 4:
                    pe.wait_ge(vb_used, 1)
                mm = nc.tensor.matmul(ps[:, 4 + b % 4, :], ident[0:NB, b:b + 1].to_broadcast([NB, P]), vsam[:],
                                      start=True, stop=True)
                if b % 4 == 3:
                    mm.then_inc(vb_sum, 1)
            pe.wait_ge(sam_state, 1)
            pe.wait_ge(o_copied, GC - 1)
            for h in range(4):
                for b in range(NB):
                    r0, hp = 64 * (h % 2), h // 2
                    mm = nc.tensor.matmul(ps[:, h % 2, TS * hp + b:TS * hp + b + 1], gla_s0[r0:r0 + 64, b, hp, :],
                                          pj[r0:r0 + 64, AB_Q + hp, TP + b:TP + b + 1], start=True, stop=True)
            mm.then_inc(sam_o, 1)
            pe.wait_ge(rms_squared, 1)
            for i in range(5):
                mm = nc.tensor.matmul(ps[:, i, 0:416], ones, rms_sq[:, 416 * i:416 * i + 416], start=True, stop=True)
            mm.then_inc(rms_sum, 1)

            product("ab_out", split=KD, idx=0)
            sums(0)
            product("f0_in", split=2 * KD)
            product("f0_out", idx=1)
            sums(1)

            def forget_logits():
                for h in range(2):
                    for k in range(KD):
                        a = PARAM_AT["w_f"] + 40 * k
                        mm = nc.tensor.matmul(ps[0:40, 4 + h, 0:HT], par[:, a:a + 40], x[:, k, HT * h:HT * h + HT],
                                              start=k == 0, stop=k == KD - 1)
                mm.then_inc(f_sum, 1)

            def turn_scores(b):
                pe.wait_ge(ks_copied, b + 3)
                pe.wait_ge(s_ready_all, b)
                for s in range(4):
                    mm = nc.tensor.transpose(ps[:, 6, P * s:P * s + P], score_rows[:, P * s:P * s + P], ident)
                mm.then_inc(kt_done, 1)

            def key_slots(i, j, first):
                two = j // 2
                if j % 2 == 0:
                    if first and two == 0:
                        pe.wait_ge(f_log, 1)
                    else:
                        if first:
                            pe.wait_ge(decay_ready, 1)
                        turn_scores(i * 2 + (two - 3))
                    pe.wait_ge(q_staged, i * 2 + (two - 1))
                    pe.wait_ge(ks_copied, i * 2 + (two - 1))
                for h in range(2):
                    s = 2 * (j % 2) + h
                    pe.wait_ge(page_in[s], i * 128 + (64 * two - 64))
                    for pair in range(4):
                        for g in range(4):
                            mm = nc.tensor.matmul(ps[32 * g:32 * g + 32, 5 + 2 * two, P * s:P * s + P],
                                                  q_wide[:, two, 32 * pair:32 * pair + 32], pages[:, s, g, P * pair:P * pair + P],
                                                  start=pair == 0, stop=pair == 3)
                    mm.then_inc(pages_free, 1)
                if first and j == 1:
                    pe.wait_ge(later_in, 1)
                    for h in range(2):
                        out = ps[:, 6 + h, :]
                        nc.tensor.matmul(out, later, lf_pages[:, 8 * h:8 * h + 8].rearrange("p g b h -> p (g b h)"),
                                         start=True, stop=False)
                        nc.tensor.matmul(out, ones, lf_later[:, 8 * h:8 * h + 8, :].rearrange("p g n -> p (g n)"),
                                         start=False, stop=False)
                        mm = nc.tensor.matmul(out.rearrange("p (g n) -> p g n", g=8), ones[0:8, :],
                                              small_b[0:8, None, :].to_broadcast([8, 8, 64]), start=False, stop=True)
                    mm.then_inc(later_sum, 1)

            product("cd_in", split=3 * KD, behind_first=forget_logits, behind_tile=key_slots)

            turn_scores(NB - 1)
            pe.wait_ge(acc_free[0], PH["cd_in"][2] // 2 + 10 + 1)
            pe.wait_ge(acc_free[1], PH["cd_in"][2] // 2 + 10 + 1)
            for c in range(GC):
                for h in range(4):
                    mm = nc.tensor.transpose(ps[:, c, P * h:P * h + P], pj2[:, CD_V + h, P * c:P * c + P], ident)
            mm.then_inc(v_turned, 1)
            pe.wait_ge(self_in, 1)
            nc.tensor.matmul(ps[0:1, 5, 0:64], ones[:, 0:1], small_a[:], start=True, stop=True).then_inc(self_sum, 1)

            pe.wait_ge(m_turned, 1)
            nc.tensor.transpose(ps[0:64, 5, 0:P], small_a[:], ident).then_inc(m_turned, 1)
            pe.wait_ge(m_diag, 1)
            nc.tensor.matmul(ps[:, 6, 0:64], ones[0:64, :], small_b[0:64, :], start=True, stop=True).then_inc(m_cast, 1)
            pe.wait_ge(l_part, 1)
            nc.tensor.matmul(ps[:, 7, 0:64], ones, small_c[:], start=True, stop=True).then_inc(l_sum, 1)
            nc.tensor.matmul(ps[:, 6, 64:128], ones[0:1, :], s_all[0:1, :, :, PAGES].rearrange("p b h -> p (b h)"),
                             start=True, stop=True).then_inc(self_cast, 1)
            def scores(hp, u):
                n = hp * 8 + u
                h2, tt = u // 4, u % 4
                r0, w = 64 * h2, P * (tt + 1)
                pe.wait_ge(exp_done, n + 1)
                out = ps[:, u % 2, 0:w]
                nc.tensor.matmul(out, q_st[r0:r0 + 64, P * tt:P * tt + P], k_st[r0:r0 + 64, 0:w], start=True, stop=False)
                nc.tensor.matmul(out, grow[:, P * tt:P * tt + P], hsel[:, h2, 0:w], start=False, stop=False)
                nc.tensor.matmul(ps[:, u % 2, P * tt:w], ident_b[:], causal_b[:], start=False, stop=True).then_inc(s_ready, 1)

            def value_slot(hp, u):
                two, s = u // 4, u % 4
                if s == 0:
                    pe.wait_ge(p_staged, hp * 2 + (two + 1))
                pe.wait_ge(page_in[s], hp * 128 + (64 * two + 64 * 9))
                for g in range(4):
                    mm = nc.tensor.matmul(ps[32 * g:32 * g + 32, 5 + 2 * two, :], p_blocks[:, two, 4 * s + g, :],
                                          pages[:, s, g, :], start=s == 0, stop=s == 3)
                mm.then_inc(pages_free, 1)

            pe.wait_ge(v_tok, 2)
            pe.wait_ge(setup, 2)
            with pe.Fori(0, 4) as hp:
                pe.wait_ge(fox_staged, hp + 1)
                scores(hp, 0)
                for u in range(8):
                    n = hp * 8 + u
                    h2, tt = u // 4, u % 4
                    r0 = 64 * h2
                    if u < 7:
                        scores(hp, u + 1)
                    value_slot(hp, u)
                    pe.wait_ge(p_ready, n + 1)
                    pe.wait_ge(pt_copied, n + 1)
                    for c in range(tt + 1):
                        mm = nc.tensor.transpose(ps[:, 2 + u % 2, P * c:P * c + P], prob[:, u % 2, P * c:P * c + P], ident)
                    mm.then_inc(p_turned, 1)
                    pe.wait_ge(pt_copied, n + 3)
                    if u == 0:
                        pe.wait_ge(o_evac, hp)
                    for c in range(tt + 1):
                        mm = nc.tensor.matmul(ps[r0:r0 + 64, 4, P * tt:P * tt + P], v_st[:, c, r0:r0 + 64],
                                              prob_t[:, u % 2, P * c:P * c + P], start=c == 0, stop=c == tt)
                    mm.then_inc(pv_done, 1)
                    if u % 4 == 3:
                        pe.wait_ge(v_masked, hp * 2 + (u // 4 + 1))
                        for pair in range(4):
                            mm = nc.tensor.matmul(ps[:, 6, bass.ds(hp * 8 + (4 * (u // 4) + pair), 1)], v_rows[:, P * pair:P * pair + P],
                                                  ones[:, 0:1], start=True, stop=True)
                        mm.then_inc(pv_all, 1)

            sums_d()

            product("cd_out", split=4 * KD, idx=3)
            sums(3)
            product("f1_in", split=5 * KD)
            product("f1_out", idx=4)
            sums(4)

        @block.vector
        def _(dve):
            own = [0]
            V = nc.vector

            def link(ins):
                own[0] += 1
                ins.then_inc(dve_own, 1)
                dve.wait_ge(dve_own, own[0])

            dve.sem_inc(acc_free[0], 1)
            dve.sem_inc(acc_free[1], 1)

            def acc(j):
                return ps[:, 2 * (j % 2):2 * (j % 2) + 2, 0:HT]

            def copy_tile(name, dst, m, j):
                dve.wait_ge(slot_used, m + (SPLIT + PH[name][0] + 1))
                V.tensor_copy(dst[:, bass.ds(m, 1), :].rearrange("p o (h n) -> p (o h) n", h=2), acc(j))\
                    .then_inc(acc_free[j % 2], 1)

            def copy_tiles(name, dst, first, behind):
                with dve.Fori(first // 2, behind // 2) as i:
                    for j in range(2):
                        copy_tile(name, dst, i * 2 + j, j)

            def residual_and_center(name, idx):
                s, slots, t, tiles = PH[name]
                j, base = LN_OF[idx], LN_BASE[idx]

                def add_squares(i):
                    dve.wait_ge(ln_sq, base + i + 1)
                    if i > 1:
                        dve.wait_ge(ln_added, 6 * j + i - 1)
                    V.tensor_tensor(gate_t[:], gate_t[:], hid_t[:], ALU.add).then_inc(ln_added, 1)

                done = 0
                for m in range(tiles):
                    dve.wait_ge(slot_used, SPLIT + s + (m + 1) * slots // tiles)
                    V.scalar_tensor_tensor(out=halves(x[:, m, :]), in0=halves(x[:, m, :]), scalar=ALPHA, in1=acc(m),
                                           op0=ALU.mult, op1=ALU.add).then_inc(acc_free[m % 2], 1)
                    if m > 0:
                        dve.wait_ge(acc_free[m % 2], (t + m) // 2 + 2)
                    if m == 1:
                        dve.wait_ge(acc_free[0], t // 2 + 2)
                        link(V.tensor_tensor(rstd[:], x[:, 0, :], x[:, 1, :], ALU.add))
                    elif m == 2:
                        V.tensor_tensor(rstd[:], rstd[:], x[:, 2, :], ALU.add).then_inc(ln_first, 1)
                    elif m == 4:
                        dve.wait_ge(acc_free[1], (t + 3) // 2 + 2)
                        dve.wait_ge(ln_guess, j + 1)
                    if m >= 4:
                        first = done
                        while done < (3, 5, 7, 8)[m - 4]:
                            k = CENTERED[done]
                            V.scalar_tensor_tensor(out=halves(x[:, k, :]), in0=ps[:, 4:6, 0:HT], scalar=-1.0 / (P * GUESS),
                                                   in1=halves(x[:, k, :]), op0=ALU.mult, op1=ALU.add).then_inc(ln_centered, 1)
                            done += 1
                        if m < 7:
                            dve.wait_ge(ln_centered, base + done)
                            if m == 4:
                                link(V.tensor_tensor(rstd[:], x[:, CENTERED[0], :], x[:, CENTERED[1], :], ALU.add))
                                first = 2
                            for i in range(first, done):
                                last = V.tensor_tensor(rstd[:], rstd[:], x[:, CENTERED[i], :], ALU.add)
                                if i == 6:
                                    last.then_inc(ln_part, 1)
                                else:
                                    link(last)
                            for i in range(max(first, 1) if m > 4 else 1, done):
                                add_squares(i)

            def normalise_x(idx):
                base = LN_BASE[idx]
                dve.wait_ge(ln_sum, idx + 1)
                link(V.tensor_scalar(halves(rstd[:]), ps[:, 6:8, 0:HT], 1.0 / D, None, ALU.mult))
                link(V.tensor_tensor(rstd[:], rstd[:], rstd[:], ALU.mult))

                def center(k):
                    return V.scalar_tensor_tensor(out=halves(x[:, k, :]), in0=ps[:, 6:8, 0:HT], scalar=-1.0 / D,
                                                  in1=halves(x[:, k, :]), op0=ALU.mult, op1=ALU.add)
                center(0)
                dve.wait_ge(ln_var, idx + 1)
                V.scalar_tensor_tensor(out=halves(rstd[:]), in0=ps[:, 4:6, 0:HT], scalar=1.0 / D, in1=halves(rstd[:]),
                                       op0=ALU.mult, op1=ALU.subtract).then_inc(ln_veps, 1)
                for k in range(1, KD):
                    last = center(k)
                dve.wait_ge(ln_std, idx + 1)
                link(last)
                link(V.reciprocal(rstd[:], rstd[:]))
                for k in range(KD):
                    V.tensor_tensor(x[:, k, :], x[:, k, :], rstd[:], ALU.mult).then_inc(ln_scaled, 1)

            def rest_rows(src, lo):
                for k in range(KD):
                    dve.wait_ge(x_hi, lo + k + 1)
                    V.tensor_tensor(xl[:, k, :], src(k), xh[:, k, :].bitcast(F32), ALU.subtract).then_inc(x_split, 1)

            def normalise_d():
                idx, n = D_LN, 4

                def src(k):
                    return pj2[:, CD_GATE + k, :]

                dve.wait_ge(ln_sum, idx + 1)
                for k in range(n):
                    V.scalar_tensor_tensor(out=halves(src(k)), in0=ps[:, 4:6, 0:HT], scalar=-1.0 / (P * n),
                                           in1=halves(src(k)), op0=ALU.mult, op1=ALU.add).then_inc(ln_centered, 1)
                dve.wait_ge(ln_var, idx + 1)
                V.tensor_scalar(halves(rstd[:]), ps[:, 6:8, 0:HT], 1.0 / (P * n), None, ALU.mult).then_inc(ln_veps, 1)
                dve.wait_ge(ln_std, idx + 1)
                link(V.reciprocal(rstd[:], rstd[:]))
                dve.wait_ge(ln_centered, LN_BASE[idx] + n)
                for k in range(n):
                    V.tensor_tensor(src(k), src(k), rstd[:], ALU.mult).then_inc(ln_scaled, 1)

            def x_rows(k):
                return x[:, k, :]

            def hidden(name):
                s, _, _, _ = PH[name]
                m0 = 0 if name == "f0_in" else 22
                with dve.Fori(0, 22) as m:
                    dve.wait_ge(gate_ready, m0 + m + 1)
                    dve.wait_ge(slot_used, m * 2 + (SPLIT + s + 2))
                    dve.wait_ge(hid_split, m0 + m)
                    V.tensor_tensor(halves(hid_t[:]), acc(1), halves(gate_t[:]), ALU.mult).then_inc(hid_ready, 1)
                    dve.wait_ge(hid_ready, m0 + m + 1)
                    dve.sem_inc(acc_free[1], 1)

            V.memset(q_wide[:], 0.0)
            link(V.memset(qblk[:], 0.0))
            link(V.memset(small_b[:], 0.0))
            rest_rows(x_rows, 0)
            dve.wait_ge(r_sum, 1)
            V.tensor_copy(halves(r_t[:]), ps[0:16, 4:6, 0:HT]).then_inc(r_copied, 1)
            copy_tiles("ab_in", pj, 0, TILES_AB)
            dve.wait_ge(acc_free[0], 13)
            dve.wait_ge(acc_free[1], 13)
            dve.wait_ge(par_in, 32)
            dve.wait_ge(state_in, 64)

            link(V.tensor_scalar(pj[:, AB_Q:AB_Q + 2, :], pj[:, AB_Q:AB_Q + 2, :], 64 ** -0.5, None, ALU.mult))
            dve.wait_ge(z_log, 1)
            link(V.scalar_tensor_tensor(out=loga[:], in0=zpre[:], scalar=0.0, in1=zexp[:], op0=ALU.min, op1=ALU.subtract))
            V.tensor_scalar(loga[:], loga[:], 1.0 / 16.0, None, ALU.mult).then_inc(log_a, 1)
            dve.wait_ge(log_a, 1)
            for t in range(2):
                last = V.tensor_tensor_scan(gcum[:, t, :], scan_on, loga[:, t, 0:TP], 0.0, ALU.mult, ALU.add)
            link(last)

            def level_diff(l):
                half = P >> (l + 1)
                g = gcum[:].rearrange("p t (n b) -> p (t n) b", b=2 * half)
                d = gdiff[:, l % 2].rearrange("p t (n b) -> p (t n) b", b=2 * half)
                mid = g[:, :, half - 1:half].to_broadcast([P, 2 * TP // (2 * half), half])
                V.tensor_tensor(d[:, :, half:], g[:, :, half:], mid, ALU.subtract)
                V.tensor_tensor(d[:, :, 0:half], mid, g[:, :, 0:half], ALU.subtract).then_inc(lv_diff, 1)

            def level_qk(l):
                half = P >> (l + 1)

                def by_block(ap):
                    return ap.rearrange("p t (n b) -> p t n b", b=2 * half)
                d, o = by_block(gdiff[:, l % 2]), by_block(qk[:, l % 2])
                q, k = by_block(pj[:, AB_Q:AB_Q + 2, 0:TP]), by_block(pj[:, AB_K:AB_K + 2, 0:TP])
                dve.wait_ge(lv_exp, l + 1)
                if l >= 2:
                    dve.wait_ge(lv_scores, l - 1)
                V.tensor_tensor(o[:, :, :, half:], q[:, :, :, half:], d[:, :, :, half:], ALU.mult)
                V.tensor_tensor(o[:, :, :, 0:half], k[:, :, :, 0:half], d[:, :, :, 0:half], ALU.mult).then_inc(lv_qk, 1)

            def level_keep(l):
                half = P >> (l + 1)
                dve.wait_ge(lv_scores, l + 1)
                if l >= 1:
                    dve.wait_ge(lv_kept, l)
                out = attn[:].rearrange("p u (n b) -> p u n b", b=2 * half)[:, :, :, half:]
                mask = imask[:, None, 64 * l:64 * l + 64].to_broadcast([P, 16, 64]).rearrange("p u (n b) -> p u n b", b=half)
                bank = 4 + 2 * (l % 2)
                V.copy_predicated(out, mask, ps[:, bank:bank + 2, :].rearrange("p k (u n b) -> p (k u) n b", u=8, b=half))\
                    .then_inc(lv_kept, 1)

            level_diff(0)
            dve.wait_ge(attn_zero, 1)
            for l in range(LEVELS):
                if l + 1 < LEVELS:
                    if l >= 1:
                        dve.wait_ge(lv_qk, l)
                    level_diff(l + 1)
                level_qk(l)
                if l >= 1:
                    level_keep(l - 1)
            dve.wait_ge(lv_qk, LEVELS)
            g4 = gcum[:].rearrange("p t (n b) -> p (t n) b", b=P)
            V.tensor_tensor(gdiff[:, 0].rearrange("p t (n b) -> p (t n) b", b=P),
                            g4[:, :, P - 1:P].to_broadcast([P, 8, P]), g4, ALU.subtract).then_inc(kw_diff, 1)
            level_keep(LEVELS - 1)
            for part in range(2):
                bank = 4 + 2 * ((LEVELS + part) % 2)
                dve.wait_ge(lv_scores, LEVELS + part + 1)
                dve.wait_ge(lv_kept, LEVELS + part)
                V.copy_predicated(attn[:, 8 * part:8 * part + 8, :],
                                  imask[:, None, 64 * LEVELS:64 * LEVELS + P].to_broadcast([P, 8, P]),
                                  ps[:, bank:bank + 2, :].rearrange("p k (u t) -> p (k u) t", u=4)).then_inc(lv_kept, 1)
            dve.wait_ge(kw_exp, 1)
            V.tensor_tensor(qk[:, 0], pj[:, AB_K:AB_K + 2, 0:TP], gdiff[:, 0], ALU.mult)
            V.tensor_tensor(qk[:, 1], pj[:, AB_Q:AB_Q + 2, 0:TP], gdiff[:, 1], ALU.mult).then_inc(kw_ready, 1)
            for c in range(GC):
                dve.wait_ge(kv_sum, c + 1)
                if c > 0:
                    dve.wait_ge(state_c, c)
                for hp in range(2):
                    for h2 in range(2):
                        r = slice(64 * h2, 64 * h2 + 64)
                        src = ps[r, 4 + c, 256 * hp + P * h2:256 * hp + P * h2 + P]
                        if c == 0:
                            last = V.tensor_copy(gla_s[r, 0, hp, :], src)
                        else:
                            last = V.scalar_tensor_tensor(out=gla_s[r, c, hp, :], in0=gla_s[r, c - 1, hp, :],
                                                          scalar=gdiff[r, 1, hp, P * c + P - 1:P * c + P], in1=src,
                                                          op0=ALU.mult, op1=ALU.add)
                last.then_inc(state_c, 1)
            dve.wait_ge(sam_decay, 1)
            for b in range(NB):
                dve.wait_ge(vb_sum, b // 4 + 1)
                for h2 in range(2):
                    r = slice(64 * h2, 64 * h2 + 64)
                    last = V.tensor_tensor(gla_kv[r, b], ps[r, 4 + b % 4, :].rearrange("p (a c v) -> p a c v", a=2, c=2)[:, :, h2, :],
                                           pj[r, AB_K:AB_K + 2, TP + b:TP + b + 1].to_broadcast([64, 2, P]), ALU.mult)
                if b == 3:
                    last.then_inc(vb_used, 1)
            link(last)
            link(V.tensor_tensor(gla_s0[:], gla_s0[:],
                                 tiny[:].rearrange("p (a b) -> p b a", a=2)[:, :, :, None].to_broadcast([P, NB, 2, P]), ALU.mult))
            V.tensor_tensor(gla_s0[:], gla_s0[:], gla_kv[:], ALU.add).then_inc(sam_state, 1)

            U, Y = AB_CG, AB_HV
            link(V.tensor_tensor(pj[:, U:U + 4, :], pj[:, U:U + 4, :], pj[:, Y:Y + 4, :], ALU.mult))
            wa = par_of("conv_a", 12).rearrange("p (t j) -> p t j", j=3)
            for t in range(4):
                last = V.tensor_scalar(pj[:, Y + t, :], pj[:, U + t, :], wa[:, t, 2:3], None, ALU.mult)
            link(last)
            for s in (1, 2):
                for t in range(4):
                    V.scalar_tensor_tensor(out=pj[:, Y + t, s:TP], in0=pj[:, U + t, 0:TP - s], scalar=wa[:, t, 2 - s:3 - s],
                                           in1=pj[:, Y + t, s:TP], op0=ALU.mult, op1=ALU.add)
                    last = V.scalar_tensor_tensor(out=pj[:, Y + t, TP:T], in0=conv_a_state[:, t, :, 2 - s], scalar=wa[:, t, 2 - s:3 - s],
                                                  in1=pj[:, Y + t, TP:T], op0=ALU.mult, op1=ALU.add)
                link(last)
            link(V.tensor_copy(conv_a_state[:, :, :, 0], conv_a_state[:, :, :, 1]))
            V.tensor_copy(conv_a_state[:, :, :, 1], pj[:, U:U + 4, TP:T]).then_inc(conv_a_ready, 1)
            V.tensor_tensor(pj[:, Y:Y + 4, :], pj[:, Y:Y + 4, :], pj[:, AB_BG:AB_BG + 4, :], ALU.mult)
            dve.wait_ge(rms_sum, 1)
            V.tensor_scalar(rms_r[:].rearrange("p (i n) -> p i n", i=5), ps[:, 0:5, 0:416], 1.0 / P, EPS, ALU.mult, ALU.add)\
                .then_inc(rms_eps, 1)
            dve.wait_ge(rms_std, 1)
            link(V.reciprocal(rms_r[:], rms_r[:]))
            flat = gla_o[:].rearrange("p h t -> p (h t)")
            link(V.scalar_tensor_tensor(out=flat, in0=flat, scalar=par_of("norm_g", 1), in1=rms_r[:], op0=ALU.mult, op1=ALU.mult))
            dve.wait_ge(g_silu, 1)
            V.tensor_tensor(gla_o[:], gla_o[:], pj[:, AB_G:AB_G + 4, :], ALU.mult).then_inc(y_ab, 1)
            rest_rows(lambda k: pj[:, AB_HV + k, :] if k < 4 else gla_o[:, k - 4, :], KD)
            residual_and_center("ab_out", 0)
            normalise_x(0)
            hidden("f0_in")
            residual_and_center("f0_out", 1)
            normalise_x(1)
            dve.wait_ge(lf_in, 16 * PAGES * NB)
            lfp = lf_pages[:].rearrange("p g b h -> p g (b h)")
            V.memset(lf_later[:, PAGES - 1, :], 0.0)
            link(V.tensor_copy(lf_later[:, PAGES - 2, :], lfp[:, PAGES - 1, :]))
            for g in range(PAGES - 3, -1, -1):
                link(V.tensor_tensor(lf_later[:, g, :], lf_later[:, g + 1, :], lfp[:, g + 1, :], ALU.add))
            copy_tiles("cd_in", pj2, 0, 4)
            for j in range(2):
                dve.wait_ge(acc_free[j], PH["cd_in"][2] // 2 + 2 + 1)
            for h2 in range(2):
                r = slice(64 * h2, 64 * h2 + 64)
                last = V.tensor_scalar(qblk[r, :, :, h2], pj2[r, CD_Q:CD_Q + 4, TP:T], 64 ** -0.5, None, ALU.mult)
            link(last)

            def stage_query(b, two):
                dve.wait_ge(pages_free, b * 4)
                V.tensor_copy(q_wide[:, two, :].rearrange("p (a c) -> p a c", c=34)[:, :, 0:2],
                              qblk[:, :, bass.ds(b, 1), :].rearrange("p a o c -> p a (o c)")).then_inc(q_staged, 1)

            for two in range(2):
                stage_query(two, two)
            z, e, lf, t4, t5 = (frow[i][:] for i in range(5))
            dve.wait_ge(f_log, 1)
            link(V.tensor_scalar(t4, e, 1.0, None, ALU.add))
            link(V.scalar_tensor_tensor(out=t5, in0=t4, scalar=-1.0, in1=e, op0=ALU.add, op1=ALU.subtract))
            link(V.reciprocal(t4, t4))
            link(V.tensor_tensor(t5, t5, t4, ALU.mult))
            link(V.tensor_tensor(t5, t5, lf, ALU.subtract))
            link(V.scalar_tensor_tensor(out=lf, in0=z, scalar=0.0, in1=t5, op0=ALU.min, op1=ALU.add))
            dve.sem_inc(f_done, 1)
            link(V.tensor_tensor(small_b[0:8, :].rearrange("p (b h) -> p b h", h=8),
                                 lf[0:8, TP:T][:, :, None].to_broadcast([8, NB, 8]),
                                 ident[0:8, None, 0:8].to_broadcast([8, NB, 8]), ALU.mult))
            dve.sem_inc(later_in, 1)
            link(V.memset(t4[:, 0:TP], 1.0))
            V.tensor_tensor_scan(t5[:, 0:TP], t4[:, 0:TP], lf[:, 0:TP], 0.0, ALU.mult, ALU.add).then_inc(f_done, 1)

            def add_decay(b):
                dve.wait_ge(kt_done, b + 1)
                one = bass.ds(b, 1)
                V.tensor_tensor(s_all[:, one, :, 0:PAGES].rearrange("p o h (s g) -> p (o h) s g", s=4),
                                ps[:, 6, :].rearrange("p (s g c) -> p c s g", s=4, g=4)[:, 0:8],
                                decay[:, one].rearrange("p o h (s g) -> p (o h) s g", s=4), ALU.add).then_inc(s_ready_all, 1)

            def tiles_and_keys(i, first=False, last=False):
                for j in range(4):
                    copy_tile("cd_in", pj2, i * 4 + j, j)
                    if j == 1 and first:
                        dve.wait_ge(later_sum, 1)
                        V.tensor_copy(decay[:].rearrange("p b h g -> p g (b h)"),
                                      ps[:, 6:8, :].rearrange("p k (g n) -> p (k g) n", g=8)).then_inc(decay_ready, 1)
                        dve.wait_ge(decay_ready, 1)
                    if j % 2 == 0 and not (first and j == 0):
                        add_decay(i * 2 + (j // 2 - 3))
                    if (j == 1 and not first) or (j == 3 and not last):
                        stage_query(i * 2 + (-1 if j == 1 else 0), int(j == 1))

            tiles_and_keys(1, first=True)
            with dve.Fori(2, 4) as i:
                tiles_and_keys(i)
            tiles_and_keys(4, last=True)
            add_decay(NB - 1)
            a0 = PH["cd_in"][2] // 2 + 10 + 1
            dve.wait_ge(acc_free[0], a0)
            dve.wait_ge(acc_free[1], a0)
            V.tensor_tensor(small_a[:].rearrange("p (a b c) -> p a b c", a=4, b=NB), qblk[:],
                            pj2[:, CD_K:CD_K + 4, TP:T][:, :, :, None].to_broadcast([P, 4, NB, 2]), ALU.mult).then_inc(self_in, 1)
            link(V.memset(s_all[:, :, :, PAGES], NEG))
            V.memset(hrow[:], 0.0)
            V.memset(grow[:], 0.0)
            link(V.memset(hsel[:], 0.0))
            V.memset(hrow[0:8, :], 1.0)
            V.memset(grow[32:40, :], 1.0)
            V.tensor_copy(grow[0:8, :], t5[0:8, 0:TP])
            V.tensor_scalar(hrow[32:40, :], t5[32:40, 0:TP], -1.0, None, ALU.mult).then_inc(rows_used, 1)
            dve.wait_ge(self_sum, 1)
            V.tensor_copy(s_all[0:1, :, :, PAGES].rearrange("p b (a c) -> p b a c", a=4),
                          ps[0:1, 5, 0:64].rearrange("p (a b c) -> p b a c", a=4, b=NB)).then_inc(s_ready_all, 1)
            dve.wait_ge(s_ready_all, NB + 1)
            sa = s_all[:].rearrange("p b h g -> p (b h) g")
            V.tensor_reduce(small_a[:], sa, AX, ALU.max).then_inc(m_turned, 1)
            link(V.memset(p_blocks[:], 0.0))
            dve.wait_ge(m_turned, 2)
            link(V.tensor_reduce(small_c[0:64, 0:1], ps[0:64, 5, 0:P], AX, ALU.max))
            V.tensor_scalar(small_b[0:64, :], ident[0:64, 0:64], small_c[0:64, 0:1], None, ALU.mult).then_inc(m_diag, 1)
            dve.wait_ge(m_cast, 1)
            V.tensor_tensor(sa, sa, ps[:, 6, 0:64][:, :, None].to_broadcast([P, 64, PAGES + 1]), ALU.subtract).then_inc(s_shifted, 1)
            dve.wait_ge(d_sig, 1)
            U = CD_GATE
            wd = par_of("conv_d", 4 * CF_TAPS).rearrange("p (t j) -> p t j", j=CF_TAPS)
            link(V.tensor_tensor(pj2[:, U:U + 4, :], pj2[:, U:U + 4, :], pj2[:, CD_A:CD_A + 4, :], ALU.mult))
            V.memset(upad[:, :, 0:U_PAD], 0.0)
            link(V.tensor_copy(upad[:, :, U_PAD:U_PAD + TP], pj2[:, U:U + 4, 0:TP]))
            for t in range(4):
                last = V.tensor_scalar(pj2[:, U + t, 0:TP], upad[:, t, 0:TP], wd[:, t, 0:1], None, ALU.mult)
            link(last)
            dve.wait_ge(p_all, 1)
            V.tensor_reduce(small_c[:], sa, AX, ALU.add).then_inc(l_part, 1)
            dve.wait_ge(l_sum, 1)
            link(V.reciprocal(small_d[:], ps[:, 7, 0:64]))

            dve.wait_ge(v_tok, 2)

            def unit_max(hp, u):
                tt = u % 4
                dve.wait_ge(s_ready, hp * 8 + u + 1)
                V.tensor_reduce(tiny[:, u % 2:u % 2 + 1], ps[:, u % 2, 0:P * (tt + 1)], AX, ALU.max, negate=True).then_inc(neg_max, 1)

            def tap(j, tiles):
                if tiles[0] == 0:
                    dve.wait_ge(d_tap, 4 * j - 4)
                for t in tiles:
                    V.scalar_tensor_tensor(out=pj2[:, U + t, 0:TP], in0=upad[:, t, bass.ds(j, TP)], scalar=wd[:, t, bass.ds(j, 1)],
                                           in1=pj2[:, U + t, 0:TP], op0=ALU.mult, op1=ALU.add).then_inc(d_tap, 1)

            TAPS = (CF_TAPS - 1) // 4
            o0 = own[0]
            with dve.Fori(0, 4) as hp:
                dve.wait_ge(pv_done, hp * 8 + 2)
                V.tensor_scalar(q_st[:], pj2[:, bass.ds(hp, 1), 0:TP].rearrange("p o n -> p (o n)"), 64 ** -0.5, None, ALU.mult)
                V.tensor_copy(k_st[:], pj2[:, bass.ds(hp + CD_K, 1), 0:TP].rearrange("p o n -> p (o n)"))
                V.tensor_copy(v_st[:], vtok2[:, :, bass.ds(hp * P, P)])
                for h2 in range(2):
                    last = V.tensor_scalar(hsel[:, h2, :], hrow[:], pick[:, bass.ds(hp * 2 + h2, 1)], None, ALU.mult)
                last.then_inc(fox_staged, 1)
                for two in range(2):
                    dve.wait_ge(pages_free, hp * 8 + (4 * two + 32))
                    V.tensor_copy(p_blocks[:, two, :, 0:8],
                                  s_all[:, bass.ds(hp * 2 + two, 1), :, 0:PAGES].rearrange("p o h g -> p g (o h)")).then_inc(p_staged, 1)
                unit_max(hp, 0)
                for u in range(8):
                    tt = u % 4
                    if u < 7:
                        unit_max(hp, u + 1)
                        tap(hp * TAPS + (u + 1), (0, 1))
                    dve.wait_ge(exp_done, hp * 8 + u + 3)
                    V.reciprocal(tiny[:, 4 + u % 2:5 + u % 2], tiny[:, 2 + u % 2:3 + u % 2]).then_inc(dve_own, 1)
                    dve.wait_ge(dve_own, hp * 8 + (o0 + u + 1))
                    V.tensor_scalar(prob[:, u % 2, 0:P * (tt + 1)], prob[:, u % 2, 0:P * (tt + 1)],
                                    tiny[:, 4 + u % 2:5 + u % 2], None, ALU.mult).then_inc(p_ready, 1)
                    if u < 7:
                        tap(hp * TAPS + (u + 1), (2, 3))
                    if u % 4 == 3:
                        dve.wait_ge(pages_free, hp * 8 + (4 * (u // 4) + 40))
                        dve.wait_ge(pv_all, hp * 2 + u // 4)
                        V.tensor_tensor(v_rows[:].rearrange("p (h d) -> p h d", h=8),
                                        ps[:, 5 + 2 * (u // 4), :].rearrange("p (h d) -> p h d", h=8),
                                        pick[:, :, None].to_broadcast([P, 8, 64]), ALU.mult).then_inc(v_masked, 1)
            own[0] += 32
            for j in range(4 * TAPS + 1, CF_TAPS):
                tap(j, range(4))
            dve.wait_ge(conv_d_in, 16)
            link(V.tensor_copy(ext_d[:, :, :, CF_TAPS - 1], pj2[:, U:U + 4, TP:T]))
            link(V.tensor_tensor(prod_d[:], ext_d[:], wd[:, :, None, :].to_broadcast([P, 4, TS, CF_TAPS]), ALU.mult))
            V.tensor_reduce(pj2[:, U:U + 4, TP:T], prod_d[:], AX, ALU.add).then_inc(d_u, 1)
            dve.wait_ge(self_cast, 1)
            dve.wait_ge(pv_all, NB)
            for h2 in range(2):
                r = slice(64 * h2, 64 * h2 + 64)

                def of(ap):
                    return ap.rearrange("p (b a c) -> p a b c", b=NB, a=4)[:, :, :, h2]

                past = ps[r, 6, 0:32].rearrange("p (b a) -> p a b", a=4)
                acc_o = small_a[r, 0:32].rearrange("p (a b) -> p a b", a=4)
                link(V.tensor_tensor(acc_o, of(ps[r, 6, 64:128]), pj2[r, CD_V:CD_V + 4, TP:T], ALU.mult))
                link(V.tensor_tensor(acc_o, acc_o, past, ALU.add))
                last = V.tensor_tensor(pj2[r, CD_Q:CD_Q + 4, TP:T], acc_o, of(small_d[r, :]), ALU.mult)
            last.then_inc(y_cd, 1)
            normalise_d()
            rest_rows(lambda k: pj2[:, k if k < 4 else CD_GATE + k - 4, :], 4 * KD)
            residual_and_center("cd_out", 3)
            normalise_x(3)
            hidden("f1_in")
            residual_and_center("f1_out", 4)
            normalise_x(4)


D_LN = 2
LN_BASE = [0, 8, 16, 20, 28]
LN_OF = [0, 1, None, 2, 3]
NEXT = {"ab_in": "ab_out", "ab_out": "f0_in", "f0_in": "f0_out", "f0_out": "cd_in", "cd_in": "cd_out",
        "cd_out": "f1_in", "f1_in": "f1_out", "f1_out": None}
OUT_AB = 4
OUT_CD = 8

_OUTS = {
    "y": (P, KD, T), "conv_a_p": (P, 4, 2), "conv_a_s": (P, 4, TS, 2), "gla_p": (P, 2, P), "gla_s": (P, NB, 2, P),
    "kt": (P, 4, T), "vt": (P, 4, T), "logf": (8, T), "conv_d_p": (P, 4, 30), "conv_d_s": (P, 4, TS, 30),
}


def _chunks(a):
    return np.moveaxis(a.reshape((a.shape[0] // P, P) + a.shape[1:]), 0, 1)


def _slots(w, blocks):
    parts = w.shape[0] // (P * blocks)
    w = w.reshape(parts, blocks, P, w.shape[1] // P, P)
    return np.ascontiguousarray(w.transpose(3, 0, 2, 1, 4)).reshape(-1, P, blocks * P)


def _constants():
    c = np.zeros((P, CONST_COLS), np.float32)
    i = np.arange(P)
    c[:, 0:128] = np.eye(P)
    c[:, 128:256] = 1.0
    c[:, 256:384] = i[:, None] > i[None, :]
    c[:, 384:896] = np.arange(TP) % P != 0
    c[0:8, 896:904] = np.eye(8)
    c[32:40, 896:904] = np.eye(8)
    c[64:72, 896:904] = np.eye(8)
    c[96:104, 896:904] = np.eye(8)
    c[:, 904:1032] = np.where(i[None, :] > i[:, None], NEG, 0.0)
    m = np.zeros((P, IMASK_COLS), np.int32)
    for l in range(LEVELS):
        half = P >> (l + 1)
        t = i[(i % (2 * half)) >= half]
        s = i[:, None]
        m[:, 64 * l:64 * l + 64] = (s // (2 * half) == t // (2 * half)) & (s % (2 * half) < half)
    m[:, 64 * LEVELS:] = np.eye(P)
    return c, m


def kernel(x_prompt, x_sample, state_conv_a, state_gla, cache_k, cache_v, cache_logf, state_conv_d, page_table,
           ab_w_in, ab_conv_w, gla_w_gate2, gla_b_gate, gla_norm_g, ab_w_out,
           cd_w_in, fox_b_f, cf_conv_w, cf_conv_b, cf_ln_g, cf_ln_b, cd_w_out,
           ffn_w_in, ffn_w_out, ln_g, ln_b):
    import concourse.bacc as _bacc
    from concourse import mybir as _mybir
    from concourse.bass_utils import run_bass_kernel_spmd as _run

    def arr(a):
        return np.asarray(a)

    arrays = {}
    tokens = np.concatenate([arr(x_prompt)[0], arr(x_sample)[:, 0]], 0)
    arrays["xt"] = _chunks(tokens.T)
    w = arr(ab_w_in)
    bg, cg, hv, q, k, v, g, r = np.split(w, np.cumsum([512, 512, 512, 256, 256, 512, 512]), axis=1)
    arrays["w_ab_in"] = _slots(np.concatenate([v, q, k, g, cg, hv, bg], 1), KD)
    arrays["w_ab_out"] = _slots(arr(ab_w_out), KD)
    cq, ck, cv, cf, ca, cgate = np.split(arr(cd_w_in), np.cumsum([512, 512, 512, 8, 512]), axis=1)
    arrays["w_cd_in"] = _slots(np.concatenate([cq, ck, cv, cgate, ca], 1), KD)
    arrays["w_cd_out"] = _slots(arr(cd_w_out), KD)
    for l in range(2):
        wi = arr(ffn_w_in)[l].reshape(D, 2, KF, P).transpose(0, 2, 1, 3).reshape(D, 2 * DFF)
        arrays[f"w_f{l}_in"] = _slots(wi, KD)
        arrays[f"w_f{l}_out"] = _slots(arr(ffn_w_out)[l], HALF_KF)
    par = np.zeros((P, PARAM_COLS), np.float32)

    def put(name, a, rows=slice(0, P)):
        a = np.asarray(a)
        a = a.reshape(a.shape[0], -1)
        par[rows, PARAM_AT[name]:PARAM_AT[name] + a.shape[1]] = a

    put("ln_g", _chunks(arr(ln_g).reshape(4, D).T).transpose(0, 2, 1))
    put("ln_b", _chunks(arr(ln_b).reshape(4, D).T).transpose(0, 2, 1))
    put("conv_a", _chunks(arr(ab_conv_w).T))
    put("conv_d", _chunks(arr(cf_conv_w).T))
    put("cf_b", _chunks(arr(cf_conv_b)))
    put("cf_g", _chunks(arr(cf_ln_g)))
    put("cf_lb", _chunks(arr(cf_ln_b)))
    put("b_gate", _chunks(arr(gla_b_gate)))
    put("norm_g", arr(gla_norm_g)[:, None])
    put("b_f", arr(fox_b_f)[:, None], slice(0, 8))
    put("b_f", arr(fox_b_f)[:, None], slice(32, 40))
    put("w_gate2", arr(gla_w_gate2), slice(0, 16))
    put("w_r", _chunks(r))
    wf = np.zeros((D, 40), np.float32)
    wf[:, 0:8] = cf
    wf[:, 32:40] = cf
    put("w_f", _chunks(wf))
    arrays["params"] = par
    arrays["consts"], arrays["imask"] = _constants()
    arrays["table"] = arr(page_table).astype(np.int32).reshape(1, -1)
    arrays["conv_a_state"] = arr(state_conv_a).reshape(TS, 2, 4, P).transpose(3, 2, 0, 1)
    arrays["conv_d_state"] = arr(state_conv_d).reshape(TS, 30, 4, P).transpose(3, 2, 0, 1)
    arrays["gla_state"] = arr(state_gla).reshape(NB, 2, 2, 64, P).transpose(2, 3, 0, 1, 4).reshape(P, NB, 2, P)
    arrays["cache_kt"] = arr(cache_k).reshape(PHYS, P, 4, P).transpose(0, 3, 2, 1).reshape(PHYS, P, 512)
    arrays["cache_v"] = arr(cache_v).reshape(PHYS, P, 512)
    arrays["cache_logf"] = arr(cache_logf)

    nc = _bacc.Bacc("TRN2", target_bir_lowering=False, num_devices=1)
    A, O, feed = {}, {}, {}
    for name, a in arrays.items():
        a = np.ascontiguousarray(a)
        feed[f"in_{name}"] = a
        A[name] = nc.dram_tensor(f"in_{name}", a.shape, _mybir.dt.from_np(a.dtype), kind="ExternalInput").ap()
    for name, shape in _OUTS.items():
        O[name] = nc.dram_tensor(f"out_{name}", shape, F32, kind="ExternalOutput").ap()
    bass_hybrid_step(nc, A, O)
    res = _run(nc, [feed], core_ids=[0]).results[0]
    o = {n: np.asarray(res[f"out_{n}"]) for n in _OUTS}

    def rows(a):
        return np.ascontiguousarray(a.transpose(2, 1, 0)).reshape(a.shape[2], -1)

    y, kt, vt, lf = rows(o["y"]), rows(o["kt"]), rows(o["vt"]), o["logf"].T
    conv_a_p = np.ascontiguousarray(o["conv_a_p"].transpose(2, 1, 0)).reshape(1, 2, 512)
    conv_a_s = np.ascontiguousarray(o["conv_a_s"].transpose(2, 3, 1, 0)).reshape(NB, 2, 512)
    conv_d_p = np.ascontiguousarray(o["conv_d_p"].transpose(2, 1, 0)).reshape(1, 30, 512)
    conv_d_s = np.ascontiguousarray(o["conv_d_s"].transpose(2, 3, 1, 0)).reshape(NB, 30, 512)
    gla_p = np.ascontiguousarray(o["gla_p"].reshape(2, 64, 2, P).transpose(2, 0, 1, 3)).reshape(1, 4, 64, P)
    gla_s = np.ascontiguousarray(o["gla_s"].reshape(2, 64, NB, 2, P).transpose(2, 3, 0, 1, 4)).reshape(NB, 4, 64, P)

    def heads(a, n):
        return np.ascontiguousarray(a).reshape(n + (8, 64))

    return (y[None, :TP], y[TP:, None], conv_a_p, conv_a_s, gla_p, gla_s,
            heads(kt[:TP], (1, TP)), heads(kt[TP:], (TS, 1)), heads(vt[:TP], (1, TP)), heads(vt[TP:], (TS, 1)),
            np.ascontiguousarray(lf[None, :TP]), np.ascontiguousarray(lf[TP:, None]), conv_d_p, conv_d_s)
```

```python
from contextlib import ExitStack

import numpy as np
import concourse.bass as bass
from concourse import mybir

F32 = mybir.dt.float32
F32R = mybir.dt.float32r
BF16 = mybir.dt.bfloat16
I32 = mybir.dt.int32
ALU = mybir.AluOpType
ACT = mybir.ActivationFunctionType
AX = mybir.AxisListType.X

P = 128
D = 1024
KD = D // P
TP = 512
TS = 8
T = TP + TS
HT = T // 2
NB = 8
PAGES = 16
PHYS = 160
DFF = 2816
KF = DFF // P
HALF_KF = KF // 2
ALPHA = float(4 ** 0.25)
EPS = 1e-5
GUESS = 3
CENTERED = (3, 4, 0, 5, 1, 6, 2, 7)
CENTERED_AT = {4: (0, 1, 2), 5: (3, 4), 6: (5, 6), 7: (7,)}
NEG = -1e30
GC = TP // P
LEVELS = 7
CF_TAPS = 31
DVE_TILES = 3
D_SAMPLE_STEPS = 8
RAW = 4
SPLIT = 2
TILES_AB = 24
TILES_CD = 20
AB_V, AB_Q, AB_K, AB_CG, AB_HV, AB_BG, AB_G = 0, 4, 6, 8, 12, 16, 20
CD_Q, CD_K, CD_V, CD_GATE, CD_A = 0, 4, 8, 12, 16

_PARAMS = [("ln_g", 32), ("ln_b", 32), ("conv_a", 12), ("conv_d", 124), ("cf_b", 4), ("cf_g", 4), ("cf_lb", 4),
           ("b_gate", 2), ("norm_g", 1), ("b_f", 1), ("w_gate2", 256), ("w_r", 128), ("w_f", 320)]
PARAM_AT, _n = {}, 0
for _name, _w in _PARAMS:
    PARAM_AT[_name] = _n
    _n += _w
PARAM_COLS = _n
CONST_AT = {"ident": 0, "ones": 128, "later": 256, "scan": 384, "pick": 896, "causal": 904}
CONST_COLS = 904 + 128
IMASK_COLS = LEVELS * 64 + 128


def bass_hybrid_step(nc, A, O):
    with ExitStack() as ctx:
        base = (nc.sbuf_base + 31) // 32 * 32

        def at(name, shape, offset, dt=F32):
            return nc.alloc_sbuf_tensor_at(name, shape, dt, offset=base + offset)

        def sem(name):
            return ctx.enter_context(nc.semaphore(name))

        TB = T * 4
        x = at("x", [P, KD, T], 0)
        o_xs = KD * TB
        xh = at("xh", [P, KD, T], o_xs, F32R)
        xl = at("xl", [P, KD, T], o_xs + KD * TB, F32R)
        o_w = o_xs + 2 * KD * TB
        SLOT = HALF_KF * P
        raw = at("raw", [P, RAW, SLOT], o_w)
        wh = at("wh", [P, SPLIT, SLOT], o_w + RAW * SLOT * 4, F32R)
        wl = at("wl", [P, SPLIT, SLOT], o_w + (RAW + SPLIT) * SLOT * 4, F32R)
        o_z = o_w + (RAW + 2 * SPLIT) * SLOT * 4
        zone = 2 * KF * TB
        o_s = o_z + zone
        small = [o_s]

        def keep(name, shape, dt=F32):
            n = int(np.prod(shape[1:])) * (2 if dt == BF16 else 4)
            t = at(name, shape, small[0], dt)
            small[0] += (n + 31) // 32 * 32
            return t

        par = keep("par", [P, PARAM_COLS])
        con = keep("con", [P, CONST_COLS])
        imask = keep("imask", [P, IMASK_COLS], I32)
        table = keep("table", [1, NB * PAGES], I32)
        ident_b = keep("ident_b", [P, P], BF16)
        causal_b = keep("causal_b", [P, P], BF16)
        o_rstd = small[0]
        rstd = keep("rstd", [P, T])
        conv_a_state = keep("conv_a_state", [P, 4, TS, 2])
        tap_t = at("tap_t", [P, 4 - DVE_TILES, TP], small[0])
        o_lf_pages = small[0]
        lf_pages = keep("lf_pages", [P, PAGES, NB, 8])
        qblk = keep("qblk", [P, 4, NB, 2])
        q_wide = keep("q_wide", [P, 2, 4 * 34])
        small_a = keep("small_a", [P, 64])
        small_b = keep("small_b", [P, 64])
        small_c = keep("small_c", [P, 64])
        small_d = keep("small_d", [P, 64])
        tiny = keep("tiny", [P, 16])
        eps_c = keep("eps_c", [P, 1])
        assert base + small[0] <= nc.sbuf_usable_end, (base + small[0], nc.sbuf_usable_end)

        def par_of(name, w):
            return par[:, PARAM_AT[name]:PARAM_AT[name] + w]

        ident = con[:, 0:128]
        ones = con[:, 128:256]
        later = con[:, 256:384]
        scan_on = con[:, 384:896]
        pick = con[:, 896:904]

        hh = at("hh", [P, KF, T], o_z, F32R)
        hl = at("hl", [P, KF, T], o_z + KF * TB, F32R)
        o_gate_t = small[0]
        gate_t = keep("gate_t", [P, T])
        hid_t = keep("hid_t", [P, T])
        assert base + small[0] <= nc.sbuf_usable_end, (base + small[0], nc.sbuf_usable_end)

        pj = at("pj", [P, TILES_AB, T], o_z)
        o_g = o_z + TILES_AB * TB
        attn = at("attn", [P, GC * 4, P], o_g)
        vtok = at("vtok", [P, GC, 512], o_g + 8192)
        gla_o = at("gla_o", [P, 4, T], o_g + 24576)
        gla_s0 = at("gla_s0", [P, NB, 2, P], o_g + 24576 + 8320)
        assert 24576 + 8320 + 8192 + TILES_AB * TB <= zone
        kwtok = at("kwtok", [P, GC, 256], o_xs)
        gla_s = at("gla_s", [P, GC, 2, P], o_xs + 4096)
        sam_q = at("sam_q", [P, NB, 2, 32], o_xs + 8192)
        sam_copy = at("sam_copy", [P, 512], o_xs + 10240)
        gla_kv = at("gla_kv", [P, NB, 2, P], o_z + AB_V * TB)
        rms_sq = at("rms_sq", [P, 4, T], o_z + AB_Q * TB)
        gdiff = at("gdiff", [P, 2, 2, TP], o_g + 16384)
        zpre = at("zpre", [P, 2, T], o_g)
        zexp = at("zexp", [P, 2, T], o_g + 16384)
        r_t = at("r_t", [16, T], o_g + 24576)
        gcum = at("gcum", [P, 2, TP], o_g + 24576)
        loga = at("loga", [P, 2, T], o_g + 28672)
        qk = [at("qk0", [P, 2, TP], o_lf_pages), at("qk1", [P, 2, TP], o_gate_t)]
        vsam = at("vsam", [NB, 512], o_rstd)

        pj2 = at("pj2", [P, TILES_CD, T], o_z)
        U_PAD = CF_TAPS - 1
        upad = at("upad", [P, 4, U_PAD + TP], o_z + CD_A * TB)
        o_k = o_z + TILES_CD * TB + 384
        assert 4 * (U_PAD + TP) * 4 <= 4 * TB + 384
        pages = at("pages", [P, 4, 4, 512], o_k)
        o_d = o_k + 32768
        lf_later = at("lf_later", [P, PAGES, 64], o_d)
        frow = [at(f"frow{i}", [40, T], o) for i, o in enumerate((o_gate_t, o_gate_t + TB, o_d + 8448, o_d + 8448 + TB,
                                                                  o_d + 8448 + 2 * TB))]
        squares_d = at("squares_d", [P, 4, T], o_k)
        s_all = at("s_all", [P, NB, 8, PAGES + 1], o_k + 32768)
        decay = at("decay", [P, NB, 8, PAGES], o_k + 32768 + 4352)
        ext_d = at("ext_d", [P, 4, TS, 31], o_k + 32768 + 8448)
        prod_d = at("prod_d", [P, 4, TS, 31], o_lf_pages)
        vtok2 = at("vtok2", [P, GC, 512], o_xs)
        prob = at("prob", [P, 2, 512], o_xs + 8192)
        prob_t = at("prob_t", [P, 2, 512], o_xs + 12288)
        grow = at("grow", [P, 512], o_xs + 20480)
        hrow = at("hrow", [P, 512], o_xs + 22528)
        q_st = [at(f"q_st{i}", [P, 512], o) for i, o in enumerate((o_xs + 16384, o_gate_t))]
        v_st = [at(f"v_st{i}", [P, GC, P], o) for i, o in enumerate((o_xs + 18432, o_gate_t + TB))]
        k_st = [at("k_st0", [P, 512], o_xs + 28672), rstd]
        o_hsel = o_d + 8448 + 3968
        assert o_hsel + 4096 <= o_z + zone
        hsel = [at(f"hsel{i}", [P, 2, 512], o) for i, o in enumerate((o_xs + 24576, o_hsel))]
        score_rows = at("score_rows", [P, 512], o_d + 8448 + TB)
        v_rows = at("v_rows", [P, 512], o_xs + 30720)
        assert 30720 + 2048 <= 2 * KD * TB
        p_blocks = at("p_blocks", [P, 2, PAGES, 32], o_d + 4352)

        ps = ctx.enter_context(nc.psum_tensor("ps", [P, 8, 512], F32))


        x_in = [sem(f"x_in{i}") for i in range(4)]
        par_in = sem("par_in")
        con_in = sem("con_in")
        state_in = sem("state_in")
        conv_d_in = sem("conv_d_in")
        w_landed = [sem(f"w_landed{i}") for i in range(RAW)]
        w_rounded = sem("w_rounded")
        w_rest = sem("w_rest")
        slot_used = sem("slot_used")
        x_hi = sem("x_hi")
        x_split = sem("x_split")
        acc_free = [sem(f"acc_free{i}") for i in range(2)]
        dve_own = sem("dve_own")
        act_own = sem("act_own")
        setup = sem("setup")
        ln_first = sem("ln_first")
        ln_guess = sem("ln_guess")
        ln_part = sem("ln_part")
        ln_added = sem("ln_added")
        ln_middle = sem("ln_middle")
        ln_squared = sem("ln_squared")
        ln_sum = sem("ln_sum")
        ln_centered = sem("ln_centered")
        ln_sq = sem("ln_sq")
        ln_var = sem("ln_var")
        ln_veps = sem("ln_veps")
        ln_std = sem("ln_std")
        ln_scaled = sem("ln_scaled")
        ln_out = sem("ln_out")
        gate_ready = sem("gate_ready")
        hid_ready = sem("hid_ready")
        hid_hi = sem("hid_hi")
        hid_split = sem("hid_split")
        out_sent = sem("out_sent")
        y_sent = sem("y_sent")
        logf_sent = sem("logf_sent")
        r_sum, r_copied, z_sum, z_log, log_a = (sem(n) for n in ("r_sum", "r_copied", "z_sum", "z_log", "log_a"))
        v_turned, v_tok = sem("v_turned"), sem("v_tok")
        lv_diff, lv_exp, lv_qk, lv_scores, lv_kept = (sem(n) for n in ("lv_diff", "lv_exp", "lv_qk", "lv_scores", "lv_kept"))
        attn_zero = sem("attn_zero")
        kw_diff, kw_exp, kw_ready, kw_turned, kw_tok = (sem(n) for n in ("kw_diff", "kw_exp", "kw_ready", "kw_turned", "kw_tok"))
        kv_sum, state_c, o_sum, o_copied = (sem(n) for n in ("kv_sum", "state_c", "o_sum", "o_copied"))
        sam_decay, sam_decayed, vsam_turned, vsam_copied, vb_sum, vb_used, sam_state, sq_staged, sam_rows, sam_o = (
            sem(n) for n in ("sam_decay", "sam_decayed", "vsam_turned", "vsam_copied", "vb_sum", "vb_used", "sam_state", "sq_staged", "sam_rows", "sam_o"))
        rms_squared, rms_sum, rms_eps, rms_std, rms_root, rms_cast, g_silu, conv_y, y_ab = (
            sem(n) for n in ("rms_squared", "rms_sum", "rms_eps", "rms_std", "rms_root", "rms_cast", "g_silu", "conv_y", "y_ab"))
        conv_a_ready = sem("conv_a_ready")
        f_sum, f_log, f_done, later_in, later_sum, decay_ready, rows_used, q_staged, ks_copied, kt_done, p_staged, v_masked = (
            sem(n) for n in ("f_sum", "f_log", "f_done", "later_in", "later_sum", "decay_ready", "rows_used", "q_staged", "ks_copied",
                          "kt_done", "p_staged", "v_masked"))
        fox_staged, s_ready, neg_max, exp_done, p_ready, p_turned, pt_copied, pv_done, o_evac = (
            sem(n) for n in ("fox_staged", "s_ready", "neg_max", "exp_done", "p_ready", "p_turned", "pt_copied", "pv_done", "o_evac"))
        self_in, self_sum = sem("self_in"), sem("self_sum")
        page_in = [sem(f"page_in{i}") for i in range(4)]
        lf_in = sem("lf_in")
        pages_free = sem("pages_free")
        s_ready_all, m_turned, m_diag, m_cast, s_shifted, p_all, l_part, l_sum, pv_all, self_cast = (
            sem(n) for n in ("s_ready_all", "m_turned", "m_diag", "m_cast", "s_shifted", "p_all", "l_part", "l_sum", "pv_all", "self_cast"))
        d_sig, u_ready, d_tap, tap_product, pool_tap, d_sampled, y_cd = (sem(n) for n in ("d_sig", "u_ready", "d_tap", "tap_product", "pool_tap", "d_sampled", "y_cd"))

        block = ctx.enter_context(nc.Block())

        PH = {}
        s0 = t0 = 0
        for name, slots, tiles in (("ab_in", 24, 24), ("ab_out", 8, 8), ("f0_in", 44, 44), ("f0_out", 16, 8),
                                   ("cd_in", 20, 20), ("cd_out", 8, 8), ("f1_in", 44, 44), ("f1_out", 16, 8)):
            PH[name] = (s0, slots, t0, tiles)
            s0, t0 = s0 + slots, t0 + tiles
        SLOTS = s0
        BLOCKS = {"f0_out": HALF_KF, "f1_out": HALF_KF}

        def halves(ap):
            return ap.rearrange("p (h n) -> p h n", h=2)

        @block.sync
        def _(sp):
            def weights(name, i):
                for j in range(RAW):
                    weight_slot(name, i, j)

            def weight_slot(name, i, j, first=False):
                if not first:
                    sp.wait_ge(w_rest, PH[name][0] + 4 * i + j + 1 - RAW)
                src = A["w_" + name][bass.ds(4 * i + j, 1)].rearrange("o p n -> p (o n)")
                sp.dma_start(raw[:, j, 0:BLOCKS.get(name, KD) * P], src).then_inc(w_landed[j], 16)

            for c in range(4):
                sp.dma_start(x[:, 2 * c:2 * c + 2, :], A["xt"][:, 2 * c:2 * c + 2, :]).then_inc(x_in[c], 16)
                if c < 2:
                    weight_slot("ab_in", 0, c, first=True)
                if c == 0:
                    sp.dma_start(par[:], A["params"]).then_inc(par_in, 16)
            weight_slot("ab_in", 0, 2, first=True)
            weight_slot("ab_in", 0, 3, first=True)
            sp.dma_start(con[:], A["consts"]).then_inc(con_in, 16)
            sp.dma_start(imask[:], A["imask"]).then_inc(state_in, 16)
            sp.dma_start(table[:], A["table"]).then_inc(state_in, 16)
            sp.dma_start(conv_a_state[:], A["conv_a_state"]).then_inc(state_in, 16)
            sp.dma_start(gla_s0[:], A["gla_state"]).then_inc(state_in, 16)
            with sp.Fori(1, 6) as i:
                weights("ab_in", i)
            with sp.Fori(0, 2) as i:
                weights("ab_out", i)
            sp.wait_ge(state_in, 64)
            with sp.Fori(0, NB) as i:
                weights("f0_in", i)
                for g in range(PAGES):
                    if g % 8 == 0:
                        ids = nc.values_load_multi_w_load_instructions(
                            table[0:1, bass.ds(i * PAGES + g, 8)], engines=(mybir.EngineType.SP,),
                            min_val=0, max_val=PHYS - 1)[1]
                    sp.dma_start(lf_pages[:, g, bass.ds(i, 1), :].rearrange("p o h -> p (o h)"),
                                 A["cache_logf"][bass.ds(ids[g % 8], 1)].rearrange("o p h -> p (o h)")).then_inc(lf_in, 16)
            with sp.Fori(NB, 11) as i:
                weights("f0_in", i)
            with sp.Fori(0, 4) as i:
                weights("f0_out", i)
            for i in range(2):
                weights("cd_in", i)

            def page_slots(cache, n, used):
                ids = nc.values_load_multi_w_load_instructions(
                    table[0:1, bass.ds(n, 8)], engines=(mybir.EngineType.SP,), min_val=0, max_val=PHYS - 1)[1]
                for h, count in enumerate(used):
                    sp.wait_ge(pages_free, count + 1)
                    s = used_slot[0] % 4
                    used_slot[0] += 1
                    for g in range(4):
                        sp.dma_start(pages[:, s, g, :], cache[bass.ds(ids[4 * h + g], 1)].rearrange("o p n -> p (o n)"))\
                          .then_inc(page_in[s], 16)

            used_slot = [0]

            def weights_and_keys(i, name, k):
                for j in range(4):
                    weight_slot(name, k, j)
                    page_slots(A["cache_kt"], (i - 1) * 32 + 8 * j, [(i - 1) * 8 + (2 * j), (i - 1) * 8 + (2 * j + 1)])

            with sp.Fori(1, 4) as i:
                weights_and_keys(i, "cd_in", i + 1)
            weights_and_keys(4, "cd_out", 0)

            def values(b):
                for half in range(2):
                    page_slots(A["cache_v"], b * PAGES + 8 * half, [b * 4 + (32 + 2 * half), b * 4 + (33 + 2 * half)])

            values(0)
            sp.wait_ge(rows_used, 1)
            sp.wait_ge(logf_sent, 16)
            sp.dma_start(ext_d[:, :, :, 0:CF_TAPS - 1], A["conv_d_state"]).then_inc(conv_d_in, 16)
            with sp.Fori(1, NB) as b:
                values(b)
            weights("cd_out", 1)
            with sp.Fori(0, 11) as i:
                weights("f1_in", i)
            with sp.Fori(0, 4) as i:
                weights("f1_out", i)
            for c in range(4):
                sp.wait_ge(ln_out, 3 * KD + 4 + 2 * c + 2)
                sp.dma_start(O["y"][:, 2 * c:2 * c + 2, :], x[:, 2 * c:2 * c + 2, :]).then_inc(y_sent, 16)
            sp.wait_ge(y_sent, 64)
            sp.wait_ge(out_sent, 16 * OUT_CD)

        @block.scalar
        def _(act):
            own = [0]

            def link(ins):
                own[0] += 1
                ins.then_inc(act_own, 1)
                act.wait_ge(act_own, own[0])

            act.sem_inc(exp_done, 2)
            act.sem_inc(pt_copied, 2)
            act.sem_inc(ks_copied, 2)

            def rounded(i4, n, j, b):
                act.wait_ge(w_landed[j], i4)
                act.wait_ge(slot_used, n + 1)
                nc.scalar.activation(wh[:, j % SPLIT, 0:b * P], raw[:, j, 0:b * P], ACT.Copy).then_inc(w_rounded, 1)

            def next_rounded(name, i, j, last):
                s = PH[name][0]
                b = BLOCKS.get(name, KD)
                if last and j >= 4 - SPLIT:
                    if NEXT[name] is None:
                        return
                    b = BLOCKS.get(NEXT[name], KD)
                group = s // 4 + i + (j + SPLIT) // 4
                rounded(group * 16 + 16, s + 4 * i + j + SPLIT, (j + SPLIT) % 4, b)

            def product(name, tile=None, peeled=1, behind_first=None, inside=None, behind=None):
                n = PH[name][1] // 4
                start = 0
                if behind:
                    for i in range(n):
                        for j in range(4):
                            next_rounded(name, i, j, i == n - 1)
                            if j == 0:
                                inside(i)
                        behind(i)
                    return
                if behind_first:
                    for j in range(4):
                        next_rounded(name, 0, j, False)
                    behind_first()
                    for j in range(4):
                        next_rounded(name, 1, j, False)
                        tile(1, j)
                    start = 2
                if n > peeled:
                    with act.Fori(start, n - peeled) as i:
                        for j in range(4):
                            next_rounded(name, i, j, False)
                            if tile and peeled == 1:
                                tile(i, j)
                for i in range(n - peeled, n):
                    for j in range(4):
                        next_rounded(name, i, j, i == n - 1)
                        if tile:
                            tile(i, j)

            def split_rows(src, k):
                nc.scalar.activation(xh[:, k, :], src, ACT.Copy).then_inc(x_hi, 1)

            def normalise_d():
                g, b = par_of("cf_g", 4), par_of("cf_lb", 4)
                base = LN_BASE[D_LN]
                for k in range(4):
                    act.wait_ge(ln_centered, base + k + 1)
                    nc.scalar.activation(squares_d[:, k, :], pj2[:, CD_GATE + k, :], ACT.Square).then_inc(ln_sq, 1)
                act.wait_ge(ln_veps, D_LN + 1)
                nc.scalar.activation(rstd[:], rstd[:], ACT.Sqrt, bias=eps_c[:, 0:1]).then_inc(ln_std, 1)
                for k in range(4):
                    act.wait_ge(ln_scaled, base + k + 1)
                    nc.scalar.activation(pj2[:, CD_GATE + k, :], pj2[:, CD_GATE + k, :], ACT.Silu,
                                         bias=b[:, k:k + 1], scale=g[:, k:k + 1]).then_inc(ln_out, 1)
                for k in range(4):
                    act.wait_ge(ln_out, base + k + 1)
                    split_rows(pj2[:, CD_GATE + k, :], 4 + k)

            def squares_of(idx):
                base, of_d = LN_BASE[idx], LN_OF[idx]

                def after_tile(m):
                    for i in CENTERED_AT.get(m, ()):
                        act.wait_ge(ln_centered, base + i + 1)
                        if i >= 2:
                            act.wait_ge(ln_added, 6 * of_d + i - 1)
                        nc.scalar.activation((gate_t if i == 0 else hid_t)[:], x[:, CENTERED[i], :], ACT.Square).then_inc(ln_sq, 1)
                return after_tile

            def product_and_squares(name, idx):
                after_tile = squares_of(idx)
                if name in BLOCKS:
                    product(name, lambda i, j: after_tile(2 * i + j // 2) if j % 2 == 1 else None, peeled=2)
                else:
                    product(name, lambda i, j: after_tile(4 * i + j), peeled=2)

            def normalise_x(idx, split):
                at_g, at_b = (PARAM_AT[n] + 8 * LN_OF[idx] for n in ("ln_g", "ln_b"))
                base = LN_BASE[idx]
                act.wait_ge(ln_sum, idx + 1)
                nc.scalar.activation(halves(rstd[:]), ps[:, 6:8, 0:HT], ACT.Square).then_inc(ln_squared, 1)
                act.wait_ge(ln_veps, idx + 1)
                nc.scalar.activation(rstd[:], rstd[:], ACT.Sqrt, bias=eps_c[:, 0:1], scale=1.0 / D).then_inc(ln_std, 1)
                for k in range(KD + 1):
                    if k < KD:
                        act.wait_ge(ln_scaled, base + k + 1)
                        nc.scalar.activation(x[:, k, :], x[:, k, :], ACT.Identity, bias=par[:, at_b + k:at_b + k + 1],
                                             scale=par[:, at_g + k:at_g + k + 1]).then_inc(ln_out, 1)
                    if k > 0 and split:
                        act.wait_ge(ln_out, base + k)
                        split_rows(x[:, k - 1, :], k - 1)

            def gate_up(name):
                s, _, _, _ = PH[name]
                m0 = 0 if name == "f0_in" else 22

                def tile(i, j):
                    m = i * 2 + j // 2
                    act.wait_ge(slot_used, i * 4 + (SPLIT + s + j + 1))
                    if j % 2 == 0:
                        act.wait_ge(hid_ready, m0 + m + 1)
                        nc.scalar.activation(halves(gate_t[:]), ps[:, 0:2, 0:HT], ACT.Silu).then_inc(gate_ready, 1)
                        act.wait_ge(gate_ready, m0 + m + 1)
                        nc.scalar.sem_inc(acc_free[0], 1)
                    else:
                        act.wait_ge(hid_ready, m0 + m + 2)
                        nc.scalar.activation(hh[:, bass.ds(m, 1), :].rearrange("p o n -> p (o n)"), hid_t[:], ACT.Copy)\
                            .then_inc(hid_hi, 1)
                return tile

            rounded(16, 0, 0, KD)
            for k in range(KD):
                act.wait_ge(x_in[k // 2], 16)
                split_rows(x[:, k, :], k)
                if k == 1:
                    rounded(16, 1, 1, KD)
            act.wait_ge(par_in, 16)
            act.wait_ge(con_in, 16)
            nc.scalar.activation(ident_b[:], ident, ACT.Copy)
            nc.scalar.activation(causal_b[:], con[:, 904:1032], ACT.Copy).then_inc(setup, 1)
            act.wait_ge(setup, 2)
            def level_exps(levels):
                for l in levels:
                    act.wait_ge(lv_diff, l + 1)
                    nc.scalar.activation(gdiff[:, l % 2], gdiff[:, l % 2], ACT.Exp).then_inc(lv_exp, 1)

            def linear_attention(i):
                if i == 0:
                    act.wait_ge(z_sum, 1)
                    for t in range(2):
                        last = nc.scalar.activation(halves(zpre[:, t, :]), ps[:, 4 + 2 * t:6 + 2 * t, 0:HT], ACT.Identity,
                                                    bias=par[:, PARAM_AT["b_gate"] + t:PARAM_AT["b_gate"] + t + 1])
                    link(last)
                    link(nc.scalar.activation(zexp[:], zpre[:], ACT.Abs))
                    link(nc.scalar.activation(zexp[:], zexp[:], ACT.Exp, scale=-1.0))
                    nc.scalar.activation(zexp[:], zexp[:], ACT.Ln, bias=1.0).then_inc(z_log, 1)
                elif i == 1:
                    act.wait_ge(v_turned, 1)
                    for c in range(GC):
                        last = nc.scalar.activation(vtok[:, c, :], ps[:, 4 + c, :], ACT.Copy)
                    last.then_inc(v_tok, 1)
                    act.wait_ge(log_a, 1)
                    nc.scalar.activation(tiny[:].rearrange("p (a b) -> p a b", a=2), loga[:, :, TP:T], ACT.Exp).then_inc(sam_decay, 1)
                    level_exps((0, 1))
                elif i == 2:
                    act.wait_ge(vsam_turned, 1)
                    nc.scalar.activation(vsam[:], ps[0:NB, 7, :], ACT.Copy).then_inc(vsam_copied, 1)
                elif i == 5:
                    for j in range(2):
                        act.wait_ge(acc_free[j], TILES_AB // 2 + 1)
                    nc.scalar.activation(pj[:, AB_G:AB_G + 4, :], pj[:, AB_G:AB_G + 4, :], ACT.Silu).then_inc(g_silu, 1)

            def exps_inside(i):
                if i == 2 or i == 3:
                    level_exps((2 * i - 2, 2 * i - 1))
                elif i == 4:
                    level_exps((6,))
                elif i == 5:
                    act.wait_ge(kw_diff, 1)
                    nc.scalar.activation(gdiff[:, 0], gdiff[:, 0], ACT.Exp)
                    nc.scalar.activation(gdiff[:, 1], gcum[:], ACT.Exp).then_inc(kw_exp, 1)

            product("ab_in", inside=exps_inside, behind=linear_attention)
            act.wait_ge(kw_turned, 1)
            for c in range(GC):
                last = nc.scalar.activation(kwtok[:, c, :], ps[:, 4 + c // 2, 256 * (c % 2):256 * (c % 2) + 256], ACT.Copy)
            last.then_inc(kw_tok, 1)
            for c in range(GC):
                act.wait_ge(o_sum, c + 1)
                nc.scalar.activation(gla_o[:, :, P * c:P * c + P].rearrange("p (a c) t -> p c a t", c=2),
                                     ps[:, 2 * (c % 2):2 * (c % 2) + 2, 0:256].rearrange("p c (a t) -> p c a t", a=2),
                                     ACT.Copy).then_inc(o_copied, 1)
            act.wait_ge(o_copied, GC)
            nc.scalar.activation(rms_sq[:, :, 0:TP], gla_o[:, :, 0:TP], ACT.Square).then_inc(rms_squared, 1)
            act.wait_ge(sam_rows, 1)
            nc.scalar.activation(sam_copy[:], ps[:, 0, :], ACT.Copy).then_inc(sam_rows, 1)
            act.wait_ge(sam_o, 1)
            for part in range(2):
                last = nc.scalar.activation(gla_o[:, :, TP + 4 * part:TP + 4 * part + 4].rearrange("p (a c) g -> p a g c", c=2),
                                            ps[:, 1, 256 * part:256 * part + 256].rearrange("p (a g c) -> p a g c", a=2, g=4)[:, :, :, 0:2],
                                            ACT.Copy)
            link(last)
            nc.scalar.activation(rms_sq[:, :, TP:T], gla_o[:, :, TP:T], ACT.Square).then_inc(rms_squared, 1)
            act.wait_ge(rms_eps, 1)
            nc.scalar.activation(small_c[:, 0:20], small_c[:, 0:20], ACT.Sqrt).then_inc(rms_std, 1)
            act.wait_ge(out_sent, 16 * OUT_AB)
            act.wait_ge(conv_y, 1)
            for k in range(4):
                split_rows(pj[:, AB_HV + k, :], k)
            for h in range(4):
                act.wait_ge(y_ab, h + 1)
                split_rows(gla_o[:, h, :], 4 + h)
            product_and_squares("ab_out", 0)
            normalise_x(0, True)
            product("f0_in", gate_up("f0_in"))
            product_and_squares("f0_out", 1)
            normalise_x(1, True)

            def forget_gates():
                act.wait_ge(f_sum, 1)
                link(nc.scalar.activation(halves(frow[0][:]), ps[0:40, 4:6, 0:HT], ACT.Identity,
                                          bias=par[0:40, PARAM_AT["b_f"]:PARAM_AT["b_f"] + 1]))
                link(nc.scalar.activation(frow[1][:], frow[0][:], ACT.Abs))
                link(nc.scalar.activation(frow[1][:], frow[1][:], ACT.Exp, scale=-1.0))
                nc.scalar.activation(frow[2][:], frow[1][:], ACT.Ln, bias=1.0).then_inc(f_log, 1)

            def keys(i, j):
                if isinstance(i, int) and (i, j) == (4, 0):
                    for half in range(2):
                        act.wait_ge(acc_free[half], (PH["cd_in"][2] + CD_A) // 2 + 1)
                    nc.scalar.activation(pj2[:, CD_GATE:CD_GATE + 4, :], pj2[:, CD_GATE:CD_GATE + 4, :], ACT.Sigmoid)\
                        .then_inc(d_sig, 1)
                if j % 2 == 1:
                    act.wait_ge(f_done, 2)
                    act.wait_ge(pages_free, i * 8 + (4 * (j // 2)))
                    act.wait_ge(kt_done, i * 2 + (j // 2 - 2))
                    nc.scalar.activation(score_rows[:], ps[:, 5 + 2 * (j // 2), :], ACT.Copy).then_inc(ks_copied, 1)

            product("cd_in", tile=keys, behind_first=forget_gates)

            act.wait_ge(v_turned, 2)
            for c in range(GC):
                last = nc.scalar.activation(vtok2[:, c, :], ps[:, c, :], ACT.Copy)
            last.then_inc(v_tok, 1)

            act.wait_ge(s_shifted, 1)
            nc.scalar.activation(s_all[:], s_all[:], ACT.Exp).then_inc(p_all, 1)

            def exps(i, u):
                n = i * 16 + u
                tt = u % 4
                act.wait_ge(neg_max, n + 1)
                act.wait_ge(p_turned, n + 1)
                nc.scalar.activation(prob[:, u % 2, 0:P * (tt + 1)], ps[:, u % 2, 0:P * (tt + 1)], ACT.Exp,
                                     bias=tiny[:, u % 2:u % 2 + 1], accum_out=tiny[:, 2 + u % 2:3 + u % 2]).then_inc(exp_done, 1)

            def pt_copy(i, u):
                n = i * 16 + u
                tt = u % 4
                act.wait_ge(p_turned, n + 3)
                act.wait_ge(pv_done, n + 1)
                nc.scalar.activation(prob_t[:, u % 2, 0:P * (tt + 1)], ps[:, 2 + u % 2, 0:P * (tt + 1)], ACT.Copy)\
                    .then_inc(pt_copied, 1)

            def stage(hp, at_):
                i, one = hp
                pair = i * 2 + one
                if at_ == 1:
                    nc.scalar.activation(q_st[one][:], pj2[:, bass.ds(pair, 1), 0:TP].rearrange("p o n -> p (o n)"),
                                         ACT.Copy, scale=64 ** -0.5)
                elif at_ == 0:
                    nc.scalar.activation(k_st[one][:, 0:TP], pj2[:, bass.ds(pair + CD_K, 1), 0:TP].rearrange("p o n -> p (o n)"),
                                         ACT.Copy)
                elif at_ in (2, 3):
                    h2 = at_ - 2
                    nc.scalar.activation(hsel[one][:, h2, :], hrow[:], ACT.Copy, scale=pick[:, bass.ds(pair * 2 + h2, 1)])
                else:
                    nc.scalar.activation(v_st[one][:], vtok2[:, :, bass.ds(i * 2 * P + one * P, P)], ACT.Copy)\
                        .then_inc(fox_staged, 1)

            act.wait_ge(rows_used, 1)
            act.wait_ge(v_tok, 2)
            with act.Fori(0, 2) as i:
                act.wait_ge(pv_done, i * 16 + 2)
                for part in range(5):
                    stage((i, 0), part)
                exps(i, 0)
                for u in range(16):
                    if u < 15:
                        exps(i, u + 1)
                    pt_copy(i, u)
                    if u < 5:
                        stage((i, 1), u)
            act.wait_ge(y_cd, 1)
            for k in range(4):
                split_rows(pj2[:, k, :], k)
            normalise_d()
            product_and_squares("cd_out", 3)
            normalise_x(3, True)
            act.wait_ge(out_sent, 16 * OUT_CD)
            product("f1_in", gate_up("f1_in"))
            product_and_squares("f1_out", 4)
            normalise_x(4, False)

        @block.gpsimd
        def _(pool):
            def rest(n, j, b):
                pool.wait_ge(w_rounded, n + 1)
                nc.gpsimd.tensor_tensor(wl[:, j % SPLIT, 0:b * P], raw[:, j, 0:b * P],
                                        wh[:, j % SPLIT, 0:b * P].bitcast(F32), ALU.subtract).then_inc(w_rest, 1)

            def next_rest(name, i, j, last):
                s = PH[name][0]
                b = BLOCKS.get(name, KD)
                if last and j >= 4 - SPLIT:
                    if NEXT[name] is None:
                        return
                    b = BLOCKS.get(NEXT[name], KD)
                rest(s + 4 * i + j + SPLIT, (j + SPLIT) % 4, b)

            def product(name, tile=None, peeled=1, behind=None):
                n = PH[name][1] // 4
                if behind:
                    for i in range(n):
                        for j in range(4):
                            next_rest(name, i, j, i == n - 1)
                        behind(i)
                    return
                if n > peeled:
                    with pool.Fori(0, n - peeled) as i:
                        for j in range(4):
                            next_rest(name, i, j, False)
                            if tile and peeled == 1:
                                tile(i, j)
                for i in range(n - peeled, n):
                    for j in range(4):
                        next_rest(name, i, j, i == n - 1)
                        if tile:
                            tile(i, j)

            def hidden(name):
                m0 = 0 if name == "f0_in" else 22

                def tile(i, j):
                    if j % 2 == 1:
                        m = i * 2 + j // 2
                        pool.wait_ge(hid_hi, m0 + m + 1)
                        nc.gpsimd.tensor_tensor(hl[:, bass.ds(m, 1), :].rearrange("p o n -> p (o n)"), hid_t[:],
                                                hh[:, bass.ds(m, 1), :].rearrange("p o n -> p (o n)").bitcast(F32),
                                                ALU.subtract).then_inc(hid_split, 1)
                return tile

            def squares_added(name, idx):
                base, of_d = LN_BASE[idx], LN_OF[idx]

                def after_tile(m):
                    for i in CENTERED_AT.get(m, ()):
                        if 1 <= i < KD - 1:
                            pool.wait_ge(ln_sq, base + i + 1)
                            if i > 1:
                                pool.wait_ge(ln_added, 6 * of_d + i - 1)
                            nc.gpsimd.tensor_tensor(gate_t[:], gate_t[:], hid_t[:], ALU.add).then_inc(ln_added, 1)

                if name in BLOCKS:
                    product(name, lambda i, j: after_tile(2 * i + j // 2) if j % 2 == 1 else None, peeled=2)
                else:
                    product(name, lambda i, j: after_tile(4 * i + j), peeled=2)

            def x_rest(lo):
                for k in range(KD):
                    pool.wait_ge(x_hi, lo + k + 1)
                    nc.gpsimd.tensor_tensor(xl[:, k, :], x[:, k, :], xh[:, k, :].bitcast(F32), ALU.subtract).then_inc(x_split, 1)

            nc.gpsimd.memset(eps_c[:], EPS).then_inc(setup, 1)
            pool.sem_inc(hid_split, 1)
            for j in range(SPLIT):
                rest(j, j, KD)
            def zero_attn(i):
                if i == 1:
                    pool.wait_ge(log_a, 1)
                    nc.gpsimd.memset(attn[:], 0.0).then_inc(attn_zero, 1)

            product("ab_in", behind=zero_attn)
            pool.wait_ge(conv_a_ready, 1)
            pool.dma_start(O["conv_a_p"], pj[:, AB_CG:AB_CG + 4, TP - 2:TP]).then_inc(out_sent, 16)
            pool.dma_start(O["conv_a_s"], conv_a_state[:]).then_inc(out_sent, 16)
            pool.wait_ge(state_c, GC)
            pool.dma_start(O["gla_p"], gla_s[:, GC - 1]).then_inc(out_sent, 16)
            pool.wait_ge(sam_state, 1)
            pool.dma_start(O["gla_s"], gla_s0[:]).then_inc(out_sent, 16)
            squares_added("ab_out", 0)
            x_rest(2 * KD)
            product("f0_in", hidden("f0_in"))
            squares_added("f0_out", 1)
            x_rest(3 * KD)
            product("cd_in")
            pool.wait_ge(acc_free[1], PH["cd_in"][2] // 2 + 10 + 1)
            pool.wait_ge(acc_free[0], PH["cd_in"][2] // 2 + 10 + 1)
            pool.dma_start(O["kt"], pj2[:, CD_K:CD_K + 4, :]).then_inc(out_sent, 16)
            pool.dma_start(O["vt"], pj2[:, CD_V:CD_V + 4, :]).then_inc(out_sent, 16)
            pool.wait_ge(f_done, 1)
            pool.dma_start(O["logf"], frow[2][0:8, :]).then_inc(logf_sent, 16)
            pool.wait_ge(u_ready, 1)
            wd = par_of("conv_d", 4 * CF_TAPS).rearrange("p (t j) -> p t j", j=CF_TAPS)
            POOL_TILES = 4 - DVE_TILES
            for t in range(DVE_TILES, 4):
                nc.gpsimd.tensor_scalar(pj2[:, CD_GATE + t, 0:TP], upad[:, t, 0:TP], wd[:, t, 0:1],
                                        par_of("cf_b", 4)[:, t:t + 1], ALU.mult, ALU.add)\
                    .then_inc(pool_tap, 1)
            with pool.Fori(1, CF_TAPS) as j:
                pool.wait_ge(pool_tap, j * POOL_TILES)
                for t in range(DVE_TILES, 4):
                    nc.gpsimd.tensor_tensor(tap_t[:, t - DVE_TILES, :], upad[:, t, bass.ds(j, TP)],
                                            wd[:, t, bass.ds(j, 1)].to_broadcast([P, TP]), ALU.mult).then_inc(tap_product, 1)
                pool.wait_ge(tap_product, j * POOL_TILES)
                for t in range(DVE_TILES, 4):
                    nc.gpsimd.tensor_tensor(pj2[:, CD_GATE + t, 0:TP], pj2[:, CD_GATE + t, 0:TP], tap_t[:, t - DVE_TILES, :],
                                            ALU.add).then_inc(pool_tap, 1)
            U = CD_GATE
            pool.wait_ge(conv_d_in, 16)
            pool.wait_ge(pool_tap, CF_TAPS * POOL_TILES)
            nc.gpsimd.tensor_copy(ext_d[:, :, :, CF_TAPS - 1], pj2[:, U:U + 4, TP:T]).then_inc(d_sampled, 1)
            pool.wait_ge(d_sampled, 1)
            pool.dma_start(O["conv_d_p"], upad[:, :, TP:TP + CF_TAPS - 1]).then_inc(out_sent, 16)
            pool.dma_start(O["conv_d_s"], ext_d[:, :, :, 1:CF_TAPS]).then_inc(out_sent, 16)
            nc.gpsimd.tensor_tensor(prod_d[:], ext_d[:], wd[:, :, None, :].to_broadcast([P, 4, TS, CF_TAPS]), ALU.mult)\
                .then_inc(d_sampled, 1)
            n, step = CF_TAPS, 2
            while n > 1:
                half = n // 2
                pool.wait_ge(d_sampled, step)
                nc.gpsimd.tensor_tensor(prod_d[:, :, :, 0:half], prod_d[:, :, :, 0:half], prod_d[:, :, :, n - half:n], ALU.add)\
                    .then_inc(d_sampled, 1)
                n, step = n - half, step + 1
            pool.wait_ge(d_sampled, step)
            nc.gpsimd.tensor_tensor(pj2[:, U:U + 4, TP:T], prod_d[:, :, :, 0], par_of("cf_b", 4)[:, :, None].to_broadcast([P, 4, TS]),
                                    ALU.add).then_inc(d_sampled, 1)
            squares_added("cd_out", 3)
            x_rest(5 * KD)
            product("f1_in", hidden("f1_in"))
            squares_added("f1_out", 4)

        @block.tensor
        def _(pe):
            pe.sem_inc(slot_used, SPLIT)
            pe.sem_inc(p_turned, 2)
            pe.sem_inc(pv_done, 2)
            pe.sem_inc(pages_free, 4)
            pe.sem_inc(pv_all, 1)

            def three(out, slot, k, block_at, hi, lo, start, stop):
                for w, rows, a, z in ((wh, hi, True, False), (wh, lo, False, False), (wl, hi, False, True)):
                    for h in range(2):
                        mm = nc.tensor.matmul(out[h], w[:, slot, block_at * P:block_at * P + P],
                                              rows[:, k, HT * h:HT * h + HT], start=start and a, stop=stop and z)
                return mm

            def product(name, split=None, idx=None, behind_first=None, behind_tile=None, behind_body=None,
                        behind_chunk=None):
                s, slots, t, _ = PH[name]

                def body(i, first_slots=False, behind=None):
                    for j in range(4):
                        n = s + i * 4 + j
                        pe.wait_ge(w_rest, n + 1)
                        if name in BLOCKS:
                            par2, tile, first, lastk = j // 2, t // 2 + i, j % 2 == 0, j % 2 == 1
                            if first:
                                pe.wait_ge(acc_free[par2], tile + 1)
                            pe.wait_ge(hid_split, (0 if name == "f0_out" else KF) + (HALF_KF if first else KF) + 1)
                            out = [ps[:, 2 * par2 + h, 0:HT] for h in range(2)]
                            for k in range(HALF_KF):
                                kk = k + (0 if first else HALF_KF)
                                mm = three(out, j % 2, kk, k, hh, hl, first and k == 0, lastk and k == HALF_KF - 1)
                            mm.then_inc(slot_used, 1)
                        else:
                            pe.wait_ge(acc_free[j % 2], t // 2 + i * 2 + j // 2 + 1)
                            out = [ps[:, 2 * (j % 2) + h, 0:HT] for h in range(2)]
                            for k in range(KD):
                                if first_slots and j == 0:
                                    pe.wait_ge(x_split, split + k + 1)
                                mm = three(out, j % 2, k, k, xh, xl, k == 0, k == KD - 1)
                                if first_slots and j == 0 and behind_chunk:
                                    if k == KD - 1:
                                        mm.then_inc(slot_used, 1)
                                    behind_chunk(k)
                            if not (first_slots and j == 0 and behind_chunk):
                                mm.then_inc(slot_used, 1)
                            if behind:
                                behind(j)

                start = 0
                if split is not None:
                    body(0, True)
                    start = 1
                if behind_body:
                    behind_body(0)
                    for i in range(1, slots // 4):
                        body(i)
                        behind_body(i)
                    return
                if behind_tile:
                    behind_first()
                    body(1, behind=lambda j: behind_tile(1, j, True))
                    with pe.Fori(2, slots // 4) as i:
                        body(i, behind=lambda j: behind_tile(i, j, False))
                    return
                if idx is not None:
                    half = slots // 8
                    if start < half:
                        with pe.Fori(start, half) as i:
                            body(i)
                    pe.wait_ge(ln_first, LN_OF[idx] + 1)
                    for h in range(2):
                        mm = nc.tensor.matmul(ps[:, 4 + h, 0:HT], ones, rstd[:, HT * h:HT * h + HT], start=True, stop=True)
                    mm.then_inc(ln_guess, 1)
                    start = half
                with pe.Fori(start, slots // 4) as i:
                    body(i)

            def sums(idx):
                j, base = LN_OF[idx], LN_BASE[idx]
                pe.wait_ge(ln_part, j + 1)
                nc.tensor.matmul(ps[:, 6, 0:HT], ones, rstd[:, 0:HT], start=True, stop=False)
                nc.tensor.matmul(ps[:, 7, 0:HT], ones, rstd[:, HT:T], start=True, stop=False)
                pe.wait_ge(ln_centered, base + KD)
                nc.tensor.matmul(ps[:, 6, 0:HT], ones, x[:, KD - 1, 0:HT], start=False, stop=True)
                nc.tensor.matmul(ps[:, 7, 0:HT], ones, x[:, KD - 1, HT:T], start=False, stop=True).then_inc(ln_sum, 1)
                pe.wait_ge(ln_added, 6 * j + 6)
                nc.tensor.matmul(ps[:, 4, 0:HT], ones, gate_t[:, 0:HT], start=True, stop=False)
                nc.tensor.matmul(ps[:, 5, 0:HT], ones, gate_t[:, HT:T], start=True, stop=False)
                pe.wait_ge(ln_sq, base + KD)
                nc.tensor.matmul(ps[:, 4, 0:HT], ones, hid_t[:, 0:HT], start=False, stop=True)
                nc.tensor.matmul(ps[:, 5, 0:HT], ones, hid_t[:, HT:T], start=False, stop=True).then_inc(ln_var, 1)

            def sums_d():
                base = LN_BASE[D_LN]
                pe.wait_ge(d_tap, CF_TAPS * DVE_TILES)
                pe.wait_ge(pool_tap, CF_TAPS * (4 - DVE_TILES))
                pe.wait_ge(d_sampled, D_SAMPLE_STEPS)
                pe.wait_ge(o_evac, 4 + 1)
                for h in range(2):
                    for k in range(4):
                        mm = nc.tensor.matmul(ps[:, 4 + h, 0:HT], ones, pj2[:, CD_GATE + k, HT * h:HT * h + HT],
                                              start=k == 0, stop=k == 3)
                mm.then_inc(ln_sum, 1)
                for k in range(4):
                    pe.wait_ge(ln_sq, base + k + 1)
                    for h in range(2):
                        mm = nc.tensor.matmul(ps[:, 6 + h, 0:HT], ones, squares_d[:, k, HT * h:HT * h + HT],
                                              start=k == 0, stop=k == 3)
                mm.then_inc(ln_var, 1)


            def level_scores(l):
                half = P >> (l + 1)
                pe.wait_ge(lv_qk, l + 1)
                if l >= 2:
                    pe.wait_ge(lv_kept, l - 1)
                for u in range(GC * 4):
                    h2, hp, c = u % 2, u // 2 % 2, u // 4
                    r0, place = 64 * h2, 2 * c + hp
                    rows = qk[l % 2][r0:r0 + 64, hp, P * c:P * c + P]
                    bank = 4 + 2 * (l % 2) + h2
                    out = ps[:, bank, 64 * place:64 * place + 64].rearrange("p (n b) -> p n b", b=half)
                    mm = nc.tensor.matmul(out, rows, rows.rearrange("p (n b) -> p n b", b=2 * half)[:, :, half:],
                                          start=True, stop=True)
                mm.then_inc(lv_scores, 1)

            def diagonal_scores(part):
                pe.wait_ge(lv_kept, LEVELS - 1 + part)
                for u in range(8):
                    h2, hp, c = u % 2, u // 2 % 2, 2 * part + u // 4
                    r0, place = 64 * h2, 2 * (c % 2) + hp
                    bank = (4 + 2 * ((LEVELS + part) % 2)) + h2
                    mm = nc.tensor.matmul(ps[:, bank, P * place:P * place + P],
                                          pj[r0:r0 + 64, AB_K + hp, P * c:P * c + P],
                                          pj[r0:r0 + 64, AB_Q + hp, P * c:P * c + P], start=True, stop=True)
                mm.then_inc(lv_scores, 1)

            def linear_attention(i):
                if i == 0:
                    pe.wait_ge(r_copied, 1)
                    for t in range(2):
                        for h in range(2):
                            a = PARAM_AT["w_gate2"] + P * t
                            mm = nc.tensor.matmul(ps[:, 4 + 2 * t + h, 0:HT], par[0:16, a:a + P], r_t[:, HT * h:HT * h + HT],
                                                  start=True, stop=True)
                    mm.then_inc(z_sum, 1)
                elif i == 1:
                    pe.wait_ge(z_log, 1)
                    for j in range(2):
                        pe.wait_ge(acc_free[j], 2 + 1)
                    for c in range(GC):
                        for h in range(4):
                            mm = nc.tensor.transpose(ps[:, 4 + c, P * h:P * h + P], pj[:, AB_V + h, P * c:P * c + P], ident)
                    mm.then_inc(v_turned, 1)
                elif i == 2:
                    pe.wait_ge(v_tok, 1)
                    for h in range(4):
                        mm = nc.tensor.transpose(ps[0:NB, 7, P * h:P * h + P], pj[:, AB_V + h, TP:T], ident)
                    mm.then_inc(vsam_turned, 1)
                    level_scores(0)
                    pe.wait_ge(vsam_copied, 1)
                    level_scores(1)
                elif i <= 4:
                    level_scores(2 * i - 4)
                    level_scores(2 * i - 3)
                else:
                    level_scores(6)
                    for part in range(2):
                        diagonal_scores(part)

            def gate_rows(k):
                if k == 0:
                    pe.wait_ge(par_in, 16)
                for h in range(2):
                    a = PARAM_AT["w_r"] + 16 * k
                    mm = nc.tensor.matmul(ps[0:16, 4 + h, 0:HT], par[:, a:a + 16], x[:, k, HT * h:HT * h + HT],
                                          start=k == 0, stop=k == KD - 1)
                if k == KD - 1:
                    mm.then_inc(r_sum, 1)

            product("ab_in", split=0, behind_chunk=gate_rows, behind_body=linear_attention)
            def sample_values(part):
                for b in range(4 * part, 4 * part + 4):
                    mm = nc.tensor.matmul(ps[:, b % 4, :], ident[0:NB, b:b + 1].to_broadcast([NB, P]), vsam[:],
                                          start=True, stop=True)
                mm.then_inc(vb_sum, 1)

            for j in range(2):
                pe.wait_ge(acc_free[j], TILES_AB // 2 + 1)
            sample_values(0)
            pe.wait_ge(kw_ready, 1)
            pe.wait_ge(lv_kept, LEVELS + 2)
            for c in range(GC):
                for hp in range(2):
                    mm = nc.tensor.transpose(ps[:, 4 + c // 2, 256 * (c % 2) + P * hp:256 * (c % 2) + P * hp + P],
                                             qk[0][:, hp, P * c:P * c + P], ident)
            mm.then_inc(kw_turned, 1)
            pe.wait_ge(vb_used, 1)
            sample_values(1)
            pe.wait_ge(kw_tok, 1)
            pe.wait_ge(v_tok, 1)
            for c in range(GC):
                for hp in range(2):
                    mm = nc.tensor.matmul(ps[:, 4 + c, 256 * hp:256 * hp + 256], kwtok[:, c, P * hp:P * hp + P],
                                          vtok[:, c, 256 * hp:256 * hp + 256], start=True, stop=True)
                mm.then_inc(kv_sum, 1)
            pe.wait_ge(vb_used, 2)
            for c in range(GC):
                if c > 0:
                    pe.wait_ge(state_c, c)
                if c >= 2:
                    pe.wait_ge(o_copied, c - 1)
                for h in range(4):
                    r0, hp = 64 * (h % 2), h // 2
                    out = ps[:, 2 * (c % 2) + h % 2, P * hp:P * hp + P]
                    mm = nc.tensor.matmul(out, vtok[:, c, P * h:P * h + P], attn[:, 8 * (h % 2) + 2 * c + hp, :], start=True, stop=c == 0)
                    if c > 0:
                        mm = nc.tensor.matmul(out, gla_s[r0:r0 + 64, c - 1, hp, :],
                                              qk[1][r0:r0 + 64, hp, P * c:P * c + P], start=False, stop=True)
                mm.then_inc(o_sum, 1)
            pe.wait_ge(sam_state, 1)
            pe.wait_ge(o_copied, GC - 1)
            pe.wait_ge(sq_staged, 1)
            for part in range(2):
                for hp in range(2):
                    for g in range(4):
                        b, place = 4 * part + g, 2 * part + hp
                        mm = nc.tensor.matmul(ps[32 * g:32 * g + 32, 0, P * place:P * place + P], sam_q[:, b, hp, :],
                                              gla_s0[:, b, hp, :], start=True, stop=True)
            mm.then_inc(sam_rows, 1)
            pe.wait_ge(rms_squared, 1)
            for h in range(4):
                for c in range(GC):
                    nc.tensor.matmul(ps[:, 5, GC * h + c:GC * h + c + 1], rms_sq[:, h, P * c:P * c + P], ones[:, 0:1],
                                     start=True, stop=True)
            pe.wait_ge(sam_rows, 2)
            for place in range(4):
                mm = nc.tensor.transpose(ps[:, 1, P * place:P * place + P], sam_copy[:, P * place:P * place + P], ident)
            mm.then_inc(sam_o, 1)
            pe.wait_ge(rms_squared, 2)
            for h in range(4):
                mm = nc.tensor.matmul(ps[0:TS, 5, 16 + h:17 + h], rms_sq[:, h, TP:T], ones[:, 0:1], start=True, stop=True)
            mm.then_inc(rms_sum, 1)
            pe.wait_ge(rms_root, 1)
            for h in range(4):
                for c in range(GC):
                    at_ = GC * h + c
                    nc.tensor.matmul(ps[:, 4 + h, P * c:P * c + P], small_c[:, at_:at_ + 1].to_broadcast([P, P]), ident,
                                     start=True, stop=True)
                mm = nc.tensor.matmul(ps[:, 3, TS * h:TS * h + TS], small_c[0:TS, 16 + h:17 + h].to_broadcast([TS, P]),
                                      ident[0:TS, 0:TS], start=True, stop=True)
            mm.then_inc(rms_cast, 1)

            product("ab_out", split=KD, idx=0)
            sums(0)
            product("f0_in", split=2 * KD)
            product("f0_out", idx=1)
            sums(1)

            def forget_logits():
                for h in range(2):
                    for k in range(KD):
                        a = PARAM_AT["w_f"] + 40 * k
                        mm = nc.tensor.matmul(ps[0:40, 4 + h, 0:HT], par[:, a:a + 40], x[:, k, HT * h:HT * h + HT],
                                              start=k == 0, stop=k == KD - 1)
                mm.then_inc(f_sum, 1)

            def turn_scores(b):
                pe.wait_ge(ks_copied, b + 3)
                pe.wait_ge(s_ready_all, b)
                for s in range(4):
                    mm = nc.tensor.transpose(ps[:, 6, P * s:P * s + P], score_rows[:, P * s:P * s + P], ident)
                mm.then_inc(kt_done, 1)

            def key_slots(i, j, first):
                two = j // 2
                if j % 2 == 0:
                    if first and two == 0:
                        pe.wait_ge(f_log, 1)
                    else:
                        if first:
                            pe.wait_ge(decay_ready, 1)
                        turn_scores(i * 2 + (two - 3))
                    pe.wait_ge(q_staged, i * 2 + (two - 1))
                    pe.wait_ge(ks_copied, i * 2 + (two - 1))
                for h in range(2):
                    s = 2 * (j % 2) + h
                    pe.wait_ge(page_in[s], i * 128 + (64 * two - 64))
                    for pair in range(4):
                        for g in range(4):
                            mm = nc.tensor.matmul(ps[32 * g:32 * g + 32, 5 + 2 * two, P * s:P * s + P],
                                                  q_wide[:, two, 32 * pair:32 * pair + 32], pages[:, s, g, P * pair:P * pair + P],
                                                  start=pair == 0, stop=pair == 3)
                    mm.then_inc(pages_free, 1)
                if first and j == 1:
                    pe.wait_ge(later_in, 1)
                    for h in range(2):
                        out = ps[:, 6 + h, :]
                        nc.tensor.matmul(out, later, lf_pages[:, 8 * h:8 * h + 8].rearrange("p g b h -> p (g b h)"),
                                         start=True, stop=False)
                        nc.tensor.matmul(out, ones, lf_later[:, 8 * h:8 * h + 8, :].rearrange("p g n -> p (g n)"),
                                         start=False, stop=False)
                        mm = nc.tensor.matmul(out.rearrange("p (g n) -> p g n", g=8), ones[0:8, :],
                                              small_b[0:8, None, :].to_broadcast([8, 8, 64]), start=False, stop=True)
                    mm.then_inc(later_sum, 1)

            product("cd_in", split=3 * KD, behind_first=forget_logits, behind_tile=key_slots)

            turn_scores(NB - 1)
            pe.wait_ge(acc_free[0], PH["cd_in"][2] // 2 + 10 + 1)
            pe.wait_ge(acc_free[1], PH["cd_in"][2] // 2 + 10 + 1)
            for c in range(GC):
                for h in range(4):
                    mm = nc.tensor.transpose(ps[:, c, P * h:P * h + P], pj2[:, CD_V + h, P * c:P * c + P], ident)
            mm.then_inc(v_turned, 1)
            pe.wait_ge(self_in, 1)
            nc.tensor.matmul(ps[0:1, 5, 0:64], ones[:, 0:1], small_a[:], start=True, stop=True).then_inc(self_sum, 1)

            pe.wait_ge(m_turned, 1)
            nc.tensor.transpose(ps[0:64, 5, 0:P], small_a[:], ident).then_inc(m_turned, 1)
            pe.wait_ge(m_diag, 1)
            nc.tensor.matmul(ps[:, 6, 0:64], ones[0:64, :], small_b[0:64, :], start=True, stop=True).then_inc(m_cast, 1)
            pe.wait_ge(l_part, 1)
            nc.tensor.matmul(ps[:, 7, 0:64], ones, small_c[:], start=True, stop=True).then_inc(l_sum, 1)
            nc.tensor.matmul(ps[:, 6, 64:128], ones[0:1, :], s_all[0:1, :, :, PAGES].rearrange("p b h -> p (b h)"),
                             start=True, stop=True).then_inc(self_cast, 1)
            def scores(i, u):
                one, h2, tt = u // 8, u // 4 % 2, u % 4
                r0, w = 64 * h2, P * (tt + 1)
                if u % 8 == 0:
                    pe.wait_ge(fox_staged, i * 2 + (one + 1))
                pe.wait_ge(exp_done, i * 16 + (u + 1))
                out = ps[:, u % 2, 0:w]
                nc.tensor.matmul(out, q_st[one][r0:r0 + 64, P * tt:P * tt + P], k_st[one][r0:r0 + 64, 0:w], start=True, stop=False)
                nc.tensor.matmul(out, grow[:, P * tt:P * tt + P], hsel[one][:, h2, 0:w], start=False, stop=False)
                nc.tensor.matmul(ps[:, u % 2, P * tt:w], ident_b[:], causal_b[:], start=False, stop=True).then_inc(s_ready, 1)

            def turned(i, u):
                n = i * 16 + u
                pe.wait_ge(p_ready, n + 1)
                pe.wait_ge(pt_copied, n + 1)
                for c in range(u % 4 + 1):
                    mm = nc.tensor.transpose(ps[:, 2 + u % 2, P * c:P * c + P], prob[:, u % 2, P * c:P * c + P], ident)
                mm.then_inc(p_turned, 1)

            def outputs(i, u):
                one, h2, tt = u // 8, u // 4 % 2, u % 4
                r0 = 64 * h2
                pe.wait_ge(pt_copied, i * 16 + (u + 3))
                if u % 8 == 0:
                    pe.wait_ge(o_evac, i * 2 + (one + 1))
                for c in range(tt + 1):
                    mm = nc.tensor.matmul(ps[r0:r0 + 64, 4, P * tt:P * tt + P], v_st[one][:, c, r0:r0 + 64],
                                          prob_t[:, u % 2, P * c:P * c + P], start=c == 0, stop=c == tt)
                mm.then_inc(pv_done, 1)

            def value_slot(i, u):
                two, s = u // 4 % 2, u % 4
                if s == 0:
                    pe.wait_ge(p_staged, i * 4 + (u // 4 + 1))
                pe.wait_ge(page_in[s], i * 256 + (64 * (u // 4) + 64 * 9))
                for g in range(4):
                    mm = nc.tensor.matmul(ps[32 * g:32 * g + 32, 5 + 2 * two, :], p_blocks[:, two, 4 * s + g, :],
                                          pages[:, s, g, :], start=s == 0, stop=s == 3)
                mm.then_inc(pages_free, 1)

            def value_sums(i, b):
                pe.wait_ge(v_masked, i * 4 + (b + 1))
                for pair in range(4):
                    mm = nc.tensor.matmul(ps[:, 6, bass.ds(i * 16 + (4 * b + pair), 1)], v_rows[:, P * pair:P * pair + P],
                                          ones[:, 0:1], start=True, stop=True)
                mm.then_inc(pv_all, 1)

            pe.wait_ge(v_tok, 2)
            with pe.Fori(0, 2) as i:
                scores(i, 0)
                for u in range(16):
                    if u < 15:
                        scores(i, u + 1)
                    value_slot(i, u)
                    turned(i, u)
                    if u > 0:
                        outputs(i, u - 1)
                    if u > 0 and u % 4 == 0:
                        value_sums(i, u // 4 - 1)
                outputs(i, 15)
                value_sums(i, 3)
            sums_d()

            product("cd_out", split=4 * KD, idx=3)
            sums(3)
            product("f1_in", split=5 * KD)
            product("f1_out", idx=4)
            sums(4)

        @block.vector
        def _(dve):
            own = [0]
            V = nc.vector

            def link(ins):
                own[0] += 1
                ins.then_inc(dve_own, 1)
                dve.wait_ge(dve_own, own[0])

            for free in (acc_free[0], acc_free[1], hid_ready, o_evac):
                dve.sem_inc(free, 1)

            def acc(j):
                return ps[:, 2 * (j % 2):2 * (j % 2) + 2, 0:HT]

            def copy_tile(name, dst, m, j):
                dve.wait_ge(slot_used, m + (SPLIT + PH[name][0] + 1))
                V.tensor_copy(dst[:, bass.ds(m, 1), :].rearrange("p o (h n) -> p (o h) n", h=2), acc(j))\
                    .then_inc(acc_free[j % 2], 1)

            def copy_tiles(name, dst, first, behind):
                with dve.Fori(first // 2, behind // 2) as i:
                    for j in range(2):
                        copy_tile(name, dst, i * 2 + j, j)

            def residual_and_center(name, idx):
                s, slots, t, tiles = PH[name]
                j, base = LN_OF[idx], LN_BASE[idx]

                done = 0
                for m in range(tiles):
                    dve.wait_ge(slot_used, SPLIT + s + (m + 1) * slots // tiles)
                    V.scalar_tensor_tensor(out=halves(x[:, m, :]), in0=halves(x[:, m, :]), scalar=ALPHA, in1=acc(m),
                                           op0=ALU.mult, op1=ALU.add).then_inc(acc_free[m % 2], 1)
                    if m > 0:
                        dve.wait_ge(acc_free[m % 2], (t + m) // 2 + 2)
                    if m == 1:
                        dve.wait_ge(acc_free[0], t // 2 + 2)
                        link(V.tensor_tensor(rstd[:], x[:, 0, :], x[:, 1, :], ALU.add))
                    elif m == 2:
                        V.tensor_tensor(rstd[:], rstd[:], x[:, 2, :], ALU.add).then_inc(ln_first, 1)
                    elif m == 4:
                        dve.wait_ge(acc_free[1], (t + 3) // 2 + 2)
                        dve.wait_ge(ln_guess, j + 1)
                    if m >= 4:
                        first = done
                        while done < (3, 5, 7, 8)[m - 4]:
                            k = CENTERED[done]
                            V.scalar_tensor_tensor(out=halves(x[:, k, :]), in0=ps[:, 4:6, 0:HT], scalar=-1.0 / (P * GUESS),
                                                   in1=halves(x[:, k, :]), op0=ALU.mult, op1=ALU.add).then_inc(ln_centered, 1)
                            done += 1
                        if m < 7:
                            dve.wait_ge(ln_centered, base + done)
                            if m == 4:
                                link(V.tensor_tensor(rstd[:], x[:, CENTERED[0], :], x[:, CENTERED[1], :], ALU.add))
                                first = 2
                            for i in range(first, done):
                                last = V.tensor_tensor(rstd[:], rstd[:], x[:, CENTERED[i], :], ALU.add)
                                if i == 6:
                                    last.then_inc(ln_part, 1)
                                else:
                                    link(last)

            def normalise_x(idx):
                base = LN_BASE[idx]
                dve.wait_ge(ln_squared, LN_OF[idx] + 1)

                def center(k):
                    return V.scalar_tensor_tensor(out=halves(x[:, k, :]), in0=ps[:, 6:8, 0:HT], scalar=-1.0 / D,
                                                  in1=halves(x[:, k, :]), op0=ALU.mult, op1=ALU.add).then_inc(ln_middle, 1)
                center(0)
                dve.wait_ge(ln_var, idx + 1)
                V.scalar_tensor_tensor(out=halves(rstd[:]), in0=halves(rstd[:]), scalar=-1.0 / D, in1=ps[:, 4:6, 0:HT],
                                       op0=ALU.mult, op1=ALU.add).then_inc(ln_veps, 1)
                center(1)
                dve.wait_ge(ln_std, idx + 1)
                link(V.reciprocal(rstd[:], rstd[:]))
                for k in range(KD):
                    dve.wait_ge(ln_middle, KD * LN_OF[idx] + k + 1)
                    V.tensor_tensor(x[:, k, :], x[:, k, :], rstd[:], ALU.mult).then_inc(ln_scaled, 1)
                    if k + 2 < KD:
                        center(k + 2)

            def rest_rows(src, lo):
                for k in range(KD):
                    dve.wait_ge(x_hi, lo + k + 1)
                    V.tensor_tensor(xl[:, k, :], src(k), xh[:, k, :].bitcast(F32), ALU.subtract).then_inc(x_split, 1)

            def normalise_d():
                idx, n = D_LN, 4

                def src(k):
                    return pj2[:, CD_GATE + k, :]

                dve.wait_ge(ln_sum, idx + 1)
                for k in range(n):
                    V.scalar_tensor_tensor(out=halves(src(k)), in0=ps[:, 4:6, 0:HT], scalar=-1.0 / (P * n),
                                           in1=halves(src(k)), op0=ALU.mult, op1=ALU.add).then_inc(ln_centered, 1)
                for k in range(4):
                    dve.wait_ge(x_hi, 4 * KD + k + 1)
                    V.tensor_tensor(xl[:, k, :], pj2[:, k, :], xh[:, k, :].bitcast(F32), ALU.subtract).then_inc(x_split, 1)
                dve.wait_ge(ln_var, idx + 1)
                V.tensor_scalar(halves(rstd[:]), ps[:, 6:8, 0:HT], 1.0 / (P * n), None, ALU.mult).then_inc(ln_veps, 1)
                dve.wait_ge(ln_std, idx + 1)
                link(V.reciprocal(rstd[:], rstd[:]))
                dve.wait_ge(ln_centered, LN_BASE[idx] + n)
                for k in range(n):
                    V.tensor_tensor(src(k), src(k), rstd[:], ALU.mult).then_inc(ln_scaled, 1)

            def x_rows(k):
                return x[:, k, :]

            def hidden(name):
                s, _, _, _ = PH[name]
                m0 = 0 if name == "f0_in" else 22
                with dve.Fori(0, 22) as m:
                    dve.wait_ge(gate_ready, m0 + m + 1)
                    dve.wait_ge(slot_used, m * 2 + (SPLIT + s + 2))
                    dve.wait_ge(hid_split, m0 + m + 1)
                    V.tensor_tensor(halves(hid_t[:]), acc(1), halves(gate_t[:]), ALU.mult).then_inc(hid_ready, 1)
                    dve.wait_ge(hid_ready, m0 + m + 2)
                    dve.sem_inc(acc_free[1], 1)

            V.memset(q_wide[:], 0.0)
            link(V.memset(qblk[:], 0.0))
            link(V.memset(small_b[:], 0.0))
            rest_rows(x_rows, 0)
            dve.wait_ge(r_sum, 1)
            V.tensor_copy(halves(r_t[:]), ps[0:16, 4:6, 0:HT]).then_inc(r_copied, 1)
            copy_tiles("ab_in", pj, 0, 4)
            dve.wait_ge(par_in, 16)
            dve.wait_ge(con_in, 16)
            dve.wait_ge(z_log, 1)
            link(V.scalar_tensor_tensor(out=loga[:], in0=zpre[:], scalar=0.0, in1=zexp[:], op0=ALU.min, op1=ALU.subtract))
            V.tensor_scalar(loga[:], loga[:], 1.0 / 16.0, None, ALU.mult).then_inc(log_a, 1)
            dve.wait_ge(log_a, 1)
            for t in range(2):
                last = V.tensor_tensor_scan(gcum[:, t, :], scan_on, loga[:, t, 0:TP], 0.0, ALU.mult, ALU.add)
            link(last)
            copy_tiles("ab_in", pj, 4, 8)
            dve.wait_ge(acc_free[0], 4 + 1)
            dve.wait_ge(acc_free[1], 4 + 1)
            link(V.tensor_scalar(pj[:, AB_Q:AB_Q + 2, :], pj[:, AB_Q:AB_Q + 2, :], 64 ** -0.5, None, ALU.mult))
            dve.wait_ge(state_in, 64)

            def level_diff(l):
                half = P >> (l + 1)
                g = gcum[:].rearrange("p t (n b) -> p (t n) b", b=2 * half)
                d = gdiff[:, l % 2].rearrange("p t (n b) -> p (t n) b", b=2 * half)
                mid = g[:, :, half - 1:half].to_broadcast([P, 2 * TP // (2 * half), half])
                V.tensor_tensor(d[:, :, half:], g[:, :, half:], mid, ALU.subtract)
                V.tensor_tensor(d[:, :, 0:half], mid, g[:, :, 0:half], ALU.subtract).then_inc(lv_diff, 1)

            def level_qk(l):
                half = P >> (l + 1)

                def by_block(ap):
                    return ap.rearrange("p t (n b) -> p t n b", b=2 * half)
                d, o = by_block(gdiff[:, l % 2]), by_block(qk[l % 2][:])
                q, k = by_block(pj[:, AB_Q:AB_Q + 2, 0:TP]), by_block(pj[:, AB_K:AB_K + 2, 0:TP])
                dve.wait_ge(lv_exp, l + 1)
                if l >= 2:
                    dve.wait_ge(lv_scores, l - 1)
                V.tensor_tensor(o[:, :, :, half:], q[:, :, :, half:], d[:, :, :, half:], ALU.mult)
                V.tensor_tensor(o[:, :, :, 0:half], k[:, :, :, 0:half], d[:, :, :, 0:half], ALU.mult).then_inc(lv_qk, 1)

            def level_keep(l):
                half = P >> (l + 1)
                dve.wait_ge(lv_scores, l + 1)
                if l >= 1:
                    dve.wait_ge(lv_kept, l)
                out = attn[:].rearrange("p u (n b) -> p u n b", b=2 * half)[:, :, :, half:]
                mask = imask[:, None, 64 * l:64 * l + 64].to_broadcast([P, 16, 64]).rearrange("p u (n b) -> p u n b", b=half)
                bank = 4 + 2 * (l % 2)
                V.copy_predicated(out, mask, ps[:, bank:bank + 2, :].rearrange("p k (u n b) -> p (k u) n b", u=8, b=half))\
                    .then_inc(lv_kept, 1)

            def next_diff(l):
                dve.wait_ge(lv_qk, l - 1)
                level_diff(l)

            for l in range(2):
                level_diff(l)
            for l in range(2):
                level_qk(l)
            for l in (2, 3):
                next_diff(l)
            dve.wait_ge(attn_zero, 1)
            g4 = gcum[:].rearrange("p t (n b) -> p (t n) b", b=P)
            U, Y = AB_CG, AB_HV
            wa = par_of("conv_a", 12).rearrange("p (t j) -> p t j", j=3)

            def conv_a(part):
                if part == 0:
                    link(V.tensor_tensor(pj[:, U:U + 4, :], pj[:, U:U + 4, :], pj[:, Y:Y + 4, :], ALU.mult))
                elif part == 1:
                    for t in range(4):
                        last = V.tensor_scalar(pj[:, Y + t, :], pj[:, U + t, :], wa[:, t, 2:3], None, ALU.mult)
                    link(last)
                else:
                    s = part - 1
                    for t in range(4):
                        V.scalar_tensor_tensor(out=pj[:, Y + t, s:TP], in0=pj[:, U + t, 0:TP - s], scalar=wa[:, t, 2 - s:3 - s],
                                               in1=pj[:, Y + t, s:TP], op0=ALU.mult, op1=ALU.add)
                        last = V.scalar_tensor_tensor(out=pj[:, Y + t, TP:T], in0=conv_a_state[:, t, :, 2 - s],
                                                      scalar=wa[:, t, 2 - s:3 - s], in1=pj[:, Y + t, TP:T],
                                                      op0=ALU.mult, op1=ALU.add)
                    link(last)

            for i in range(2, 6):
                for j in range(4):
                    copy_tile("ab_in", pj, 4 * i + j, j)
                    if i == 5:
                        conv_a(j)
                l = 2 * i - 4
                level_keep(l)
                if i < 5:
                    level_qk(l + 2)
                    level_keep(l + 1)
                if i == 3:
                    dve.wait_ge(sam_decay, 1)
                    V.tensor_tensor(gla_s0[:], gla_s0[:],
                                    tiny[:].rearrange("p (a b) -> p b a", a=2)[:, :, :, None].to_broadcast([P, NB, 2, P]),
                                    ALU.mult).then_inc(sam_decayed, 1)
                if i < 4:
                    level_qk(l + 3)
                    next_diff(l + 4)
                if i == 2:
                    next_diff(l + 5)
                if i == 4:
                    dve.wait_ge(lv_qk, LEVELS)
                    V.tensor_tensor(gdiff[:, 0].rearrange("p t (n b) -> p (t n) b", b=P),
                                    g4[:, :, P - 1:P].to_broadcast([P, 8, P]), g4, ALU.subtract).then_inc(kw_diff, 1)
            dve.wait_ge(kw_exp, 1)
            V.tensor_tensor(qk[0][:], pj[:, AB_K:AB_K + 2, 0:TP], gdiff[:, 0], ALU.mult)
            V.tensor_tensor(qk[1][:], pj[:, AB_Q:AB_Q + 2, 0:TP], gdiff[:, 1], ALU.mult).then_inc(kw_ready, 1)
            for part in range(2):
                bank = 4 + 2 * ((LEVELS + part) % 2)
                dve.wait_ge(lv_scores, LEVELS + part + 1)
                dve.wait_ge(lv_kept, LEVELS + part)
                V.copy_predicated(attn[:].rearrange("p (h u) t -> p h u t", h=2)[:, :, 4 * part:4 * part + 4, :],
                                  imask[:, None, None, 64 * LEVELS:64 * LEVELS + P].to_broadcast([P, 2, 4, P]),
                                  ps[:, bank:bank + 2, :].rearrange("p k (u t) -> p k u t", u=4)).then_inc(lv_kept, 1)
            link(V.memset(sam_q[:], 0.0))
            for b in range(NB):
                dve.wait_ge(vb_sum, b // 4 + 1)
                for h2 in range(2):
                    r = slice(64 * h2, 64 * h2 + 64)
                    last = V.tensor_tensor(gla_kv[r, b], ps[r, b % 4, :].rearrange("p (a c v) -> p a c v", a=2, c=2)[:, :, h2, :],
                                           pj[r, AB_K:AB_K + 2, TP + b:TP + b + 1].to_broadcast([64, 2, P]), ALU.mult)
                if b % 4 == 3:
                    last.then_inc(vb_used, 1)
            for c in range(GC):
                dve.wait_ge(kv_sum, c + 1)
                if c > 0:
                    dve.wait_ge(state_c, c)
                for hp in range(2):
                    for h2 in range(2):
                        r = slice(64 * h2, 64 * h2 + 64)
                        src = ps[r, 4 + c, 256 * hp + P * h2:256 * hp + P * h2 + P]
                        if c == 0:
                            last = V.tensor_copy(gla_s[r, 0, hp, :], src)
                        else:
                            last = V.scalar_tensor_tensor(out=gla_s[r, c, hp, :], in0=gla_s[r, c - 1, hp, :],
                                                          scalar=gdiff[r, 1, hp, P * c + P - 1:P * c + P], in1=src,
                                                          op0=ALU.mult, op1=ALU.add)
                last.then_inc(state_c, 1)
            for h2 in range(2):
                r = slice(64 * h2, 64 * h2 + 64)
                last = V.tensor_copy(sam_q[r, :, :, h2].rearrange("p b a -> p a b"), pj[r, AB_Q:AB_Q + 2, TP:T])
            last.then_inc(sq_staged, 1)
            dve.wait_ge(sam_decayed, 1)
            dve.wait_ge(vb_used, 2)
            link(V.tensor_tensor(gla_s0[:], gla_s0[:], gla_kv[:], ALU.add))
            dve.sem_inc(sam_state, 1)
            V.tensor_copy(conv_a_state[:, :, :, 0], conv_a_state[:, :, :, 1])
            V.tensor_tensor(pj[:, Y:Y + 4, :], pj[:, Y:Y + 4, :], pj[:, AB_BG:AB_BG + 4, :], ALU.mult).then_inc(conv_y, 1)
            link(V.memset(small_c[:, 0:20], 1.0))
            V.tensor_copy(conv_a_state[:, :, :, 1], pj[:, U:U + 4, TP:T]).then_inc(conv_a_ready, 1)
            dve.wait_ge(rms_sum, 1)
            V.tensor_scalar(small_c[:, 0:16], ps[:, 5, 0:16], 1.0 / P, EPS, ALU.mult, ALU.add)
            V.tensor_scalar(small_c[0:TS, 16:20], ps[0:TS, 5, 16:20], 1.0 / P, EPS, ALU.mult, ALU.add).then_inc(rms_eps, 1)
            dve.wait_ge(rms_std, 1)
            V.reciprocal(small_c[:, 0:20], small_c[:, 0:20]).then_inc(rms_root, 1)
            dve.wait_ge(g_silu, 1)
            link(V.tensor_tensor(gla_o[:], gla_o[:], pj[:, AB_G:AB_G + 4, :], ALU.mult))
            for k in range(4):
                dve.wait_ge(x_hi, KD + k + 1)
                V.tensor_tensor(xl[:, k, :], pj[:, AB_HV + k, :], xh[:, k, :].bitcast(F32), ALU.subtract).then_inc(x_split, 1)
            dve.wait_ge(rms_cast, 1)
            V.scalar_tensor_tensor(out=gla_o[:, :, TP:T], in0=gla_o[:, :, TP:T], scalar=par_of("norm_g", 1),
                                   in1=ps[:, 3, 0:4 * TS].rearrange("p (h b) -> p h b", h=4), op0=ALU.mult, op1=ALU.mult)
            for h in range(4):
                V.scalar_tensor_tensor(out=gla_o[:, h, 0:TP], in0=gla_o[:, h, 0:TP], scalar=par_of("norm_g", 1), in1=ps[:, 4 + h, :],
                                       op0=ALU.mult, op1=ALU.mult).then_inc(y_ab, 1)
            for h in range(4):
                dve.wait_ge(x_hi, KD + 5 + h)
                V.tensor_tensor(xl[:, 4 + h, :], gla_o[:, h, :], xh[:, 4 + h, :].bitcast(F32), ALU.subtract).then_inc(x_split, 1)
            residual_and_center("ab_out", 0)
            normalise_x(0)
            hidden("f0_in")
            residual_and_center("f0_out", 1)
            normalise_x(1)
            dve.wait_ge(lf_in, 16 * PAGES * NB)
            lfp = lf_pages[:].rearrange("p g b h -> p g (b h)")
            V.memset(lf_later[:, PAGES - 1, :], 0.0)
            link(V.tensor_copy(lf_later[:, PAGES - 2, :], lfp[:, PAGES - 1, :]))
            for g in range(PAGES - 3, -1, -1):
                link(V.tensor_tensor(lf_later[:, g, :], lf_later[:, g + 1, :], lfp[:, g + 1, :], ALU.add))
            copy_tiles("cd_in", pj2, 0, 4)
            for j in range(2):
                dve.wait_ge(acc_free[j], PH["cd_in"][2] // 2 + 2 + 1)
            for h2 in range(2):
                r = slice(64 * h2, 64 * h2 + 64)
                last = V.tensor_scalar(qblk[r, :, :, h2], pj2[r, CD_Q:CD_Q + 4, TP:T], 64 ** -0.5, None, ALU.mult)
            link(last)

            def stage_query(b, two):
                dve.wait_ge(pages_free, b * 4)
                V.tensor_copy(q_wide[:, two, :].rearrange("p (a c) -> p a c", c=34)[:, :, 0:2],
                              qblk[:, :, bass.ds(b, 1), :].rearrange("p a o c -> p a (o c)")).then_inc(q_staged, 1)

            for two in range(2):
                stage_query(two, two)
            z, e, lf, t4, t5 = (frow[i][:] for i in range(5))
            dve.wait_ge(f_log, 1)
            link(V.tensor_scalar(t4, e, 1.0, None, ALU.add))
            link(V.scalar_tensor_tensor(out=t5, in0=t4, scalar=-1.0, in1=e, op0=ALU.add, op1=ALU.subtract))
            link(V.reciprocal(t4, t4))
            link(V.tensor_tensor(t5, t5, t4, ALU.mult))
            link(V.tensor_tensor(t5, t5, lf, ALU.subtract))
            link(V.scalar_tensor_tensor(out=lf, in0=z, scalar=0.0, in1=t5, op0=ALU.min, op1=ALU.add))
            dve.sem_inc(f_done, 1)
            link(V.tensor_tensor(small_b[0:8, :].rearrange("p (b h) -> p b h", h=8),
                                 lf[0:8, TP:T][:, :, None].to_broadcast([8, NB, 8]),
                                 ident[0:8, None, 0:8].to_broadcast([8, NB, 8]), ALU.mult))
            dve.sem_inc(later_in, 1)
            link(V.memset(t4[:, 0:TP], 1.0))
            V.tensor_tensor_scan(t5[:, 0:TP], t4[:, 0:TP], lf[:, 0:TP], 0.0, ALU.mult, ALU.add).then_inc(f_done, 1)

            def add_decay(b):
                dve.wait_ge(kt_done, b + 1)
                one = bass.ds(b, 1)
                V.tensor_tensor(s_all[:, one, :, 0:PAGES].rearrange("p o h (s g) -> p (o h) s g", s=4),
                                ps[:, 6, :].rearrange("p (s g c) -> p c s g", s=4, g=4)[:, 0:8],
                                decay[:, one].rearrange("p o h (s g) -> p (o h) s g", s=4), ALU.add).then_inc(s_ready_all, 1)

            def tiles_and_keys(i, first=False, last=False):
                for j in range(4):
                    copy_tile("cd_in", pj2, i * 4 + j, j)
                    if j == 1 and first:
                        dve.wait_ge(later_sum, 1)
                        V.tensor_copy(decay[:].rearrange("p b h g -> p g (b h)"),
                                      ps[:, 6:8, :].rearrange("p k (g n) -> p (k g) n", g=8)).then_inc(decay_ready, 1)
                        dve.wait_ge(decay_ready, 1)
                    if j % 2 == 0 and not (first and j == 0):
                        add_decay(i * 2 + (j // 2 - 3))
                    if (j == 1 and not first) or (j == 3 and not last):
                        stage_query(i * 2 + (-1 if j == 1 else 0), int(j == 1))

            tiles_and_keys(1, first=True)
            with dve.Fori(2, 4) as i:
                tiles_and_keys(i)
            tiles_and_keys(4, last=True)
            add_decay(NB - 1)
            a0 = PH["cd_in"][2] // 2 + 10 + 1
            dve.wait_ge(acc_free[0], a0)
            dve.wait_ge(acc_free[1], a0)
            V.tensor_tensor(small_a[:].rearrange("p (a b c) -> p a b c", a=4, b=NB), qblk[:],
                            pj2[:, CD_K:CD_K + 4, TP:T][:, :, :, None].to_broadcast([P, 4, NB, 2]), ALU.mult).then_inc(self_in, 1)
            link(V.memset(s_all[:, :, :, PAGES], NEG))
            V.memset(hrow[:], 0.0)
            link(V.memset(grow[:], 0.0))
            V.memset(hrow[0:8, :], 1.0)
            V.memset(grow[32:40, :], 1.0)
            V.tensor_copy(grow[0:8, :], t5[0:8, 0:TP])
            V.tensor_scalar(hrow[32:40, :], t5[32:40, 0:TP], -1.0, None, ALU.mult).then_inc(rows_used, 1)
            dve.wait_ge(self_sum, 1)
            V.tensor_copy(s_all[0:1, :, :, PAGES].rearrange("p b (a c) -> p b a c", a=4),
                          ps[0:1, 5, 0:64].rearrange("p (a b c) -> p b a c", a=4, b=NB)).then_inc(s_ready_all, 1)
            dve.wait_ge(s_ready_all, NB + 1)
            sa = s_all[:].rearrange("p b h g -> p (b h) g")
            V.tensor_reduce(small_a[:], sa, AX, ALU.max).then_inc(m_turned, 1)
            link(V.memset(p_blocks[:], 0.0))
            dve.wait_ge(m_turned, 2)
            link(V.tensor_reduce(small_c[0:64, 0:1], ps[0:64, 5, 0:P], AX, ALU.max))
            V.tensor_scalar(small_b[0:64, :], ident[0:64, 0:64], small_c[0:64, 0:1], None, ALU.mult).then_inc(m_diag, 1)
            dve.wait_ge(m_cast, 1)
            V.tensor_tensor(sa, sa, ps[:, 6, 0:64][:, :, None].to_broadcast([P, 64, PAGES + 1]), ALU.subtract).then_inc(s_shifted, 1)
            dve.wait_ge(d_sig, 1)
            U = CD_GATE
            wd = par_of("conv_d", 4 * CF_TAPS).rearrange("p (t j) -> p t j", j=CF_TAPS)
            link(V.tensor_tensor(pj2[:, U:U + 4, :], pj2[:, U:U + 4, :], pj2[:, CD_A:CD_A + 4, :], ALU.mult))
            V.memset(upad[:, :, 0:U_PAD], 0.0)
            link(V.tensor_copy(upad[:, :, U_PAD:U_PAD + TP], pj2[:, U:U + 4, 0:TP]))
            dve.sem_inc(u_ready, 1)
            for t in range(DVE_TILES):
                V.tensor_scalar(pj2[:, U + t, 0:TP], upad[:, t, 0:TP], wd[:, t, 0:1], par_of("cf_b", 4)[:, t:t + 1],
                                ALU.mult, ALU.add).then_inc(d_tap, 1)
            dve.wait_ge(p_all, 1)
            V.tensor_reduce(small_c[:], sa, AX, ALU.add).then_inc(l_part, 1)
            dve.wait_ge(l_sum, 1)
            link(V.reciprocal(small_d[:], ps[:, 7, 0:64]))

            dve.wait_ge(v_tok, 2)

            def unit_max(i, u):
                tt = u % 4
                dve.wait_ge(s_ready, i * 16 + (u + 1))
                V.tensor_reduce(tiny[:, u % 2:u % 2 + 1], ps[:, u % 2, 0:P * (tt + 1)], AX, ALU.max, negate=True).then_inc(neg_max, 1)

            def evacuate(i, one):
                dve.wait_ge(pv_done, i * 16 + (8 * one + 10))
                V.tensor_copy(pj2[:, bass.ds(i * 2 + one, 1), 0:TP].rearrange("p o n -> p (o n)"), ps[:, 4, :]).then_inc(o_evac, 1)

            def stage_p(i, b):
                dve.wait_ge(pages_free, i * 16 + (4 * b + 32))
                V.tensor_copy(p_blocks[:, b % 2, :, 0:8],
                              s_all[:, bass.ds(i * 4 + b, 1), :, 0:PAGES].rearrange("p o h g -> p g (o h)")).then_inc(p_staged, 1)

            TAPS = (CF_TAPS - 1) // 2
            o0 = own[0]
            with dve.Fori(0, 2) as i:
                for b in range(2):
                    stage_p(i, b)
                unit_max(i, 0)
                for u in range(16):
                    tt = u % 4
                    dve.wait_ge(exp_done, i * 16 + (u + 3))
                    V.reciprocal(tiny[:, 4 + u % 2:5 + u % 2], tiny[:, 2 + u % 2:3 + u % 2]).then_inc(dve_own, 1)
                    dve.wait_ge(dve_own, i * 16 + (o0 + u + 1))
                    V.tensor_scalar(prob[:, u % 2, 0:P * (tt + 1)], prob[:, u % 2, 0:P * (tt + 1)],
                                    tiny[:, 4 + u % 2:5 + u % 2], None, ALU.mult).then_inc(p_ready, 1)
                    if u < 15:
                        unit_max(i, u + 1)
                    if u > 0:
                        j = i * TAPS + u
                        dve.wait_ge(d_tap, DVE_TILES * u + i * (DVE_TILES * TAPS))
                        for t in range(DVE_TILES):
                            V.scalar_tensor_tensor(out=pj2[:, U + t, 0:TP], in0=upad[:, t, bass.ds(j, TP)],
                                                   scalar=wd[:, t, bass.ds(j, 1)], in1=pj2[:, U + t, 0:TP],
                                                   op0=ALU.mult, op1=ALU.add).then_inc(d_tap, 1)
                    if tt == 3:
                        b = u // 4
                        dve.wait_ge(pages_free, i * 16 + (4 * b + 40))
                        dve.wait_ge(pv_all, i * 4 + (b + 1))
                        V.tensor_tensor(v_rows[:].rearrange("p (h d) -> p h d", h=8),
                                        ps[:, 5 + 2 * (b % 2), :].rearrange("p (h d) -> p h d", h=8),
                                        pick[:, :, None].to_broadcast([P, 8, 64]), ALU.mult).then_inc(v_masked, 1)
                        if b < 2:
                            stage_p(i, b + 2)
                    if u == 8:
                        evacuate(i, 0)
                evacuate(i, 1)
            own[0] += 32
            dve.wait_ge(self_cast, 1)
            dve.wait_ge(pv_all, NB + 1)
            for h2 in range(2):
                r = slice(64 * h2, 64 * h2 + 64)

                def of(ap):
                    return ap.rearrange("p (b a c) -> p a b c", b=NB, a=4)[:, :, :, h2]

                past = ps[r, 6, 0:32].rearrange("p (b a) -> p a b", a=4)
                acc_o = small_a[r, 0:32].rearrange("p (a b) -> p a b", a=4)
                link(V.tensor_tensor(acc_o, of(ps[r, 6, 64:128]), pj2[r, CD_V:CD_V + 4, TP:T], ALU.mult))
                link(V.tensor_tensor(acc_o, acc_o, past, ALU.add))
                last = V.tensor_tensor(pj2[r, CD_Q:CD_Q + 4, TP:T], acc_o, of(small_d[r, :]), ALU.mult)
            last.then_inc(y_cd, 1)
            normalise_d()
            for k in range(4):
                dve.wait_ge(x_hi, 4 * KD + 5 + k)
                V.tensor_tensor(xl[:, 4 + k, :], pj2[:, CD_GATE + k, :], xh[:, 4 + k, :].bitcast(F32), ALU.subtract).then_inc(x_split, 1)
            residual_and_center("cd_out", 3)
            normalise_x(3)
            hidden("f1_in")
            residual_and_center("f1_out", 4)
            normalise_x(4)


D_LN = 2
LN_BASE = [0, 8, 16, 20, 28]
LN_OF = [0, 1, None, 2, 3]
NEXT = {"ab_in": "ab_out", "ab_out": "f0_in", "f0_in": "f0_out", "f0_out": "cd_in", "cd_in": "cd_out",
        "cd_out": "f1_in", "f1_in": "f1_out", "f1_out": None}
OUT_AB = 4
OUT_CD = 8

_OUTS = {
    "y": (P, KD, T), "conv_a_p": (P, 4, 2), "conv_a_s": (P, 4, TS, 2), "gla_p": (P, 2, P), "gla_s": (P, NB, 2, P),
    "kt": (P, 4, T), "vt": (P, 4, T), "logf": (8, T), "conv_d_p": (P, 4, 30), "conv_d_s": (P, 4, TS, 30),
}


def _chunks(a):
    return np.moveaxis(a.reshape((a.shape[0] // P, P) + a.shape[1:]), 0, 1)


def _slots(w, blocks):
    parts = w.shape[0] // (P * blocks)
    w = w.reshape(parts, blocks, P, w.shape[1] // P, P)
    return np.ascontiguousarray(w.transpose(3, 0, 2, 1, 4)).reshape(-1, P, blocks * P)


def _constants():
    c = np.zeros((P, CONST_COLS), np.float32)
    i = np.arange(P)
    c[:, 0:128] = np.eye(P)
    c[:, 128:256] = 1.0
    c[:, 256:384] = i[:, None] > i[None, :]
    c[:, 384:896] = np.arange(TP) % P != 0
    c[0:8, 896:904] = np.eye(8)
    c[32:40, 896:904] = np.eye(8)
    c[64:72, 896:904] = np.eye(8)
    c[96:104, 896:904] = np.eye(8)
    c[:, 904:1032] = np.where(i[None, :] > i[:, None], NEG, 0.0)
    m = np.zeros((P, IMASK_COLS), np.int32)
    for l in range(LEVELS):
        half = P >> (l + 1)
        t = i[(i % (2 * half)) >= half]
        s = i[:, None]
        m[:, 64 * l:64 * l + 64] = (s // (2 * half) == t // (2 * half)) & (s % (2 * half) < half)
    m[:, 64 * LEVELS:] = np.eye(P)
    return c, m


def kernel(x_prompt, x_sample, state_conv_a, state_gla, cache_k, cache_v, cache_logf, state_conv_d, page_table,
           ab_w_in, ab_conv_w, gla_w_gate2, gla_b_gate, gla_norm_g, ab_w_out,
           cd_w_in, fox_b_f, cf_conv_w, cf_conv_b, cf_ln_g, cf_ln_b, cd_w_out,
           ffn_w_in, ffn_w_out, ln_g, ln_b):
    import concourse.bacc as _bacc
    from concourse import mybir as _mybir
    from concourse.bass_utils import run_bass_kernel_spmd as _run

    def arr(a):
        return np.asarray(a)

    arrays = {}
    tokens = np.concatenate([arr(x_prompt)[0], arr(x_sample)[:, 0]], 0)
    arrays["xt"] = _chunks(tokens.T)
    w = arr(ab_w_in)
    bg, cg, hv, q, k, v, g, r = np.split(w, np.cumsum([512, 512, 512, 256, 256, 512, 512]), axis=1)
    arrays["w_ab_in"] = _slots(np.concatenate([v, q, k, cg, hv, bg, g], 1), KD)
    arrays["w_ab_out"] = _slots(arr(ab_w_out), KD)
    cq, ck, cv, cf, ca, cgate = np.split(arr(cd_w_in), np.cumsum([512, 512, 512, 8, 512]), axis=1)
    arrays["w_cd_in"] = _slots(np.concatenate([cq, ck, cv, cgate, ca], 1), KD)
    arrays["w_cd_out"] = _slots(arr(cd_w_out), KD)
    for l in range(2):
        wi = arr(ffn_w_in)[l].reshape(D, 2, KF, P).transpose(0, 2, 1, 3).reshape(D, 2 * DFF)
        arrays[f"w_f{l}_in"] = _slots(wi, KD)
        arrays[f"w_f{l}_out"] = _slots(arr(ffn_w_out)[l], HALF_KF)
    par = np.zeros((P, PARAM_COLS), np.float32)

    def put(name, a, rows=slice(0, P)):
        a = np.asarray(a)
        a = a.reshape(a.shape[0], -1)
        par[rows, PARAM_AT[name]:PARAM_AT[name] + a.shape[1]] = a

    put("ln_g", _chunks(arr(ln_g).reshape(4, D).T).transpose(0, 2, 1))
    put("ln_b", _chunks(arr(ln_b).reshape(4, D).T).transpose(0, 2, 1))
    put("conv_a", _chunks(arr(ab_conv_w).T))
    put("conv_d", _chunks(arr(cf_conv_w).T))
    put("cf_b", _chunks(arr(cf_conv_b)))
    put("cf_g", _chunks(arr(cf_ln_g)))
    put("cf_lb", _chunks(arr(cf_ln_b)))
    put("b_gate", _chunks(arr(gla_b_gate)))
    put("norm_g", arr(gla_norm_g)[:, None])
    put("b_f", arr(fox_b_f)[:, None], slice(0, 8))
    put("b_f", arr(fox_b_f)[:, None], slice(32, 40))
    put("w_gate2", arr(gla_w_gate2), slice(0, 16))
    put("w_r", _chunks(r))
    wf = np.zeros((D, 40), np.float32)
    wf[:, 0:8] = cf
    wf[:, 32:40] = cf
    put("w_f", _chunks(wf))
    arrays["params"] = par
    arrays["consts"], arrays["imask"] = _constants()
    arrays["table"] = arr(page_table).astype(np.int32).reshape(1, -1)
    arrays["conv_a_state"] = arr(state_conv_a).reshape(TS, 2, 4, P).transpose(3, 2, 0, 1)
    arrays["conv_d_state"] = arr(state_conv_d).reshape(TS, 30, 4, P).transpose(3, 2, 0, 1)
    arrays["gla_state"] = arr(state_gla).reshape(NB, 2, 2, 64, P).transpose(2, 3, 0, 1, 4).reshape(P, NB, 2, P)
    arrays["cache_kt"] = arr(cache_k).reshape(PHYS, P, 4, P).transpose(0, 3, 2, 1).reshape(PHYS, P, 512)
    arrays["cache_v"] = arr(cache_v).reshape(PHYS, P, 512)
    arrays["cache_logf"] = arr(cache_logf)

    nc = _bacc.Bacc("TRN2", target_bir_lowering=False, num_devices=1)
    A, O, feed = {}, {}, {}
    for name, a in arrays.items():
        a = np.ascontiguousarray(a)
        feed[f"in_{name}"] = a
        A[name] = nc.dram_tensor(f"in_{name}", a.shape, _mybir.dt.from_np(a.dtype), kind="ExternalInput").ap()
    for name, shape in _OUTS.items():
        O[name] = nc.dram_tensor(f"out_{name}", shape, F32, kind="ExternalOutput").ap()
    bass_hybrid_step(nc, A, O)
    res = _run(nc, [feed], core_ids=[0]).results[0]
    o = {n: np.asarray(res[f"out_{n}"]) for n in _OUTS}

    def rows(a):
        return np.ascontiguousarray(a.transpose(2, 1, 0)).reshape(a.shape[2], -1)

    y, kt, vt, lf = rows(o["y"]), rows(o["kt"]), rows(o["vt"]), o["logf"].T
    conv_a_p = np.ascontiguousarray(o["conv_a_p"].transpose(2, 1, 0)).reshape(1, 2, 512)
    conv_a_s = np.ascontiguousarray(o["conv_a_s"].transpose(2, 3, 1, 0)).reshape(NB, 2, 512)
    conv_d_p = np.ascontiguousarray(o["conv_d_p"].transpose(2, 1, 0)).reshape(1, 30, 512)
    conv_d_s = np.ascontiguousarray(o["conv_d_s"].transpose(2, 3, 1, 0)).reshape(NB, 30, 512)
    gla_p = np.ascontiguousarray(o["gla_p"].reshape(2, 64, 2, P).transpose(2, 0, 1, 3)).reshape(1, 4, 64, P)
    gla_s = np.ascontiguousarray(o["gla_s"].reshape(2, 64, NB, 2, P).transpose(2, 3, 0, 1, 4)).reshape(NB, 4, 64, P)

    def heads(a, n):
        return np.ascontiguousarray(a).reshape(n + (8, 64))

    return (y[None, :TP], y[TP:, None], conv_a_p, conv_a_s, gla_p, gla_s,
            heads(kt[:TP], (1, TP)), heads(kt[TP:], (TS, 1)), heads(vt[:TP], (1, TP)), heads(vt[TP:], (TS, 1)),
            np.ascontiguousarray(lf[None, :TP]), np.ascontiguousarray(lf[TP:, None]), conv_d_p, conv_d_s)
```
